# Optimizing a Trainium2 kernel written in Bass

```python
import math
import jax, jax.numpy as jnp
from jax import lax
import numpy as np
import jax
import jax.numpy as jnp

D_MODEL = 1024
BATCH = 1
SEQ = 256
DEPTH = 2

N_MIXERS = 4
D_FF = 2816
EPS = 1e-6
S5_GROUP = 16
S5_GROUPS = D_MODEL // S5_GROUP
S5_STATE = 64
DT_MIN = 1e-3
DT_MAX = 1e-1
CONV_W = 31
GM_CHUNK = 128
GM_E = 2 * D_MODEL
GM_HEADS = 8
HEAD_DIM = 64
AT_HEADS = D_MODEL // HEAD_DIM
PATTERNS = ((128, 1), (512, 4), (2048, 16))
N_PATTERNS = len(PATTERNS)
BLOCK = 128
NUM_BUCKETS = 32
MAX_DISTANCE = 2048


def rmsnorm(x, g):
    xf = x.astype(jnp.float32)
    y = xf * lax.rsqrt(jnp.mean(xf * xf, axis=-1, keepdims=True) + EPS)
    return (y * g.astype(jnp.float32)).astype(x.dtype)

def layernorm(x, g, b):
    xf = x.astype(jnp.float32)
    mu = jnp.mean(xf, axis=-1, keepdims=True)
    var = jnp.mean(jnp.square(xf - mu), axis=-1, keepdims=True)
    y = (xf - mu) * lax.rsqrt(var + EPS)
    return (y * g.astype(jnp.float32) + b.astype(jnp.float32)).astype(x.dtype)

def swiglu(h, w1, w3, w2):
    return (jax.nn.silu(h @ w1) * (h @ w3)) @ w2

def _complex_scan_op(left, right):
    a1r, a1i, b1r, b1i = left
    a2r, a2i, b2r, b2i = right
    return (a2r * a1r - a2i * a1i,
            a2r * a1i + a2i * a1r,
            a2r * b1r - a2i * b1i + b2r,
            a2r * b1i + a2i * b1r + b2i)

def s5_mixer(h, w_in, a_re, a_im, log_dt, b_re, b_im, c_re, c_im, d_skip, w_glu, b_glu, w_out):
    bsz, seq, _ = h.shape
    u = (h @ w_in).astype(jnp.float32).reshape(bsz, seq, S5_GROUPS, S5_GROUP)
    ar = a_re.astype(jnp.float32)
    ai = a_im.astype(jnp.float32)
    dt = jnp.exp(log_dt.astype(jnp.float32))[:, None]
    mag = jnp.exp(dt * ar)
    abar_re = mag * jnp.cos(dt * ai)
    abar_im = mag * jnp.sin(dt * ai)
    den = ar * ar + ai * ai
    nr = abar_re - 1.0
    f_re = (nr * ar + abar_im * ai) / den
    f_im = (abar_im * ar - nr * ai) / den
    br = b_re.astype(jnp.float32)
    bi = b_im.astype(jnp.float32)
    bb_re = f_re[..., None] * br - f_im[..., None] * bi
    bb_im = f_re[..., None] * bi + f_im[..., None] * br
    bu_re = jnp.einsum('blgh,gph->blgp', u, bb_re)
    bu_im = jnp.einsum('blgh,gph->blgp', u, bb_im)
    elems = (jnp.broadcast_to(abar_re, bu_re.shape), jnp.broadcast_to(abar_im, bu_re.shape), bu_re, bu_im)
    _, _, st_re, st_im = lax.associative_scan(_complex_scan_op, elems, axis=1)
    y = (jnp.einsum('blgp,ghp->blgh', st_re, c_re.astype(jnp.float32))
         - jnp.einsum('blgp,ghp->blgh', st_im, c_im.astype(jnp.float32))
         + d_skip.astype(jnp.float32).reshape(S5_GROUPS, S5_GROUP) * u)
    y = jax.nn.gelu(y.reshape(bsz, seq, D_MODEL)).astype(h.dtype)
    z = y * jax.nn.sigmoid(y @ w_glu + b_glu)
    return z @ w_out

def conv_mixer(h, w_in, b_in, dw, dw_b, ln_g, ln_b, w_out, b_out):
    z = h @ w_in + b_in
    a, g = jnp.split(z, 2, axis=-1)
    z = a * jax.nn.sigmoid(g)
    z = lax.conv_general_dilated(z, dw[:, None, :].astype(z.dtype), window_strides=(1,),
                                 padding=[(CONV_W - 1, 0)],
                                 dimension_numbers=('NWC', 'WIO', 'NWC'),
                                 feature_group_count=D_MODEL) + dw_b
    z = jax.nn.silu(layernorm(z, ln_g, ln_b))
    return z @ w_out + b_out

def gmlp_mixer(h, w_in, b_in, ln_g, ln_b, w_s, b_s, w_out, b_out):
    bsz, seq, _ = h.shape
    z = jax.nn.gelu(h @ w_in + b_in)
    u, v = jnp.split(z, 2, axis=-1)
    v = layernorm(v, ln_g, ln_b)
    vc = v.reshape(bsz, seq // GM_CHUNK, GM_CHUNK, GM_HEADS, GM_E // GM_HEADS)
    causal = jnp.tril(jnp.ones((GM_CHUNK, GM_CHUNK), jnp.float32))
    s = jnp.einsum('hts,bnshc->bnthc', w_s * causal, vc) + b_s.T[None, None, :, :, None]
    s = s.reshape(bsz, seq, GM_E).astype(u.dtype)
    return (u * s) @ w_out + b_out

def t5_bucket(dist):
    max_exact = NUM_BUCKETS // 2
    distf = jnp.maximum(dist, 1).astype(jnp.float32)
    large = max_exact + (jnp.log(distf / max_exact) / math.log(MAX_DISTANCE / max_exact)
                         * (NUM_BUCKETS - max_exact)).astype(jnp.int32)
    large = jnp.minimum(large, NUM_BUCKETS - 1)
    return jnp.where(dist < max_exact, dist, large)

def _band_delta():
    return (jnp.arange(BLOCK)[:, None] + BLOCK) - jnp.arange(2 * BLOCK)[None, :]

def rel_bias_block(table, dilation):
    dist = jnp.maximum(_band_delta(), 0) * dilation
    return table.astype(jnp.float32)[t5_bucket(dist)].transpose(2, 0, 1)

def dilated_window_attention(q, k, v, bias, window, dilation):
    bsz, seq, heads, hd = q.shape
    span = BLOCK * dilation
    seq_p = -(-seq // span) * span
    n_sub = seq_p // dilation
    n_blk = n_sub // BLOCK

    def to_blocks(t):
        t = jnp.pad(t.astype(jnp.float32), ((0, 0), (0, seq_p - seq), (0, 0), (0, 0)))
        t = t.reshape(bsz, n_sub, dilation, heads, hd).transpose(0, 2, 1, 3, 4)
        return t.reshape(bsz, dilation, n_blk, BLOCK, heads, hd)

    def with_prev(t):
        prev = jnp.pad(t, ((0, 0), (0, 0), (1, 0), (0, 0), (0, 0), (0, 0)))[:, :, :-1]
        return jnp.concatenate([prev, t], axis=3)

    qb = to_blocks(q)
    kk = with_prev(to_blocks(k))
    vv = with_prev(to_blocks(v))
    logits = jnp.einsum('brnqhd,brnkhd->brnhqk', qb, kk) * (hd ** -0.5) + bias[None, None, None]
    delta = _band_delta()
    in_band = (delta >= 0) & (delta <= window // dilation)
    not_before_start = (jnp.arange(n_blk)[:, None, None] > 0) | (jnp.arange(2 * BLOCK) >= BLOCK)[None, None, :]
    mask = in_band[None] & not_before_start
    logits = jnp.where(mask[None, None, :, None], logits, -jnp.inf)
    m = jnp.max(logits, axis=-1, keepdims=True)
    p = jnp.exp(logits - m)
    den = jnp.sum(p, axis=-1)
    o = jnp.einsum('brnhqk,brnkhd->brnqhd', p, vv) / jnp.swapaxes(den, -1, -2)[..., None]
    lse = jnp.swapaxes(m[..., 0] + jnp.log(den), -1, -2)
    o = o.reshape(bsz, dilation, n_sub, heads, hd).transpose(0, 2, 1, 3, 4).reshape(bsz, seq_p, heads, hd)[:, :seq]
    lse = lse.reshape(bsz, dilation, n_sub, heads).transpose(0, 2, 1, 3).reshape(bsz, seq_p, heads)[:, :seq]
    return o, lse

def attention_mixer(h, w_qkv, w_out, rel_bias):
    bsz, seq, _ = h.shape
    qkv = (h @ w_qkv).reshape(bsz, seq, N_PATTERNS, 3, AT_HEADS, HEAD_DIM)
    outs, lses = [], []
    for g, (window, dilation) in enumerate(PATTERNS):
        bias = rel_bias_block(rel_bias[:, g * AT_HEADS:(g + 1) * AT_HEADS], dilation)
        o, lse = dilated_window_attention(qkv[:, :, g, 0], qkv[:, :, g, 1], qkv[:, :, g, 2], bias, window, dilation)
        outs.append(o)
        lses.append(lse)
    wts = jax.nn.softmax(jnp.stack(lses, axis=0), axis=0)
    o = jnp.sum(wts[..., None] * jnp.stack(outs, axis=0), axis=0)
    return o.reshape(bsz, seq, AT_HEADS * HEAD_DIM).astype(h.dtype) @ w_out

def _count(kind):
    return len(range(kind, DEPTH, N_MIXERS))

def first_inputs(seed: int = 0) -> dict:
    key = jax.random.key(seed)
    ks = iter(jax.random.split(key, 48))

    def nrm(shape, scale):
        return scale * jax.random.normal(next(ks), shape, jnp.float32)

    na, nb, nc, nd = _count(0), _count(1), _count(2), _count(3)
    D, F, G, P, HG, E = D_MODEL, D_FF, S5_GROUPS, S5_STATE, S5_GROUP, GM_E
    return {
        "x": nrm((BATCH, SEQ, D), 1.0),
        "norm_pre": 1.0 + nrm((DEPTH, 3, D), 0.05),
        "norm_post": 1.0 + nrm((DEPTH, 3, D), 0.05),
        "ffn_w1": nrm((DEPTH, 2, D, F), D ** -0.5),
        "ffn_w3": nrm((DEPTH, 2, D, F), D ** -0.5),
        "ffn_w2": nrm((DEPTH, 2, F, D), F ** -0.5),
        "rel_bias": nrm((NUM_BUCKETS, N_PATTERNS * AT_HEADS), 0.5),
        "s5_w_in": nrm((na, D, D), D ** -0.5),
        "s5_a_re": -0.5 + nrm((na, G, P), 0.01),
        "s5_a_im": jnp.pi * jnp.arange(P, dtype=jnp.float32) + nrm((na, G, P), 0.01),
        "s5_log_dt": jax.random.uniform(next(ks), (na, G), jnp.float32, math.log(DT_MIN), math.log(DT_MAX)),
        "s5_b_re": nrm((na, G, P, HG), (2 * HG) ** -0.5),
        "s5_b_im": nrm((na, G, P, HG), (2 * HG) ** -0.5),
        "s5_c_re": nrm((na, G, HG, P), (2 * P) ** -0.5),
        "s5_c_im": nrm((na, G, HG, P), (2 * P) ** -0.5),
        "s5_d": nrm((na, D), 1.0),
        "s5_w_glu": nrm((na, D, D), D ** -0.5),
        "s5_b_glu": nrm((na, D), 0.01),
        "s5_w_out": nrm((na, D, D), D ** -0.5),
        "cv_w_in": nrm((nb, D, 2 * D), D ** -0.5),
        "cv_b_in": nrm((nb, 2 * D), 0.01),
        "cv_dw": nrm((nb, CONV_W, D), CONV_W ** -0.5),
        "cv_dw_b": nrm((nb, D), 0.01),
        "cv_ln_g": 1.0 + nrm((nb, D), 0.05),
        "cv_ln_b": nrm((nb, D), 0.01),
        "cv_w_out": nrm((nb, D, D), D ** -0.5),
        "cv_b_out": nrm((nb, D), 0.01),
        "gm_w_in": nrm((nc, D, 2 * E), D ** -0.5),
        "gm_b_in": nrm((nc, 2 * E), 0.01),
        "gm_ln_g": 1.0 + nrm((nc, E), 0.05),
        "gm_ln_b": nrm((nc, E), 0.01),
        "gm_w_s": nrm((nc, GM_HEADS, GM_CHUNK, GM_CHUNK), GM_CHUNK ** -0.5),
        "gm_b_s": 1.0 + nrm((nc, GM_HEADS, GM_CHUNK), 0.01),
        "gm_w_out": nrm((nc, E, D), E ** -0.5),
        "gm_b_out": nrm((nc, D), 0.01),
        "at_w_qkv": nrm((nd, D, N_PATTERNS * 3 * AT_HEADS * HEAD_DIM), D ** -0.5),
        "at_w_out": nrm((nd, AT_HEADS * HEAD_DIM, D), (AT_HEADS * HEAD_DIM) ** -0.5),
    }

def first_block(x, norm_pre, norm_post, ffn_w1, ffn_w3, ffn_w2, rel_bias,
              s5_w_in, s5_a_re, s5_a_im, s5_log_dt, s5_b_re, s5_b_im, s5_c_re, s5_c_im,
              s5_d, s5_w_glu, s5_b_glu, s5_w_out,
              cv_w_in, cv_b_in, cv_dw, cv_dw_b, cv_ln_g, cv_ln_b, cv_w_out, cv_b_out,
              gm_w_in, gm_b_in, gm_ln_g, gm_ln_b, gm_w_s, gm_b_s, gm_w_out, gm_b_out,
              at_w_qkv, at_w_out):
    for i in range(DEPTH):
        kind, j = i % N_MIXERS, i // N_MIXERS
        h = swiglu(rmsnorm(x, norm_pre[i, 0]), ffn_w1[i, 0], ffn_w3[i, 0], ffn_w2[i, 0])
        x = x + 0.5 * rmsnorm(h, norm_post[i, 0])
        h = rmsnorm(x, norm_pre[i, 1])
        if kind == 0:
            h = s5_mixer(h, s5_w_in[j], s5_a_re[j], s5_a_im[j], s5_log_dt[j], s5_b_re[j], s5_b_im[j],
                         s5_c_re[j], s5_c_im[j], s5_d[j], s5_w_glu[j], s5_b_glu[j], s5_w_out[j])
        elif kind == 1:
            h = conv_mixer(h, cv_w_in[j], cv_b_in[j], cv_dw[j], cv_dw_b[j], cv_ln_g[j], cv_ln_b[j],
                           cv_w_out[j], cv_b_out[j])
        elif kind == 2:
            h = gmlp_mixer(h, gm_w_in[j], gm_b_in[j], gm_ln_g[j], gm_ln_b[j], gm_w_s[j], gm_b_s[j],
                           gm_w_out[j], gm_b_out[j])
        else:
            h = attention_mixer(h, at_w_qkv[j], at_w_out[j], rel_bias)
        x = x + rmsnorm(h, norm_post[i, 1])
        h = swiglu(rmsnorm(x, norm_pre[i, 2]), ffn_w1[i, 1], ffn_w3[i, 1], ffn_w2[i, 1])
        x = x + 0.5 * rmsnorm(h, norm_post[i, 2])
    return x


N_A_LAYERS = DEPTH // 2
N_B_LAYERS = DEPTH - N_A_LAYERS
ALPHA = (2.0 * DEPTH) ** 0.25
BETA = (8.0 * DEPTH) ** -0.25
LN_EPS = 1e-5
NEG_INF = -1e30

RET_HEADS = 4
RET_QK_DIM = D_MODEL // RET_HEADS
RET_V_DIM = 2 * D_MODEL // RET_HEADS
RET_CHUNK = 128
RET_IN = 2 * RET_HEADS * RET_QK_DIM + 2 * RET_HEADS * RET_V_DIM

NSA_HEADS = 16
NSA_GROUPS = 4
NSA_REP = NSA_HEADS // NSA_GROUPS
NSA_HEAD_DIM = D_MODEL // NSA_HEADS
N_BRANCH = 3
CMP_STRIDE = 16
CMP_LEN = 2 * CMP_STRIDE
CMP_HIDDEN = 256
SLC_BLOCK = 64
SLC_TOPK = 16
WINDOW = 512
Q_BLOCK = 128
FORCE_BONUS = 100.0
NSA_IN = NSA_HEADS * NSA_HEAD_DIM + NSA_HEADS * N_BRANCH
NSA_KV = N_BRANCH * 2 * NSA_GROUPS * NSA_HEAD_DIM

PEER_HEADS = 8
PEER_NKEYS = 128
PEER_EXPERTS = PEER_NKEYS * PEER_NKEYS
PEER_TOPK = 16
PEER_QDIM = 256
PEER_TOKENS = 128


def layer_norm(x, g, b):
    xf = x.astype(jnp.float32)
    mu = jnp.mean(xf, axis=-1, keepdims=True)
    var = jnp.mean(jnp.square(xf - mu), axis=-1, keepdims=True)
    return ((xf - mu) * lax.rsqrt(var + LN_EPS) * g + b).astype(x.dtype)

def masked_softmax(s, mask):
    s = jnp.where(mask, s, NEG_INF)
    m = jnp.max(s, axis=-1, keepdims=True)
    e = jnp.where(mask, jnp.exp(s - m), 0.0)
    return e / jnp.maximum(jnp.sum(e, axis=-1, keepdims=True), 1e-30)

def rotate(x, cos, sin):
    x1, x2 = jnp.split(x, 2, axis=-1)
    return jnp.concatenate([x1 * cos - x2 * sin, x1 * sin + x2 * cos], axis=-1)

def retention(h, w_in, w_o):
    B, S, _ = h.shape
    H, dk, dv, C = RET_HEADS, RET_QK_DIM, RET_V_DIM, RET_CHUNK
    f32 = jnp.float32
    proj = h @ w_in
    q, k, v, g = jnp.split(proj, [H * dk, 2 * H * dk, 2 * H * dk + H * dv], axis=-1)
    to_heads = lambda t, d: t.reshape(B, S, H, d).transpose(0, 2, 1, 3).astype(f32)
    q, k, v = to_heads(q, dk), to_heads(k, dk), to_heads(v, dv)
    pos = jnp.arange(S, dtype=f32)
    theta = 1.0 / (10000.0 ** jnp.linspace(0.0, 1.0, dk // 2, dtype=f32))
    ang = pos[:, None] * theta[None, :]
    cos, sin = jnp.cos(ang), jnp.sin(ang)
    q = rotate(q, cos, sin)
    k = rotate(k, cos, sin) * (dk ** -0.5)
    log_g = jnp.log1p(-jnp.exp2(-5.0 - jnp.arange(H, dtype=f32)))
    idx = jnp.arange(C, dtype=f32)
    diff = idx[:, None] - idx[None, :]
    decay = jnp.where(diff >= 0, jnp.exp(jnp.maximum(diff, 0.0)[None] * log_g[:, None, None]), 0.0)
    q_dec = jnp.exp((idx + 1.0)[None] * log_g[:, None])
    k_dec = jnp.exp((C - 1.0 - idx)[None] * log_g[:, None])
    c_dec = jnp.exp(C * log_g)
    n_chunks = S // C
    chunks = lambda t: t.reshape(B, H, n_chunks, C, t.shape[-1]).transpose(2, 0, 1, 3, 4)

    def step(state, qkv):
        qc, kc, vc = qkv
        inner = jnp.einsum('bhqk,bhke->bhqe', jnp.einsum('bhqd,bhkd->bhqk', qc, kc) * decay, vc)
        cross = jnp.einsum('bhqd,bhde->bhqe', qc, state) * q_dec[:, :, None]
        state = state * c_dec[:, None, None] + jnp.einsum('bhkd,bhke->bhde', kc * k_dec[:, :, None], vc)
        return state, inner + cross

    state0 = jnp.zeros((B, H, dk, dv), f32)
    _, o = lax.scan(step, state0, (chunks(q), chunks(k), chunks(v)))
    o = o.transpose(1, 0, 3, 2, 4).reshape(B, S, H, dv)
    mu = jnp.mean(o, axis=-1, keepdims=True)
    var = jnp.mean(jnp.square(o - mu), axis=-1, keepdims=True)
    o = ((o - mu) * lax.rsqrt(var + LN_EPS)).reshape(B, S, H * dv)
    return (jax.nn.silu(g.astype(f32)) * o).astype(h.dtype) @ w_o

def nsa_shared_kv(xs, w_kv, cmp_pe, cmp_w1, cmp_b1, cmp_w2):
    B, S, _ = xs.shape
    G, hd = NSA_GROUPS, NSA_HEAD_DIM
    kv = (xs @ w_kv).reshape(B, S, N_BRANCH, 2, G, hd).transpose(2, 3, 0, 4, 1, 5)
    pieces = kv[0].reshape(2, B, G, S // CMP_STRIDE, CMP_STRIDE, hd)
    blocks = jnp.concatenate([pieces[:, :, :, :-1], pieces[:, :, :, 1:]], axis=4)
    blocks = blocks + cmp_pe[:, None, None, None]
    n_cmp = blocks.shape[3]
    flat = blocks.reshape(2, B, G, n_cmp, CMP_LEN * hd)
    hid = jax.nn.gelu(jnp.einsum('cbgnf,cfh->cbgnh', flat, cmp_w1) + cmp_b1[:, None, None, None])
    comp = jnp.einsum('cbgnh,chd->cbgnd', hid, cmp_w2)
    slc = kv[1].reshape(2, B, G, S // SLC_BLOCK, SLC_BLOCK, hd)
    win = jnp.pad(kv[2], ((0, 0), (0, 0), (0, 0), (WINDOW, 0), (0, 0)))
    return comp[0], comp[1], slc[0], slc[1], win[0], win[1]

def cmp_to_slc_matrix(n_cmp, n_slc):
    i = np.arange(n_cmp)[:, None] * CMP_STRIDE
    j = np.arange(n_slc)[None, :] * SLC_BLOCK
    ov = np.minimum(i + CMP_LEN, j + SLC_BLOCK) - np.maximum(i, j)
    return jnp.asarray(np.clip(ov, 0, None) / CMP_LEN, dtype=jnp.float32)

def nsa(h, w_in, w_o, k_cmp, v_cmp, k_slc, v_slc, k_win, v_win):
    B, S, _ = h.shape
    G, R, hd, QB = NSA_GROUPS, NSA_REP, NSA_HEAD_DIM, Q_BLOCK
    f32 = jnp.float32
    n_cmp = k_cmp.shape[2]
    n_slc = k_slc.shape[2]
    n_sel = min(SLC_TOPK, n_slc)
    proj = h @ w_in
    q = proj[..., :NSA_HEADS * hd].reshape(B, S, G, R, hd) * (hd ** -0.5)
    gate = jax.nn.sigmoid(proj[..., NSA_HEADS * hd:].astype(f32)).reshape(B, S, G, R, N_BRANCH)
    nqb = S // QB
    q_blocks = q.reshape(B, nqb, QB, G, R, hd).transpose(1, 0, 3, 4, 2, 5)
    g_blocks = gate.reshape(B, nqb, QB, G, R, N_BRANCH).transpose(1, 0, 3, 4, 2, 5)
    starts = jnp.arange(nqb, dtype=jnp.int32) * QB
    c2s = cmp_to_slc_matrix(n_cmp, n_slc)
    cmp_end = jnp.arange(n_cmp) * CMP_STRIDE + CMP_LEN - 1
    slc_idx = jnp.arange(n_slc)
    slc_start = slc_idx * SLC_BLOCK
    bi = jnp.arange(B)[:, None, None, None]
    gi = jnp.arange(G)[None, :, None, None]

    def block(args):
        qb, gb, start = args
        t = start + jnp.arange(QB)
        s = jnp.einsum('bgrqd,bgnd->bgrqn', qb, k_cmp, preferred_element_type=f32)
        p_cmp = masked_softmax(s, cmp_end[None, :] <= t[:, None])
        o_cmp = jnp.einsum('bgrqn,bgnd->bgrqd', p_cmp.astype(v_cmp.dtype), v_cmp)
        imp = jnp.einsum('bgqn,nj->bgqj', p_cmp.sum(axis=2), c2s)
        cur = t // SLC_BLOCK
        forced = (slc_idx[None] == 0) | (slc_idx[None] == cur[:, None]) | (slc_idx[None] == cur[:, None] - 1)
        avail = slc_start[None] <= t[:, None]
        score = jnp.where(avail, imp + jnp.where(forced, FORCE_BONUS, 0.0), -1.0)
        top_s, top_i = lax.top_k(score, n_sel)
        ks = k_slc[bi, gi, top_i]
        vs = v_slc[bi, gi, top_i]
        tok = top_i[..., None] * SLC_BLOCK + jnp.arange(SLC_BLOCK)
        smask = (tok <= t[:, None, None]) & (top_s >= 0.0)[..., None]
        s = jnp.einsum('bgrqd,bgqnkd->bgrqnk', qb, ks, preferred_element_type=f32)
        p = masked_softmax(s.reshape(B, G, R, QB, n_sel * SLC_BLOCK),
                           smask.reshape(B, G, 1, QB, n_sel * SLC_BLOCK))
        o_slc = jnp.einsum('bgrqm,bgqmd->bgrqd', p.astype(v_slc.dtype),
                           vs.reshape(B, G, QB, n_sel * SLC_BLOCK, hd))
        kw = lax.dynamic_slice_in_dim(k_win, start, WINDOW + QB, axis=2)
        vw = lax.dynamic_slice_in_dim(v_win, start, WINDOW + QB, axis=2)
        kp = start - WINDOW + jnp.arange(WINDOW + QB)
        wmask = (kp[None] <= t[:, None]) & (kp[None] > t[:, None] - WINDOW) & (kp[None] >= 0)
        s = jnp.einsum('bgrqd,bgkd->bgrqk', qb, kw, preferred_element_type=f32)
        o_win = jnp.einsum('bgrqk,bgkd->bgrqd', masked_softmax(s, wmask).astype(vw.dtype), vw)
        out = gb[..., 0:1] * o_cmp + gb[..., 1:2] * o_slc + gb[..., 2:3] * o_win
        return out.astype(qb.dtype)

    o = lax.map(block, (q_blocks, g_blocks, starts))
    o = o.transpose(1, 0, 4, 2, 3, 5).reshape(B, S, NSA_HEADS * hd)
    return o @ w_o

def peer(h, w_q, sub_keys, u_tab, v_tab):
    B, S, D = h.shape
    f32 = jnp.float32
    xt = h.reshape(-1, PEER_TOKENS, D)

    def chunk_fn(xc):
        T = xc.shape[0]
        q = (xc @ w_q).reshape(T, PEER_HEADS, 2, PEER_QDIM // 2)
        s = jnp.einsum('thcd,hcnd->thcn', q, sub_keys, preferred_element_type=f32)
        sv, si = lax.top_k(s, PEER_TOPK)
        comb = (sv[:, :, 0, :, None] + sv[:, :, 1, None, :]).reshape(T, PEER_HEADS, PEER_TOPK * PEER_TOPK)
        cv, ci = lax.top_k(comb, PEER_TOPK)
        i1 = jnp.take_along_axis(si[:, :, 0], ci // PEER_TOPK, axis=-1)
        i2 = jnp.take_along_axis(si[:, :, 1], ci % PEER_TOPK, axis=-1)
        eidx = i1 * PEER_NKEYS + i2
        w = jax.nn.softmax(cv, axis=-1)
        u = u_tab[eidx]
        a = jax.nn.gelu(jnp.einsum('td,thkd->thk', xc, u, preferred_element_type=f32)) * w
        return jnp.einsum('thk,thkd->td', a.astype(v_tab.dtype), v_tab[eidx])

    return lax.map(chunk_fn, xt).reshape(B, S, D)

def second_inputs(seed: int = 0) -> dict:
    key = jax.random.key(seed)
    ks = jax.random.split(key, 24)
    D = D_MODEL
    nrm = lambda k, shape, std: jax.random.normal(k, shape, jnp.float32) * std
    return {
        "x": nrm(ks[0], (BATCH, SEQ, D), 1.0),
        "c": nrm(ks[1], (BATCH, D), 1.0),
        "ada_w": nrm(ks[2], (DEPTH, D, 6 * D), 0.5 * D ** -0.5),
        "ada_b": nrm(ks[3], (DEPTH, 6 * D), 0.02),
        "ln_g": 1.0 + nrm(ks[4], (DEPTH, 2, D), 0.02),
        "ln_b": nrm(ks[5], (DEPTH, 2, D), 0.02),
        "ret_w_in": nrm(ks[6], (N_A_LAYERS, D, RET_IN), D ** -0.5),
        "ret_w_o": nrm(ks[7], (N_A_LAYERS, RET_HEADS * RET_V_DIM, D), BETA * (RET_HEADS * RET_V_DIM) ** -0.5),
        "kv_ada_w": nrm(ks[8], (D, 2 * D), 0.5 * D ** -0.5),
        "kv_ada_b": nrm(ks[9], (2 * D,), 0.02),
        "nsa_w_kv": nrm(ks[10], (D, NSA_KV), D ** -0.5),
        "cmp_pe": nrm(ks[11], (2, CMP_LEN, NSA_HEAD_DIM), 0.1),
        "cmp_w1": nrm(ks[12], (2, CMP_LEN * NSA_HEAD_DIM, CMP_HIDDEN), (CMP_LEN * NSA_HEAD_DIM) ** -0.5),
        "cmp_b1": nrm(ks[13], (2, CMP_HIDDEN), 0.02),
        "cmp_w2": nrm(ks[14], (2, CMP_HIDDEN, NSA_HEAD_DIM), CMP_HIDDEN ** -0.5),
        "nsa_w_in": nrm(ks[15], (N_B_LAYERS, D, NSA_IN), D ** -0.5),
        "nsa_w_o": nrm(ks[16], (N_B_LAYERS, NSA_HEADS * NSA_HEAD_DIM, D), BETA * (NSA_HEADS * NSA_HEAD_DIM) ** -0.5),
        "peer_w_q": nrm(ks[17], (DEPTH, D, PEER_HEADS * PEER_QDIM), D ** -0.5),
        "peer_keys": nrm(ks[18], (DEPTH, PEER_HEADS, 2, PEER_NKEYS, PEER_QDIM // 2), (PEER_QDIM // 2) ** -0.5),
        "peer_u": nrm(ks[19], (DEPTH, PEER_EXPERTS, D), D ** -0.5),
        "peer_v": nrm(ks[20], (DEPTH, PEER_EXPERTS, D), BETA),
    }

def second_block(x, c, ada_w, ada_b, ln_g, ln_b, ret_w_in, ret_w_o, kv_ada_w, kv_ada_b, nsa_w_kv,
              cmp_pe, cmp_w1, cmp_b1, cmp_w2, nsa_w_in, nsa_w_o, peer_w_q, peer_keys, peer_u, peer_v):
    c_act = jax.nn.silu(c)
    shared = None
    for layer in range(DEPTH):
        mod = (c_act @ ada_w[layer] + ada_b[layer])[:, None, :]
        sh1, sc1, g1, sh2, sc2, g2 = jnp.split(mod, 6, axis=-1)
        h = x * (1.0 + sc1) + sh1
        if layer < N_A_LAYERS:
            y = retention(h, ret_w_in[layer], ret_w_o[layer])
        else:
            lb = layer - N_A_LAYERS
            y = nsa(h, nsa_w_in[lb], nsa_w_o[lb], *shared)
        x = layer_norm(ALPHA * x + g1 * y, ln_g[layer, 0], ln_b[layer, 0])
        h = x * (1.0 + sc2) + sh2
        y = peer(h, peer_w_q[layer], peer_keys[layer], peer_u[layer], peer_v[layer])
        x = layer_norm(ALPHA * x + g2 * y, ln_g[layer, 1], ln_b[layer, 1])
        if layer == N_A_LAYERS - 1:
            kv_mod = (c_act @ kv_ada_w + kv_ada_b)[:, None, :]
            kv_sh, kv_sc = jnp.split(kv_mod, 2, axis=-1)
            shared = nsa_shared_kv(x * (1.0 + kv_sc) + kv_sh, nsa_w_kv, cmp_pe, cmp_w1, cmp_b1, cmp_w2)
    return x


def setup_inputs(seed=0):
    out = dict(first_inputs(seed))
    for name, value in second_inputs(seed + 1).items():
        if name != "x":
            out[name + "_2"] = value
    return out


def reference(
    x, norm_pre, norm_post, ffn_w1, ffn_w3, ffn_w2, rel_bias, s5_w_in, s5_a_re, s5_a_im,
    s5_log_dt, s5_b_re, s5_b_im, s5_c_re, s5_c_im, s5_d, s5_w_glu, s5_b_glu, s5_w_out, cv_w_in,
    cv_b_in, cv_dw, cv_dw_b, cv_ln_g, cv_ln_b, cv_w_out, cv_b_out, gm_w_in, gm_b_in, gm_ln_g,
    gm_ln_b, gm_w_s, gm_b_s, gm_w_out, gm_b_out, at_w_qkv, at_w_out, c_2, ada_w_2, ada_b_2,
    ln_g_2, ln_b_2, ret_w_in_2, ret_w_o_2, kv_ada_w_2, kv_ada_b_2, nsa_w_kv_2, cmp_pe_2,
    cmp_w1_2, cmp_b1_2, cmp_w2_2, nsa_w_in_2, nsa_w_o_2, peer_w_q_2, peer_keys_2, peer_u_2,
    peer_v_2,
):
    x = first_block(
        x, norm_pre, norm_post, ffn_w1, ffn_w3, ffn_w2, rel_bias, s5_w_in, s5_a_re, s5_a_im,
        s5_log_dt, s5_b_re, s5_b_im, s5_c_re, s5_c_im, s5_d, s5_w_glu, s5_b_glu, s5_w_out,
        cv_w_in, cv_b_in, cv_dw, cv_dw_b, cv_ln_g, cv_ln_b, cv_w_out, cv_b_out, gm_w_in,
        gm_b_in, gm_ln_g, gm_ln_b, gm_w_s, gm_b_s, gm_w_out, gm_b_out, at_w_qkv, at_w_out,
    )
    return second_block(
        x, c_2, ada_w_2, ada_b_2, ln_g_2, ln_b_2, ret_w_in_2, ret_w_o_2, kv_ada_w_2, kv_ada_b_2,
        nsa_w_kv_2, cmp_pe_2, cmp_w1_2, cmp_b1_2, cmp_w2_2, nsa_w_in_2, nsa_w_o_2, peer_w_q_2,
        peer_keys_2, peer_u_2, peer_v_2,
    )


_drawn_inputs = setup_inputs


def setup_inputs(seed=0):
    import zlib

    import numpy as np

    out = dict(_drawn_inputs(seed))
    spreads = {}
    factors = {'s5_a_re': 200.0,
     's5_b_glu': 8.0,
     'cv_b_in': 6.198,
     'cv_dw_b': 3.854,
     'cv_ln_b': 6.541,
     'cv_b_out': 4.499,
     'ada_b_2': 3.247,
     'kv_ada_b_2': 29.218,
     'cmp_pe_2': 8.0,
     'cmp_b1_2': 64.0,
     's5_a_im': 15.884,
     's5_log_dt': 15.933,
     's5_b_re': 23.762,
     's5_b_im': 24.406,
     's5_c_re': 23.658,
     's5_c_im': 24.693}
    for name, (base, spread) in spreads.items():
        noise = np.random.default_rng([zlib.crc32(name.encode()), seed]).standard_normal(out[name].shape)
        drawn = base * np.exp(spread * noise) if base else spread * noise
        out[name] = jnp.asarray(drawn.astype(out[name].dtype))
    for name, factor in factors.items():
        out[name] = (out[name] * factor).astype(out[name].dtype)
    return out
```

```python
from contextlib import ExitStack, contextmanager

import numpy as np
import concourse.bass as bass
from concourse import mybir

ALU = mybir.AluOpType
ACT = mybir.ActivationFunctionType
AX = mybir.AxisListType
F32 = mybir.dt.float32
U32 = mybir.dt.uint32
I32 = mybir.dt.int32

P = 128
D = 1024
KC = D // P
T = 256
TT = T // P
FF = 2816
TILE = 1024
RING = 6
EPS = 1e-6
LN_EPS = 1e-5
ALPHA = (2.0 * 2) ** 0.25
NEG = -1e30

GROUPS, STATE, GH = 64, 64, 16
ST = GROUPS * STATE // P
TAPS = 31
RH, RDK, RDV = 4, 256, 512
NG, NR, HD = 4, 4, 64
NH = NG * NR
CS, CL, CHID = 16, 32, 256
NCMP = T // CS - 1
PH, PK, PTOP = 8, 128, 16

FFN_TILES = 3 * (FF // P)
PEER_TILES = 2 * PK
COLS = {}
_at = 0
for _name, _n in (("norm_pre", 6 * KC), ("s5_d", KC), ("s5_b_glu", KC), ("cv_b_in", 2 * KC), ("cv_dw", TAPS * KC),
                  ("cv_dw_b", KC), ("cv_ln_g", KC), ("cv_ln_b", KC), ("c", KC), ("cmp_b1", 4), ("cmp_pe", 32)):
    COLS[_name] = _at
    _at += _n
NCOLS = _at
ROWS = {}
for _i, _name in enumerate(["post00", "post01", "post02", "post10", "post11", "post12", "cv_b_out"]
                           + [f"ada{l}{j}" for l in range(2) for j in range(6)] + ["kvada0", "kvada1"]
                           + [f"ln_{a}{l}{j}" for l in range(2) for j in range(2) for a in "gb"]):
    ROWS[_name] = _i


class Kernel:
    pass


class Ring:

    def __init__(self, k, landed, tiles_done, total):
        self.k, self.landed, self.tiles_done, self.total = k, landed, tiles_done, total
        self.issued = 0
        self.next = 0

    def take(self, n):
        first = self.next
        self.next += n
        return first

    def buf(self, n):
        return self.k.ring[:, n % RING, :]

    def wait_landed(self, pe, n, i=0):
        pe.wait_ge(self.landed[n % RING], 16 * (n // RING + 1) + 16 * i)

    def wait_done(self, eng, n, more=0):
        eng.wait_ge(self.tiles_done, n + 1 + more)

    def stream(self, sp):
        end = min(self.total, self.next + RING)
        n = self.issued

        def load(n, i=0):
            if not isinstance(i, int) or n >= RING:
                self.wait_done(sp, n - RING, i * RING if not isinstance(i, int) else 0)
            src = self.k.dram["wts"][n + i * RING] if not isinstance(i, int) else self.k.dram["wts"][n]
            sp.dma_start(self.buf(n), src).then_inc(self.landed[n % RING], 16)

        while n < end and n < RING:
            load(n)
            n += 1
        rounds = (end - n) // RING
        if rounds > 1:
            with sp.Fori(0, rounds) as i:
                for j in range(RING):
                    load(n + j, i)
            n += rounds * RING
        while n < end:
            load(n)
            n += 1
        self.issued = end


@contextmanager
def stage(k, names):
    nc = k.nc
    k.stages += 1
    sems = {n: nc.alloc_semaphore(f"{n}_{k.stages}") for n in names.split()}
    with nc.Block(no_gpsimd_drain=True) as block:
        yield sems, block
    nc.clear_and_free_semaphores(list(sems.values()))
    nc.all_engine_barrier()


class Steps:

    def __init__(self, eng, sem):
        self.eng, self.sem, self.n = eng, sem, 0

    def done(self, ins):
        ins.then_inc(self.sem, 1)
        self.n += 1

    def wait(self):
        self.eng.wait_ge(self.sem, self.n)

    def link(self, ins):
        self.done(ins)
        self.wait()


def rounds(eng, n, unroll, body):
    full = n // unroll
    for j in range(min(unroll, n)):
        body(j, j, 0)
    if full > 2:
        with eng.Fori(1, full) as i:
            for j in range(unroll):
                body(i * unroll + j, j, i)
        first = full * unroll
    else:
        first = unroll
    for f in range(first, n):
        body(f, f % unroll, f // unroll)


def known(v):
    return isinstance(v, int)


def col(k, name, i):
    at = COLS[name]
    return k.cols[:, at + i:at + i + 1] if known(i) else k.cols[:, bass.ds(i + at, 1)]


def bc(ap, shape):
    return ap.broadcast_to(shape)



def to_columns(k, rms=None, mod=None):
    with stage(k, "squared rooted normed turned dve act_ld") as (s, block):
        @block.sync
        def _(sp):
            k.w.stream(sp)

        @block.scalar
        def _(act):
            if rms is not None:
                for tt in range(TT):
                    act.activation(k.tmp[:, tt, :], k.x[:, tt, :], ACT.Square, scale=1.0 / 32,
                                   accum_out=k.stat[:, tt:tt + 1]).then_inc(s["squared"], 1)
                act.wait_ge(s["dve"], 1)
                act.activation(k.stat[:, 4:6], k.stat[:, 2:4], ACT.Sqrt).then_inc(s["rooted"], 1)
            for kp in range(4):
                act.wait_ge(s["turned"], kp + 1)
                for kc in (2 * kp, 2 * kp + 1):
                    at = (kc % 2) * T
                    scale = col(k, "norm_pre", rms * KC + kc) if rms is not None else 1.0
                    act.activation(k.hT[:, kc, :], k.ps[:, 4 + kp, at:at + T], ACT.Copy, scale=scale)

        @block.vector
        def _(v):
            st = Steps(v, s["dve"])
            if rms is not None:
                v.wait_ge(s["squared"], TT)
                st.done(v.tensor_scalar(k.stat[:, 2:4], k.stat[:, 0:2], EPS, None, ALU.add))
                v.wait_ge(s["rooted"], 1)
                st.link(v.reciprocal(k.stat[:, 6:8], k.stat[:, 4:6]))
                for tt in range(TT):
                    v.tensor_scalar(k.tmp[:, tt, :], k.x[:, tt, :], k.stat[:, 6 + tt:7 + tt], None,
                                    ALU.mult).then_inc(s["normed"], 1)
            else:
                sc, sh = mod
                for tt in range(TT):
                    st.link(v.scalar_tensor_tensor(k.tmp[:, tt, :], sc, 1.0, k.x[:, tt, :], ALU.add, ALU.mult))
                    v.tensor_tensor(k.tmp[:, tt, :], k.tmp[:, tt, :], sh, ALU.add).then_inc(s["normed"], 1)

        @block.tensor
        def _(pe):
            pe.wait_ge(s["normed"], TT)
            for kp in range(4):
                for kc in (2 * kp, 2 * kp + 1):
                    for tt in range(TT):
                        at = (kc % 2) * T + tt * P
                        last = pe.transpose(k.ps[:, 4 + kp, at:at + P], k.tmp[:, tt, kc * P:(kc + 1) * P], k.ident[:, :])
                last.then_inc(s["turned"], 1)


def rows_to_columns(k, src, dst, n):
    with stage(k, "turned copied") as (s, block):
        @block.sync
        def _(sp):
            k.w.stream(sp)

        @block.tensor
        def _(pe):
            for c2 in range(n // 2):
                if c2 >= 4:
                    pe.wait_ge(s["copied"], c2 - 3)
                for c in (2 * c2, 2 * c2 + 1):
                    for tt in range(TT):
                        at = (c % 2) * T + tt * P
                        last = pe.transpose(k.ps[:, 4 + c2 % 4, at:at + P], src[:, tt, c * P:(c + 1) * P], k.ident[:, :])
                last.then_inc(s["turned"], 1)

        @block.vector
        def _(v):
            for c2 in range(n // 2):
                v.wait_ge(s["turned"], c2 + 1)
                v.tensor_copy(dst[:, 2 * c2:2 * c2 + 2, :],
                              k.ps[:, 4 + c2 % 4, :].rearrange("p (c t) -> p c t", c=2)).then_inc(s["copied"], 1)


def residual_rms(k, row, coef, bias_row=None):
    with stage(k, "g_in b_in squared rooted dve biased") as (s, block):
        @block.sync
        def _(sp):
            sp.dma_start(k.row[:, 0, :], k.dram["rows"][ROWS[row]]).then_inc(s["g_in"], 16)
            if bias_row:
                sp.dma_start(k.row[:, 1, :], k.dram["rows"][ROWS[bias_row]]).then_inc(s["b_in"], 16)
            k.w.stream(sp)

        def y(b):
            if bias_row:
                return k.tmp[:, b // 2, (b % 2) * 512:(b % 2 + 1) * 512]
            return k.ps[:, b, :]

        @block.scalar
        def _(act):
            for b in range(4):
                if bias_row:
                    act.wait_ge(s["biased"], b + 1)
                act.activation(k.ps[:, 4 + b, :], y(b), ACT.Square, scale=1.0 / 32,
                               accum_out=k.stat[:, b:b + 1]).then_inc(s["squared"], 1)
            act.wait_ge(s["dve"], 2)
            act.activation(k.stat[:, 8:10], k.stat[:, 6:8], ACT.Sqrt).then_inc(s["rooted"], 1)

        @block.vector
        def _(v):
            if bias_row:
                v.wait_ge(s["b_in"], 16)
                for b in range(4):
                    v.tensor_tensor(y(b), k.ps[:, b, :], k.row[:, 1, (b % 2) * 512:(b % 2 + 1) * 512],
                                    ALU.add).then_inc(s["biased"], 1)
            st = Steps(v, s["dve"])
            v.wait_ge(s["squared"], 4)
            ss = k.stat[:, 0:4].rearrange("p (t h) -> p t h", h=2)
            st.link(v.tensor_tensor(k.stat[:, 4:6], ss[:, :, 0], ss[:, :, 1], ALU.add))
            st.done(v.tensor_scalar(k.stat[:, 6:8], k.stat[:, 4:6], EPS, None, ALU.add))
            v.wait_ge(s["rooted"], 1)
            st.link(v.reciprocal(k.stat[:, 10:12], k.stat[:, 8:10]))
            st.link(v.tensor_scalar(k.stat[:, 12:14], k.stat[:, 10:12], float(coef), None, ALU.mult))
            v.wait_ge(s["g_in"], 16)
            if bias_row:
                v.wait_ge(s["biased"], 4)
            for b in range(4):
                tt, half = b // 2, slice((b % 2) * 512, (b % 2 + 1) * 512)
                st.link(v.scalar_tensor_tensor(k.tmp[:, tt, half], y(b), k.stat[:, 12 + tt:13 + tt],
                                               k.row[:, 0, half], ALU.mult, ALU.mult))
                st.done(v.tensor_tensor(k.x[:, tt, half], k.x[:, tt, half], k.tmp[:, tt, half], ALU.add))


def residual_ln(k, gate, ln_g, ln_b):
    with stage(k, "g_in b_in rooted eps_in dve") as (s, block):
        @block.sync
        def _(sp):
            sp.dma_start(k.row[:, 0, :], k.dram["rows"][ROWS[ln_g]]).then_inc(s["g_in"], 16)
            sp.dma_start(k.row[:, 1, :], k.dram["rows"][ROWS[ln_b]]).then_inc(s["b_in"], 16)
            k.w.stream(sp)

        @block.scalar
        def _(act):
            act.wait_ge(s["eps_in"], 1)
            act.activation(k.stat[:, 34:36], k.stat[:, 32:34], ACT.Sqrt).then_inc(s["rooted"], 1)

        @block.vector
        def _(v):
            st = Steps(v, s["dve"])
            for b in range(4):
                tt, half = b // 2, slice((b % 2) * 512, (b % 2 + 1) * 512)
                st.done(v.tensor_tensor(k.tmp[:, tt, half], k.ps[:, b, :], gate[:, half], ALU.mult))
            st.wait()
            for tt in range(TT):
                st.done(v.scalar_tensor_tensor(k.x[:, tt, :], k.x[:, tt, :], ALPHA, k.tmp[:, tt, :], ALU.mult, ALU.add))
            st.wait()
            for b in range(4):
                st.done(v.bn_stats(k.stat[:, 6 * b:6 * b + 6], k.x[:, b // 2, (b % 2) * 512:(b % 2 + 1) * 512]))
            st.wait()
            for tt in range(TT):
                st.done(v.bn_aggr(k.stat[:, 24 + 2 * tt:26 + 2 * tt], k.stat[:, 12 * tt:12 * tt + 12]))
            st.wait()
            mv = k.stat[:, 24:28].rearrange("p (t c) -> p t c", c=2)
            v.tensor_scalar(k.stat[:, 32:34], mv[:, :, 1], LN_EPS, None, ALU.add).then_inc(s["eps_in"], 1)
            v.wait_ge(s["rooted"], 1)
            st.link(v.reciprocal(k.stat[:, 36:38], k.stat[:, 34:36]))
            for tt in range(TT):
                st.done(v.tensor_scalar(k.x[:, tt, :], k.x[:, tt, :], k.stat[:, 24 + 2 * tt:25 + 2 * tt],
                                        k.stat[:, 36 + tt:37 + tt], ALU.subtract, ALU.mult))
            st.wait()
            v.wait_ge(s["g_in"], 16)
            v.wait_ge(s["b_in"], 16)
            for tt in range(TT):
                st.done(v.tensor_tensor(k.x[:, tt, :], k.x[:, tt, :], k.row[:, 0, :], ALU.mult))
            st.wait()
            for tt in range(TT):
                st.done(v.tensor_tensor(k.x[:, tt, :], k.x[:, tt, :], k.row[:, 1, :], ALU.add))



def project_columns(k, n, evacuate):
    first = k.w.take(n)
    with stage(k, "stored") as (s, block):
        @block.sync
        def _(sp):
            k.w.stream(sp)

        @block.tensor
        def _(pe):
            def tile(f, j, i):
                k.w.wait_landed(pe, first + j, i)
                if not known(f) or f >= 3:
                    pe.wait_ge(s["stored"], f - 2)
                w = k.w.buf(first + j)
                for kc in range(KC):
                    last = pe.matmul(k.ps[:, 4 + j % 3, 0:T], w[:, kc * P:(kc + 1) * P], k.hT[:, kc, :],
                                     start=kc == 0, stop=kc == KC - 1)
                last.then_inc(k.w.tiles_done, 1)
            rounds(pe, n, RING, tile)

        @block.scalar
        def _(act):
            for f in range(n):
                k.w.wait_done(act, first + f)
                evacuate(act, f, k.ps[:, 4 + f % 3, 0:T]).then_inc(s["stored"], 1)


def project_rows(k, nk, lhsT, groups=1, evacuate=None):
    first = k.w.take(nk * groups)
    with stage(k, "stored") as (s, block):
        @block.sync
        def _(sp):
            k.w.stream(sp)

        @block.tensor
        def _(pe):
            for g in range(groups):
                if g >= 2:
                    pe.wait_ge(s["stored"], 4 * (g - 1))
                for kc in range(nk):
                    n = first + g * nk + kc
                    k.w.wait_landed(pe, n)
                    for tt in range(TT):
                        for half in range(2):
                            last = pe.matmul(k.ps[:, 4 * (g % 2) + 2 * tt + half, :], lhsT(kc, tt),
                                             k.w.buf(n)[:, half * 512:(half + 1) * 512],
                                             start=kc == 0, stop=kc == nk - 1)
                    last.then_inc(k.w.tiles_done, 1)

        if evacuate:
            @block.scalar
            def _(act):
                for g in range(groups):
                    k.w.wait_done(act, first + (g + 1) * nk - 1)
                    for tt in range(TT):
                        for half in range(2):
                            evacuate(act, g, tt, half, k.ps[:, 4 * (g % 2) + 2 * tt + half, :]).then_inc(s["stored"], 1)


def modulation(k, dst, names):
    ng = len(names)
    first = k.w.take(KC * ng)
    cb = k.tmp[:, 0, :].rearrange("p (c m) -> p c m", c=KC)
    rows = k.big[:, 18432:18432 + ng * D].rearrange("p (g n) -> p g n", g=ng)
    with stage(k, "rows_in silu wide stored") as (s, block):
        @block.sync
        def _(sp):
            for j, name in enumerate(names):
                sp.dma_start(rows[:, j, :], k.dram["rows"][ROWS[name]]).then_inc(s["rows_in"], 16)
            k.w.stream(sp)

        @block.scalar
        def _(act):
            act.activation(k.stat[:, 0:KC], k.cols[:, COLS["c"]:COLS["c"] + KC], ACT.Silu).then_inc(s["silu"], 1)

        @block.vector
        def _(v):
            v.wait_ge(s["silu"], 1)
            v.tensor_copy(cb, bc(k.stat[:, 0:KC].unsqueeze(2), [P, KC, P])).then_inc(s["wide"], 1)
            v.wait_ge(s["rows_in"], 16 * ng)
            for g in range(ng):
                k.w.wait_done(v, first + (g + 1) * KC - 1)
                for half in range(2):
                    hs = slice(half * 512, (half + 1) * 512)
                    v.tensor_tensor(dst(g)[:, hs], k.ps[:, 2 * (g % 4) + half, :], rows[:, g, hs],
                                    ALU.add).then_inc(s["stored"], 1)

        @block.tensor
        def _(pe):
            pe.wait_ge(s["wide"], 1)
            for g in range(ng):
                if g >= 4:
                    pe.wait_ge(s["stored"], 2 * (g - 3))
                for kc in range(KC):
                    n = first + g * KC + kc
                    k.w.wait_landed(pe, n)
                    for half in range(2):
                        last = pe.matmul(k.ps[:, 2 * (g % 4) + half, :], cb[:, kc, :],
                                         k.w.buf(n)[:, half * 512:(half + 1) * 512], start=kc == 0, stop=kc == KC - 1)
                    last.then_inc(k.w.tiles_done, 1)



def gated_mlp(k, items, ups, func, factor):
    per = ups + 1
    first = k.w.take(per * items)
    bufs = RING // per
    with stage(k, "activated gated") as (s, block):
        @block.sync
        def _(sp):
            k.w.stream(sp)

        @block.tensor
        def _(pe):
            def up(f, buf, n, i):
                if not known(f) or f >= bufs:
                    pe.wait_ge(s["gated"], f - bufs + 1)
                for u in range(ups):
                    k.w.wait_landed(pe, n + u, i)
                    w = k.w.buf(n + u)
                    for kc in range(KC):
                        last = pe.matmul(k.ps[:, 4 + buf, u * T:(u + 1) * T], w[:, kc * P:(kc + 1) * P], k.hT[:, kc, :],
                                         start=kc == 0, stop=kc == KC - 1)
                    last.then_inc(k.w.tiles_done, 1)

            def down(f, buf, n, i, start=False, stop=False):
                k.w.wait_landed(pe, n, i)
                pe.wait_ge(s["gated"], f + 1)
                w = k.w.buf(n)
                for tt in range(TT):
                    for half in range(2):
                        last = pe.matmul(k.ps[:, 2 * tt + half, :], k.gatedT[:, buf, tt * P:(tt + 1) * P],
                                         w[:, half * 512:(half + 1) * 512], start=start, stop=stop)
                last.then_inc(k.w.tiles_done, 1)

            def both(g, j, i):
                n = first + ups + j * per
                up(g + 1, (j + 1) % bufs, n, i)
                down(g, j % bufs, n + ups, i, start=known(g) and g == 0)

            up(0, 0, first, 0)
            rounds(pe, items - 1, bufs, both)
            f = items - 1
            down(f, f % bufs, first + per * items - 1, 0, stop=True)

        @block.scalar
        def _(act):
            def item(f, j, i):
                if known(f) and f == 0:
                    k.w.wait_done(act, first + ups - 1)
                else:
                    k.w.wait_done(act, first + ups - 2, f * per + 0)
                if not known(f) or f >= bufs:
                    act.wait_ge(s["gated"], f - bufs + 1)
                act.activation(k.acted[:, j, :], k.ps[:, 4 + j, 0:T], func).then_inc(s["activated"], 1)
            rounds(act, items, bufs, item)

        @block.vector
        def _(v):
            def item(f, j, i):
                v.wait_ge(s["activated"], f + 1)
                if not known(f) or f >= bufs:
                    k.w.wait_done(v, first + 2 * ups - bufs * per, f * per)
                v.tensor_tensor(k.gatedT[:, j, :], k.acted[:, j, :], factor(f, j), ALU.mult).then_inc(s["gated"], 1)
            rounds(v, items, bufs, item)


def ffn(k, i, j):
    to_columns(k, rms=3 * i + 2 * j)
    gated_mlp(k, FF // P, 2, ACT.Silu, lambda f, b: k.ps[:, 4 + b, T:2 * T])
    residual_rms(k, f"post{i}{2 * j}", 0.5)



def s5(k):
    big = k.big
    uT = big[:, 0:2048].rearrange("p (c t) -> p c t", c=KC)
    yT = big[:, 2048:4096].rearrange("p (c t) -> p c t", c=KC)
    cosT = big[:, 4096:12288].rearrange("p (s t) -> p s t", s=ST)
    sinT = big[:, 12288:20480].rearrange("p (s t) -> p s t", s=ST)
    prod = big[:, 20480:24576].rearrange("p (s t) -> p s t", s=ST)
    b_re = big[:, 24576:25088].rearrange("p (s h) -> p s h", s=ST)
    b_im = big[:, 25088:25600].rearrange("p (s h) -> p s h", s=ST)
    c_re = big[:, 25600:26112].rearrange("p (s h) -> p s h", s=ST)
    c_im = big[:, 26112:26624].rearrange("p (s h) -> p s h", s=ST)
    par = big[:, 26624:26624 + 40 * ST].rearrange("p (n s) -> p n s", s=ST)
    bx = [big[:, 28672 + 1024 * n:29696 + 1024 * n].rearrange("p (s h) -> p s h", s=ST) for n in range(2)]
    cx = [big[:, 30720 + 1024 * n:31744 + 1024 * n].rearrange("p (s h) -> p s h", s=ST) for n in range(2)]
    bT = [big[:, 20480 + 1024 * n:21504 + 1024 * n].rearrange("p (c m) -> p c m", c=KC) for n in range(2)]
    at, bt, zin = (big[:, 22528 + 512 * n:23040 + 512 * n] for n in range(3))
    z2 = [k.tmp[:, 0, 512 * n:512 * n + 512] for n in range(2)]
    st2 = [k.tmp[:, 1, 512 * n:512 * n + 512] for n in range(2)]
    ga, gb = k.row[:, 0, 0:512], k.row[:, 0, 512:1024]

    to_columns(k, rms=1)
    project_columns(k, KC, lambda act, f, ps: act.activation(uT[:, f, :], ps, ACT.Copy))

    (A_RE, A_IM, DT, MAG, TH, RED, KQ, SINH, COS, SIN, AB_RE, AB_IM, NR_, DEN, T0, T1, T2, T3, F_RE, F_IM) = range(20)
    POW = 20

    with stage(k, "loaded dt_exp mag_exp red sines zeroed dve") as (s, block):
        @block.sync
        def _(sp):
            for n, (dst, src) in enumerate(((par[:, A_RE, :], k.dram["s5_par"][0]), (par[:, A_IM, :], k.dram["s5_par"][1]),
                                            (par[:, DT, :], k.dram["s5_par"][2]), (b_re, k.dram["s5_bc"][0]), (b_im, k.dram["s5_bc"][1]),
                                            (c_re, k.dram["s5_bc"][2]), (c_im, k.dram["s5_bc"][3]))):
                sp.dma_start(dst, src).then_inc(s["loaded"], 16)
            k.w.stream(sp)

        @block.scalar
        def _(act):
            act.wait_ge(s["loaded"], 7 * 16)
            act.activation(par[:, DT, :], par[:, DT, :], ACT.Exp).then_inc(s["dt_exp"], 1)
            act.wait_ge(s["red"], 1)
            act.activation(par[:, MAG, :], par[:, MAG, :], ACT.Exp).then_inc(s["mag_exp"], 1)
            act.wait_ge(s["red"], 2)
            act.activation(par[:, SIN, :], par[:, RED, :], ACT.Sin).then_inc(s["sines"], 1)
            act.activation(par[:, SINH, :], par[:, RED, :], ACT.Sin, scale=0.5).then_inc(s["sines"], 1)

        @block.gpsimd
        def _(pool):
            for m in (*bx, *cx):
                pool.memset(m, 0.0).then_inc(s["zeroed"], 1)

        @block.vector
        def _(v):
            st = Steps(v, s["dve"])
            q = lambda n: par[:, n, :]
            tt = lambda o, a, b, op: st.link(v.tensor_tensor(q(o), q(a), q(b), op))
            v.wait_ge(s["dt_exp"], 1)
            v.tensor_tensor(q(MAG), q(DT), q(A_RE), ALU.mult).then_inc(s["red"], 1)
            tt(TH, DT, A_IM, ALU.mult)
            st.link(v.tensor_scalar(q(KQ), q(TH), float(np.float32(1 / (2 * np.pi))), 12582912.0, ALU.mult, ALU.add))
            st.link(v.tensor_scalar(q(KQ), q(KQ), -12582912.0, None, ALU.add))
            c1 = 6.28125
            c2 = float(np.float32(np.floor((2 * np.pi - c1) * 2 ** 21) / 2 ** 21))
            c3 = float(np.float32(2 * np.pi - c1 - c2))
            st.link(v.scalar_tensor_tensor(q(RED), q(KQ), -c1, q(TH), ALU.mult, ALU.add))
            st.link(v.scalar_tensor_tensor(q(RED), q(KQ), -c2, q(RED), ALU.mult, ALU.add))
            st.link(v.scalar_tensor_tensor(q(RED), q(KQ), -c3, q(RED), ALU.mult, ALU.add))
            v.tensor_scalar(q(RED), q(RED), 3.1415925, -3.1415925, ALU.min, ALU.max).then_inc(s["red"], 1)
            v.wait_ge(s["sines"], 2)
            v.wait_ge(s["mag_exp"], 1)
            tt(COS, SINH, SINH, ALU.mult)
            st.link(v.tensor_scalar(q(COS), q(COS), -2.0, 1.0, ALU.mult, ALU.add))
            tt(AB_RE, MAG, COS, ALU.mult)
            tt(AB_IM, MAG, SIN, ALU.mult)
            st.link(v.tensor_scalar(q(NR_), q(AB_RE), -1.0, None, ALU.add))
            tt(T0, A_RE, A_RE, ALU.mult)
            tt(T1, A_IM, A_IM, ALU.mult)
            tt(DEN, T0, T1, ALU.add)
            st.link(v.reciprocal(q(DEN), q(DEN)))
            tt(T0, NR_, A_RE, ALU.mult)
            tt(T1, AB_IM, A_IM, ALU.mult)
            tt(T0, T0, T1, ALU.add)
            tt(F_RE, T0, DEN, ALU.mult)
            tt(T2, AB_IM, A_RE, ALU.mult)
            tt(T3, NR_, A_IM, ALU.mult)
            tt(T2, T2, T3, ALU.subtract)
            tt(F_IM, T2, DEN, ALU.mult)
            v.wait_ge(s["zeroed"], 4)
            fr, fi = (bc(q(f).unsqueeze(2), [P, ST, GH]) for f in (F_RE, F_IM))
            pr = k.tmp[:, :, :].rearrange("p a (b n) -> p (a b) n", b=2)
            w = lambda n: pr[:, n, :].rearrange("p (s h) -> p s h", s=ST)
            st.done(v.tensor_tensor(w(0), b_re, fr, ALU.mult))
            st.done(v.tensor_tensor(w(1), b_im, fi, ALU.mult))
            st.done(v.tensor_tensor(w(2), b_im, fr, ALU.mult))
            st.done(v.tensor_tensor(w(3), b_re, fi, ALU.mult))
            st.wait()
            for h in range(2):
                ps, cs = slice(64 * h, 64 * h + 64), slice(GH * h, GH * h + GH)
                st.done(v.tensor_tensor(bx[0][ps, :, cs], w(0)[ps], w(1)[ps], ALU.subtract))
                st.done(v.tensor_tensor(bx[1][ps, :, cs], w(2)[ps], w(3)[ps], ALU.add))
                st.done(v.tensor_copy(cx[0][ps, :, cs], c_re[ps]))
                st.done(v.tensor_scalar(cx[1][ps, :, cs], c_im[ps], -1.0, None, ALU.mult))
            st.done(v.memset(cosT[:, :, 0:1], 1.0))
            st.done(v.memset(sinT[:, :, 0:1], 0.0))
            pc, psn = COS, SIN
            st.wait()
            for n in range(8):
                m = 1 << n
                cb, sb = (bc(q(a).unsqueeze(2), [P, ST, m]) for a in (pc, psn))
                lo, hi = slice(0, m), slice(m, 2 * m)
                pp = prod[:, :, 0:m]
                st.done(v.tensor_tensor(cosT[:, :, hi], cosT[:, :, lo], cb, ALU.mult))
                st.link(v.tensor_tensor(pp, sinT[:, :, lo], sb, ALU.mult))
                st.done(v.tensor_tensor(cosT[:, :, hi], cosT[:, :, hi], pp, ALU.subtract))
                st.done(v.tensor_tensor(sinT[:, :, hi], sinT[:, :, lo], cb, ALU.mult))
                st.wait()
                st.link(v.tensor_tensor(pp, cosT[:, :, lo], sb, ALU.mult))
                st.link(v.tensor_tensor(sinT[:, :, hi], sinT[:, :, hi], pp, ALU.add))
                if n < 7:
                    nc_, ns_ = POW + 2 * n, POW + 2 * n + 1
                    tt(T0, pc, pc, ALU.mult)
                    tt(T1, psn, psn, ALU.mult)
                    tt(nc_, T0, T1, ALU.subtract)
                    tt(T0, pc, psn, ALU.mult)
                    st.link(v.tensor_scalar(q(ns_), q(T0), 2.0, None, ALU.mult))
                    pc, psn = nc_, ns_

    with stage(k, "turned bT_in") as (s, block):
        @block.sync
        def _(sp):
            k.w.stream(sp)

        @block.tensor
        def _(pe):
            for n in range(2):
                for c in range(KC):
                    last = pe.transpose(k.ps[:, 2 * n + c // 4, (c % 4) * P:(c % 4 + 1) * P],
                                        bx[n][:, 4 * c:4 * c + 4, :].rearrange("p s h -> p (s h)"), k.ident[:, :])
                last.then_inc(s["turned"], 1)

        @block.vector
        def _(v):
            for n in range(2):
                v.wait_ge(s["turned"], n + 1)
                v.tensor_copy(bT[n], k.ps[:, 2 * n:2 * n + 2, :].rearrange("p b (c m) -> p (b c) m", m=P))

    with stage(k, "bu_ready bu_read dve zed back pool read y_ready y_read gel") as (s, block):
        @block.sync
        def _(sp):
            k.w.stream(sp)

        @block.tensor
        def _(pe):
            def bu(t):
                c, j = t // 4, t % 4
                rows = slice(32 * j, 32 * j + 32)
                if t >= 2:
                    pe.wait_ge(s["bu_read"], t - 1)
                for n in range(2):
                    last = pe.matmul(k.ps[:, 4 + t % 2, n * T:(n + 1) * T], bT[n][rows, c, :], uT[rows, c, :],
                                     start=True, stop=True)
                last.then_inc(s["bu_ready"], 1)

            def y(t):
                c, j = t // 4, t % 4
                pe.wait_ge(s["back"], t + 1)
                if j == 0 and c >= 2:
                    pe.wait_ge(s["y_read"], c - 1)
                for n in range(2):
                    last = pe.matmul(k.ps[32 * j:32 * j + 32, c % 2, 0:T], cx[n][:, t, :],
                                     st2[t % 2][:, n * T:(n + 1) * T], start=n == 0, stop=n == 1)
                last.then_inc(s["y_ready"], 1)

            bu(0)
            for t in range(ST):
                if t + 1 < ST:
                    bu(t + 1)
                y(t)

        two = lambda ap: ap.rearrange("p (n t) -> p n t", n=2)

        @block.vector
        def _(v):
            st = Steps(v, s["dve"])
            for t in range(ST):
                v.wait_ge(s["bu_ready"], t + 1)
                cb, sb = (bc(x[:, t, :].unsqueeze(1), [P, 2, T]) for x in (cosT, sinT))
                bu = k.ps[:, 4 + t % 2, :]
                st.done(v.tensor_tensor(two(at), two(bu), cb, ALU.mult))
                v.tensor_tensor(two(bt), two(bu), sb, ALU.mult).then_inc(s["bu_read"], 1)
                v.wait_ge(s["bu_read"], t + 1)
                st.wait()
                st.done(v.tensor_tensor(zin[:, 0:T], at[:, 0:T], bt[:, T:2 * T], ALU.add))
                st.done(v.tensor_tensor(zin[:, T:2 * T], at[:, T:2 * T], bt[:, 0:T], ALU.subtract))
                st.wait()
                if t >= 2:
                    v.wait_ge(s["read"], t - 1)
                mag = bc(par[:, MAG, t:t + 1], [P, T])
                for n in range(2):
                    last = v.tensor_tensor_scan(z2[t % 2][:, n * T:(n + 1) * T], mag, zin[:, n * T:(n + 1) * T], 0.0,
                                                ALU.mult, ALU.add)
                    if n == 0:
                        st.done(last)
                last.then_inc(s["zed"], 1)

        @block.gpsimd
        def _(pool):
            for t in range(ST):
                v = pool
                v.wait_ge(s["zed"], t + 1)
                cb, sb = (bc(x[:, t, :].unsqueeze(1), [P, 2, T]) for x in (cosT, sinT))
                z = z2[t % 2]
                if t >= 1:
                    v.wait_ge(s["back"], t)
                v.tensor_tensor(two(ga), two(z), cb, ALU.mult).then_inc(s["pool"], 1)
                v.tensor_tensor(two(gb), two(z), sb, ALU.mult).then_inc(s["read"], 1)
                v.wait_ge(s["pool"], 2 * t + 1)
                v.wait_ge(s["read"], t + 1)
                if t >= 2:
                    v.wait_ge(s["y_ready"], t - 1)
                v.tensor_tensor(st2[t % 2][:, 0:T], ga[:, 0:T], gb[:, T:2 * T], ALU.subtract).then_inc(s["pool"], 1)
                v.wait_ge(s["pool"], 2 * t + 2)
                v.tensor_tensor(st2[t % 2][:, T:2 * T], ga[:, T:2 * T], gb[:, 0:T], ALU.add).then_inc(s["back"], 1)

        @block.scalar
        def _(act):
            for c in range(KC):
                act.wait_ge(s["y_ready"], 4 * c + 4)
                act.activation(yT[:, c, :], uT[:, c, :], ACT.Copy, scale=col(k, "s5_d", c)).then_inc(s["gel"], 1)
                act.wait_ge(s["gel"], c + 1)
                act.activation(k.hT[:, :, :][:, c, :], k.ps[:, c % 2, 0:T], ACT.Copy).then_inc(s["y_read"], 1)

    with stage(k, "sum") as (s, block):
        @block.vector
        def _(v):
            v.tensor_tensor(yT, yT, k.hT[:, :, :], ALU.add).then_inc(s["sum"], 1)

        @block.scalar
        def _(act):
            act.wait_ge(s["sum"], 1)
            act.activation(k.hT[:, :, :], yT, ACT.Gelu_apprx_tanh)

    project_columns(k, KC, lambda act, f, ps: act.activation(uT[:, f, :], ps, ACT.Sigmoid, bias=col(k, "s5_b_glu", f)))
    with stage(k, "gated") as (s, block):
        @block.vector
        def _(v):
            v.tensor_tensor(yT, k.hT[:, :, :], uT, ALU.mult).then_inc(s["gated"], 1)
    project_rows(k, KC, lambda kc, tt: yT[:, kc, tt * P:(tt + 1) * P])
    residual_rms(k, "post01", 1.0)



def conv(k):
    big = k.big
    PAD = TAPS - 1
    L = PAD + T
    a = big[:, 0:2048].rearrange("p (c t) -> p c t", c=KC)
    g = big[:, 2048:4096].rearrange("p (c t) -> p c t", c=KC)
    zp = big[:, 4096:4096 + KC * L].rearrange("p (c t) -> p c t", c=KC)
    z = big[:, 8192:10240].rearrange("p (c t) -> p c t", c=KC)
    sq = big[:, 10240:12288].rearrange("p (c t) -> p c t", c=KC)
    mean_w = big[:, 12288:12416]
    sd = big[:, 12416:12672]
    rstd = big[:, 12672:12928]
    to_columns(k, rms=4)
    both = big[:, 0:4096].rearrange("p (c t) -> p c t", c=2 * KC)
    project_columns(k, 2 * KC, lambda act, f, ps: act.activation(
        both[:, f, :], ps, ACT.Identity if f < KC else ACT.Sigmoid, bias=col(k, "cv_b_in", f)))
    with stage(k, "dve tap mean_in centred squared_ var_in rooted normed wset") as (s, block):
        @block.sync
        def _(sp):
            k.w.stream(sp)

        @block.vector
        def _(v):
            st = Steps(v, s["dve"])
            st.done(v.memset(mean_w, 1.0 / D))
            st.done(v.memset(zp[:, :, 0:PAD], 0.0))
            st.done(v.tensor_tensor(zp[:, :, PAD:L], a, g, ALU.mult))
            st.wait()
            for f in range(KC):
                v.tensor_scalar(z[:, f, :], zp[:, f, 0:T], col(k, "cv_dw", f), col(k, "cv_dw_b", f), ALU.mult,
                                ALU.add).then_inc(s["tap"], 1)
            with v.Fori(1, TAPS) as i:
                for f in range(KC):
                    v.wait_ge(s["tap"], i * KC + f - KC + 1)
                    v.scalar_tensor_tensor(z[:, f, :], zp[:, f, bass.ds(i, T)], col(k, "cv_dw", i * KC + f),
                                           z[:, f, :], ALU.mult, ALU.add).then_inc(s["tap"], 1)
            v.wait_ge(s["mean_in"], 1)
            mean = bc(k.ps[:, 4, 0:T].unsqueeze(1), [P, KC, T])
            v.tensor_tensor(z, z, mean, ALU.subtract).then_inc(s["centred"], 1)
            v.wait_ge(s["centred"], 1)
            v.tensor_tensor(sq, z, z, ALU.mult).then_inc(s["squared_"], 1)
            v.wait_ge(s["var_in"], 1)
            st.done(v.tensor_scalar(sd, k.ps[:, 5, 0:T], EPS, None, ALU.add))
            v.wait_ge(s["rooted"], 1)
            st.link(v.reciprocal(rstd, sd))
            v.tensor_tensor(z, z, bc(rstd.unsqueeze(1), [P, KC, T]), ALU.mult).then_inc(s["normed"], 1)

        @block.tensor
        def _(pe):
            pe.wait_ge(s["tap"], TAPS * KC)
            for f in range(KC):
                last = pe.matmul(k.ps[:, 4, 0:T], mean_w, z[:, f, :], start=f == 0, stop=f == KC - 1)
            last.then_inc(s["mean_in"], 1)
            pe.wait_ge(s["squared_"], 1)
            for f in range(KC):
                last = pe.matmul(k.ps[:, 5, 0:T], mean_w, sq[:, f, :], start=f == 0, stop=f == KC - 1)
            last.then_inc(s["var_in"], 1)

        @block.scalar
        def _(act):
            act.wait_ge(s["dve"], 4)
            act.activation(sd, sd, ACT.Sqrt).then_inc(s["rooted"], 1)
            act.wait_ge(s["normed"], 1)
            for f in range(KC):
                act.activation(k.hT[:, f, :], z[:, f, :], ACT.Silu, scale=col(k, "cv_ln_g", f), bias=col(k, "cv_ln_b", f))
    project_rows(k, KC, lambda kc, tt: k.hT[:, kc, tt * P:(tt + 1) * P])
    residual_rms(k, "post11", 1.0, bias_row="cv_b_out")



def mod_row(k, j):
    return k.big[:, 26624 + 1024 * j:27648 + 1024 * j]


def retention(k):
    big = k.big
    view = lambda at, c, n: big[:, at:at + c * n].rearrange("p (c t) -> p c t", c=c)
    raw = view(0, 16, T)
    qk = view(4096, 16, T)
    val = view(8192, TT, 2048)
    gate = view(12288, TT, 2048)
    out = view(16384, TT, 2048)
    outT = view(0, 16, T)
    dec = view(20480, RH, 384)
    rope = view(22016, 2, T)
    half = view(22528, 8, T)
    prob = view(24576, 2, 384)
    to_columns(k, mod=(mod_row(k, 1), mod_row(k, 0)))
    project_columns(k, 16, lambda act, f, ps: act.activation(raw[:, f, :], ps, ACT.Copy))

    def store(act, g, tt, h, ps):
        cols = slice((g % 2) * 1024 + h * 512, (g % 2) * 1024 + h * 512 + 512)
        if g < 2:
            return act.activation(val[:, tt, cols], ps, ACT.Copy)
        return act.activation(gate[:, tt, cols], ps, ACT.Silu)
    project_rows(k, KC, lambda kc, tt: k.hT[:, kc, tt * P:(tt + 1) * P], 4, store)

    with stage(k, "loaded dve scored decayed summed st mv eps_in rooted done_ scaled") as (s, block):
        @block.sync
        def _(sp):
            sp.dma_start(dec, k.dram["decay"]).then_inc(s["loaded"], 16)
            sp.dma_start(rope, k.dram["rope"]).then_inc(s["loaded"], 16)
            k.w.stream(sp)

        @block.vector
        def _(v):
            st = Steps(v, s["dve"])
            v.wait_ge(s["loaded"], 32)
            x1 = raw.rearrange("p (h c) t -> p c h t", c=2)[:, 0]
            x2 = raw.rearrange("p (h c) t -> p c h t", c=2)[:, 1]
            y1 = qk.rearrange("p (h c) t -> p c h t", c=2)[:, 0]
            y2 = qk.rearrange("p (h c) t -> p c h t", c=2)[:, 1]
            cb, sb = (bc(rope[:, n, :].unsqueeze(1), [P, 8, T]) for n in range(2))
            st.done(v.tensor_tensor(y1, x1, cb, ALU.mult))
            st.link(v.tensor_tensor(half, x2, sb, ALU.mult))
            st.done(v.tensor_tensor(y1, y1, half, ALU.subtract))
            st.done(v.tensor_tensor(y2, x2, cb, ALU.mult))
            st.wait()
            st.link(v.tensor_tensor(half, x1, sb, ALU.mult))
            v.tensor_tensor(y2, y2, half, ALU.add).then_inc(s["scaled"], 1)
            for h in range(RH):
                v.wait_ge(s["scored"], h + 1)
                if h >= 2:
                    v.wait_ge(s["summed"], h - 1)
                v.tensor_tensor(prob[:, h % 2, :], k.ps[:, 4 + h % 2, 0:384], dec[:, h, :], ALU.mult).then_inc(s["decayed"], 1)
                v.wait_ge(s["summed"], h + 1)
                for tt in range(TT):
                    st.done(v.bn_stats(k.stat[:, 6 * tt:6 * tt + 6], k.ps[:, 2 * (h % 2) + tt, :]))
                st.wait()
                for tt in range(TT):
                    st.done(v.bn_aggr(k.stat[:, 24 + 2 * tt:26 + 2 * tt], k.stat[:, 6 * tt:6 * tt + 6]))
                st.wait()
                mv = k.stat[:, 24:28].rearrange("p (t c) -> p t c", c=2)
                v.tensor_scalar(k.stat[:, 32:34], mv[:, :, 1], LN_EPS, None, ALU.add).then_inc(s["eps_in"], 1)
                v.wait_ge(s["rooted"], h + 1)
                st.link(v.reciprocal(k.stat[:, 36:38], k.stat[:, 34:36]))
                for tt in range(TT):
                    last = v.tensor_scalar(out[:, tt, 512 * h:512 * h + 512], k.ps[:, 2 * (h % 2) + tt, :],
                                           k.stat[:, 24 + 2 * tt:25 + 2 * tt], k.stat[:, 36 + tt:37 + tt],
                                           ALU.subtract, ALU.mult)
                    if tt == 0:
                        st.done(last)
                last.then_inc(s["done_"], 1)
                v.wait_ge(s["done_"], h + 1)
            st.wait()
            for tt in range(TT):
                st.done(v.tensor_tensor(out[:, tt, :], out[:, tt, :], gate[:, tt, :], ALU.mult))

        @block.scalar
        def _(act):
            for h in range(RH):
                act.wait_ge(s["eps_in"], h + 1)
                act.activation(k.stat[:, 34:36], k.stat[:, 32:34], ACT.Sqrt).then_inc(s["rooted"], 1)

        @block.tensor
        def _(pe):
            pe.wait_ge(s["scaled"], 1)

            def score(h):
                if h >= 2:
                    pe.wait_ge(s["decayed"], h - 1)
                for c in range(2):
                    pe.matmul(k.ps[:, 4 + h % 2, 0:T], qk[:, 8 + 2 * h + c, 0:P], qk[:, 2 * h + c, :],
                              start=c == 0, stop=c == 1)
                for c in range(2):
                    last = pe.matmul(k.ps[:, 4 + h % 2, T:T + P], qk[:, 8 + 2 * h + c, P:T], qk[:, 2 * h + c, P:T],
                                     start=c == 0, stop=c == 1)
                last.then_inc(s["scored"], 1)
            score(0)
            for h in range(RH):
                if h + 1 < RH:
                    score(h + 1)
                pe.wait_ge(s["decayed"], h + 1)
                if h >= 2:
                    pe.wait_ge(s["done_"], h - 1)
                cols = slice(512 * h, 512 * h + 512)
                b = 2 * (h % 2)
                pe.matmul(k.ps[:, b, :], prob[:, h % 2, 0:P], val[:, 0, cols], start=True, stop=True)
                pe.matmul(k.ps[:, b + 1, :], prob[:, h % 2, P:T], val[:, 0, cols], start=True, stop=False)
                pe.matmul(k.ps[:, b + 1, :], prob[:, h % 2, T:T + P], val[:, 1, cols], start=False,
                          stop=True).then_inc(s["summed"], 1)
    rows_to_columns(k, out, outT, 16)
    project_rows(k, 16, lambda kc, tt: outT[:, kc, tt * P:(tt + 1) * P])
    residual_ln(k, mod_row(k, 2), "ln_g00", "ln_b00")



def peer(k, layer, sc, sh):
    big = k.big
    qT = big[:, 0:4096].rearrange("p (c t) -> p c t", c=16)
    keys = big[:, 4096:6144].rearrange("p (c n) -> p c n", c=16)
    sc_ = big[:, 6144:10240].rearrange("p (t c n) -> p t c n", t=TT, c=16)
    comb = big[:, 10240:14336].rearrange("p (t h n) -> p t h n", t=TT, h=PH)
    eq = big[:, 14336:18432].rearrange("p (t h a b) -> p t h a b", t=TT, h=PH, a=PTOP)
    sv = big[:, 18432:18944].rearrange("p (t c n) -> p t c n", t=TT, c=16)
    si = big[:, 18944:19456].bitcast(U32).rearrange("p (t c n) -> p t c n", t=TT, c=16)
    sif = big[:, 19456:19968].rearrange("p (t c n) -> p t c n", t=TT, c=16)
    cv = big[:, 19968:20224].rearrange("p (t h n) -> p t h n", t=TT, h=PH)
    ci = big[:, 20224:20480].bitcast(U32).rearrange("p (t h n) -> p t h n", t=TT, h=PH)
    ca = big[:, 20480:20736].bitcast(U32).rearrange("p (t h n) -> p t h n", t=TT, h=PH)
    caf = big[:, 20736:20992].rearrange("p (t h n) -> p t h n", t=TT, h=PH)
    pick = big[:, 20992:21760].rearrange("p (w t m) -> p w t m", w=3, t=TT)
    sm = big[:, 21760:21792]
    W = big.rearrange("p (i t) -> p i t", i=PK)
    one1 = k.tmp[:, 0, :].rearrange("p (g q i) -> p g q i", g=2, q=4)
    one2 = k.tmp[:, 1, :].rearrange("p (g q i) -> p g q i", g=2, q=4)

    to_columns(k, mod=(sc, sh))
    project_columns(k, 16, lambda act, f, ps: act.activation(qT[:, f, :], ps, ACT.Copy))

    with stage(k, "keys_in scored stored dve maxed exped picked turned") as (s, block):
        @block.sync
        def _(sp):
            sp.dma_start(keys, k.dram["peer_keys"][layer]).then_inc(s["keys_in"], 16)
            k.w.stream(sp)

        @block.tensor
        def _(pe):
            pe.wait_ge(s["keys_in"], 16)
            for tt in range(TT):
                for g in range(4):
                    for c in range(4 * g, 4 * g + 4):
                        last = pe.matmul(k.ps[:, 4 * tt + g, (c % 4) * P:(c % 4 + 1) * P], qT[:, c, tt * P:(tt + 1) * P],
                                         keys[:, c, :], start=True, stop=True)
                    last.then_inc(s["scored"], 1)
            pe.wait_ge(s["picked"], 1)
            for w in range(3):
                for tt in range(TT):
                    last = pe.transpose(k.ps[:, w, tt * P:(tt + 1) * P], pick[:, w, tt, :], k.ident[:, :])
            last.then_inc(s["turned"], 1)

        @block.scalar
        def _(act):
            for n in range(8):
                act.wait_ge(s["scored"], n + 1)
                act.activation(sc_[:, n // 4, 4 * (n % 4):4 * (n % 4) + 4, :].rearrange("p c n -> p (c n)"),
                               k.ps[:, n, :], ACT.Copy).then_inc(s["stored"], 1)
            act.wait_ge(s["maxed"], 1)
            act.activation(cv, cv, ACT.Exp).then_inc(s["exped"], 1)

        @block.vector
        def _(v):
            st = Steps(v, s["dve"])

            def best16(rows):
                for r, vo, io in rows:
                    st.done(v.max(vo[:, 0:8], r))
                st.wait()
                for r, vo, io in rows:
                    st.done(v.max_index(io[:, 0:8], vo[:, 0:8], r))
                st.wait()
                for r, vo, io in rows:
                    st.done(v.match_replace(r, vo[:, 0:8], r, -3.0e38))
                st.wait()
                for r, vo, io in rows:
                    st.done(v.max(vo[:, 8:16], r))
                st.wait()
                for r, vo, io in rows:
                    st.done(v.max_index(io[:, 8:16], vo[:, 8:16], r))
                st.wait()

            for tt in range(TT):
                v.wait_ge(s["stored"], 4 * tt + 4)
                best16([(sc_[:, tt, c, :], sv[:, tt, c, :], si[:, tt, c, :]) for c in range(16)])
            st.done(v.tensor_copy(sif, si))
            for tt in range(TT):
                s0 = sv[:, tt].rearrange("p (h c) n -> p c h n", c=2)
                st.done(v.tensor_tensor(comb[:, tt].rearrange("p h (a b) -> p h a b", a=PTOP),
                                        bc(s0[:, 0].unsqueeze(3), [P, PH, PTOP, PTOP]),
                                        bc(s0[:, 1].unsqueeze(2), [P, PH, PTOP, PTOP]), ALU.add))
            st.wait()
            for tt in range(TT):
                best16([(comb[:, tt, h, :], cv[:, tt, h, :], ci[:, tt, h, :]) for h in range(PH)])
            st.link(v.tensor_copy(sm[:, 0:16].rearrange("p (t h) -> p t h", t=TT), cv[:, :, :, 0]))
            cvf = cv.rearrange("p t h n -> p (t h) n")
            v.tensor_tensor(cvf, cvf, bc(sm[:, 0:16].unsqueeze(2), [P, TT * PH, PTOP]), ALU.subtract).then_inc(s["maxed"], 1)
            for side, (op, n) in enumerate(((ALU.logical_shift_right, 4), (ALU.bitwise_and, 15))):
                st.link(v.tensor_scalar(ca, ci, n, None, op))
                st.link(v.tensor_copy(caf, ca))
                for tt in range(TT):
                    st.done(v.tensor_tensor(eq[:, tt], bc(caf[:, tt].unsqueeze(3), [P, PH, PTOP, PTOP]),
                                            bc(k.iota[:, 0:PTOP].unsqueeze(1).unsqueeze(1), [P, PH, PTOP, PTOP]), ALU.is_equal))
                st.wait()
                for tt in range(TT):
                    rows = sif[:, tt].rearrange("p (h c) n -> p c h n", c=2)[:, side]
                    st.done(v.tensor_tensor(eq[:, tt], eq[:, tt], bc(rows.unsqueeze(2), [P, PH, PTOP, PTOP]), ALU.mult))
                st.wait()
                for tt in range(TT):
                    st.done(v.tensor_reduce(pick[:, side, tt, :].rearrange("p (h a) -> p h a", h=PH), eq[:, tt], AX.X, ALU.add))
                st.wait()
            v.wait_ge(s["exped"], 1)
            st.link(v.tensor_reduce(sm[:, 16:32], cvf, AX.X, ALU.add))
            st.link(v.reciprocal(sm[:, 16:32], sm[:, 16:32]))
            v.tensor_tensor(pick[:, 2].rearrange("p t (h n) -> p (t h) n", h=PH), cvf,
                            bc(sm[:, 16:32].unsqueeze(2), [P, TT * PH, PTOP]), ALU.mult).then_inc(s["picked"], 1)
            v.wait_ge(s["turned"], 1)
            v.tensor_copy(k.pickT[:, :, :], k.ps[:, 0:3, 0:T])

    groups = T // 4
    with stage(k, "first second scattered dve_stored act_stored") as (s, block):
        @block.sync
        def _(sp):
            k.w.stream(sp)

        @block.vector
        def _(v):
            def group(g, j, i):
                b = j % 2
                if not known(g) or g >= 2:
                    v.wait_ge(s["scattered"], g - 1)
                for q in range(4):
                    t = g * 4 + q
                    at = k.pickT[:, 0, t:t + 1] if known(t) else k.pickT[:, 0, bass.ds(t, 1)]
                    last = v.tensor_scalar(one1[:, b, q, :], k.iota[:, :], at, None, ALU.is_equal)
                last.then_inc(s["first"], 1)
                for q in range(4):
                    t = g * 4 + q
                    at, w = ((k.pickT[:, r, t:t + 1] if known(t) else k.pickT[:, r, bass.ds(t, 1)]) for r in (1, 2))
                    last = v.tensor_scalar(one2[:, b, q, :], k.iota[:, :], at, w, ALU.is_equal, ALU.mult)
                last.then_inc(s["second"], 1)
            rounds(v, groups, 4, group)

        @block.tensor
        def _(pe):
            def group(g, j, i):
                b = j % 2
                pe.wait_ge(s["second"], g + 1)
                if not known(g) or g >= 4:
                    pe.wait_ge(s["act_stored"], g - 3)
                for q in range(4):
                    last = pe.matmul(k.ps[:, j, q * P:(q + 1) * P], one2[:, b, q, :], one1[:, b, q, :],
                                     start=True, stop=True)
                last.then_inc(s["scattered"], 1)
            rounds(pe, groups, 4, group)

        @block.scalar
        def _(act):
            def group(g, j, i):
                act.wait_ge(s["scattered"], g + 1)
                dst = W[:, :, 4 * g:4 * g + 4] if known(g) else W[:, :, bass.ds(g * 4, 4)]
                act.activation(dst, k.ps[:, j, :].rearrange("p (q i) -> p i q", q=4), ACT.Copy).then_inc(s["act_stored"], 1)
            rounds(act, groups, 4, group)

    def weight(f, b):
        return W[:, f, :] if known(f) else big[:, bass.ds(f * T, T)]
    gated_mlp(k, PK, 1, ACT.Gelu_apprx_tanh, weight)



def shared_kv(k):
    big = k.big
    kvs = big[:, 0:2048].rearrange("p (c t) -> p c t", c=8)
    blk = big[:, 2048:3968].rearrange("p (c m n) -> p c m n", c=2, m=16)
    hid = big[:, 4096:4336].rearrange("p (c h n) -> p c h n", c=2, h=2)
    hidv = big[:, 4608:5632].rearrange("p (h g r n) -> p h g r n", h=2, g=NG, r=NR)
    w2k = big[:, 5632:5888].rearrange("p (h n) -> p h n", h=2)
    w2v = big[:, 5888:6016].rearrange("p (h n) -> p h n", h=2)
    mod = lambda j: big[:, 26624 + 1024 * j:27648 + 1024 * j]
    modulation(k, mod, ["kvada0", "kvada1"])
    to_columns(k, mod=(mod(1), mod(0)))

    first = k.w.take(16)
    with stage(k, "stored") as (s, block):
        @block.sync
        def _(sp):
            k.w.stream(sp)

        @block.tensor
        def _(pe):
            for f in range(16):
                k.w.wait_landed(pe, first + f)
                if f >= 3:
                    pe.wait_ge(s["stored"], f - 2)
                w = k.w.buf(first + f)
                for kc in range(KC):
                    last = pe.matmul(k.ps[:, 4 + f % 3, 0:T], w[:, kc * P:(kc + 1) * P], k.hT[:, kc, :],
                                     start=kc == 0, stop=kc == KC - 1)
                last.then_inc(k.w.tiles_done, 1)

        @block.scalar
        def _(act):
            for f in range(16):
                k.w.wait_done(act, first + f)
                ps = k.ps[:, 4 + f % 3, :]
                if f < 8:
                    act.activation(kvs[0:64, f, :], ps[0:64, 0:T], ACT.Copy)
                    last = act.activation(kvs[64:128, f, 0:T - 1], ps[64:128, 1:T], ACT.Copy)
                else:
                    last = act.activation(k.kT[:, f - 8, :], ps[:, 0:T], ACT.Copy)
                last.then_inc(s["stored"], 1)

    first = k.w.take(4)
    with stage(k, "blocked") as (s, block):
        @block.sync
        def _(sp):
            k.w.stream(sp)

        @block.tensor
        def _(pe):
            for m in range(4):
                k.w.wait_landed(pe, first + m)
                for kc in (2 * m, 2 * m + 1):
                    for tt in range(TT):
                        last = pe.matmul(k.ps[:, tt, :], k.hT[:, kc, tt * P:(tt + 1) * P],
                                         k.w.buf(first + m)[:, (kc % 2) * 512:(kc % 2 + 1) * 512],
                                         start=kc == 0, stop=kc == KC - 1)
                last.then_inc(k.w.tiles_done, 1)

        @block.scalar
        def _(act):
            k.w.wait_done(act, first + 3)
            for tt in range(TT):
                act.activation(k.val[:, tt, :], k.ps[:, tt, :], ACT.Copy)

        @block.vector
        def _(v):
            for c in range(2):
                for m in range(16):
                    v.tensor_scalar(blk[:, c, m, :].rearrange("p (g n) -> p g n", g=NG),
                                    kvs[:, 4 * c:4 * c + 4, 2 * m:2 * m + CS * (NCMP - 1) + 1:CS],
                                    col(k, "cmp_pe", 16 * c + m), None, ALU.add).then_inc(s["blocked"], 1)

    first = k.w.take(8)
    NB = NG * NCMP
    with stage(k, "w2_in gelued spread zeroed multiplied kept") as (s, block):
        @block.sync
        def _(sp):
            sp.dma_start(w2k, k.dram["cmp_w2k"]).then_inc(s["w2_in"], 16)
            sp.dma_start(w2v, k.dram["cmp_w2v"]).then_inc(s["w2_in"], 16)
            k.w.stream(sp)

        @block.tensor
        def _(pe):
            for c in range(2):
                for q in range(4):
                    n = first + 4 * c + q
                    k.w.wait_landed(pe, n)
                    w = k.w.buf(n).rearrange("p (m h) -> p m h", m=4)
                    for m in range(4):
                        for h in range(2):
                            last = pe.matmul(k.ps[:, 2 * c + h, 0:NB], w[:, m, h * P:(h + 1) * P], blk[:, c, 4 * q + m, :],
                                             start=q == 0 and m == 0, stop=q == 3 and m == 3)
                    last.then_inc(k.w.tiles_done, 1)
            pe.wait_ge(s["gelued"], 4)
            pe.wait_ge(s["w2_in"], 32)
            for h in range(2):
                last = pe.matmul(k.ps[:, 4, 0:NB], w2k[:, h, :], hid[:, 0, h, :], start=h == 0, stop=h == 1)
            last.then_inc(s["multiplied"], 1)
            pe.wait_ge(s["spread"], 1)
            for g in range(NG):
                for h in range(2):
                    last = pe.matmul(k.ps[:, 5, 64 * g:64 * g + 64], hidv[:, h, g].rearrange("p r n -> p (r n)"),
                                     w2v[:, h, :], start=h == 0, stop=h == 1)
            last.then_inc(s["multiplied"], 1)

        @block.scalar
        def _(act):
            for c in range(2):
                k.w.wait_done(act, first + 4 * c + 3)
                for h in range(2):
                    act.activation(hid[:, c, h, :], k.ps[:, 2 * c + h, 0:NB], ACT.Gelu_apprx_tanh,
                                   bias=col(k, "cmp_b1", 2 * c + h)).then_inc(s["gelued"], 1)
            act.wait_ge(s["multiplied"], 1)
            act.activation(k.kcT[:, :], k.ps[:, 4, 0:NB], ACT.Copy)
            act.wait_ge(s["multiplied"], 2)
            act.activation(k.vc[:, :], k.ps[:, 5, 0:NG * HD], ACT.Copy)

        @block.vector
        def _(v):
            v.memset(big[:, 4608:5632], 0.0).then_inc(s["zeroed"], 1)
            v.wait_ge(s["zeroed"], 1)
            v.wait_ge(s["gelued"], 4)
            for h in range(2):
                last = v.tensor_copy(hidv[:, h, :, :, 0:NCMP],
                                     bc(hid[:, 1, h, :].rearrange("p (g n) -> p g n", g=NG).unsqueeze(2),
                                        [P, NG, NR, NCMP]))
                if h == 0:
                    last.then_inc(s["zeroed"], 1)
            v.wait_ge(s["zeroed"], 2)
            last.then_inc(s["spread"], 1)



def nsa(k):
    big = k.big
    view = lambda at, c, n: big[:, at:at + c * n].rearrange("p (c t) -> p c t", c=c)
    qT = view(0, KC, T)
    oT = view(2048, KC, T)
    gates = view(4096, TT, 48)
    mask = big[:, 4352:4608]
    cmask = view(4608, TT, NCMP)
    cs = big[:, 4864:5376].rearrange("p (h n) -> p h n", h=NH)
    csT = view(5376, NG, P)
    cst = big[:, 5888:5888 + 64]
    sm = view(6144, 2, 512)
    pr = view(7168, 2, 512)
    prT = view(8192, 2, 512)
    small = view(9216, 2, 16)
    to_columns(k, mod=(mod_row(k, 1), mod_row(k, 0)))
    project_columns(k, KC, lambda act, f, ps: act.activation(qT[:, f, :], ps, ACT.Copy, scale=float(HD) ** -0.5))
    first = k.w.take(1)
    with stage(k, "loaded") as (s, block):
        @block.sync
        def _(sp):
            sp.dma_start(mask, k.dram["mask"]).then_inc(s["loaded"], 16)
            sp.dma_start(cmask, k.dram["cmask"]).then_inc(s["loaded"], 16)
            sp.wait_ge(s["loaded"], 32)
            k.w.stream(sp)

        @block.tensor
        def _(pe):
            k.w.wait_landed(pe, first)
            for tt in range(TT):
                for kc in range(KC):
                    last = pe.matmul(k.ps[:, tt, 0:48], k.hT[:, kc, tt * P:(tt + 1) * P],
                                     k.w.buf(first)[:, kc * P:kc * P + 48], start=kc == 0, stop=kc == KC - 1)
            last.then_inc(k.w.tiles_done, 1)

        @block.scalar
        def _(act):
            k.w.wait_done(act, first)
            for tt in range(TT):
                act.activation(gates[:, tt, :], k.ps[:, tt, 0:48], ACT.Sigmoid)

    for qt in range(TT):
        nk = P * (qt + 1)
        qs = slice(P * qt, P * qt + P)
        gate = gates[:, qt, :].rearrange("p (h b) -> p b h", b=3)
        msk = mask[:, T - nk:T]
        with stage(k, "scored dve maxed exped picked turned kept") as (s, block):
            @block.sync
            def _(sp):
                k.w.stream(sp)

            @block.tensor
            def _(pe):
                for h in range(NH):
                    r = slice(64 * (h % 2), 64 * (h % 2) + 64)
                    g = h // NR
                    last = pe.matmul(k.ps[:, 4 + 2 * (h % 2), 16 * h:16 * h + NCMP], qT[r, h // 2, qs], k.kcT[r, NCMP * g:NCMP * g + NCMP],
                                     start=True, stop=True)
                last.then_inc(s["scored"], 1)
                pe.wait_ge(s["picked"], 1)
                for g in range(NG):
                    last = pe.transpose(k.ps[:, 5, g * P:(g + 1) * P], cs[:, 4 * g:4 * g + 4, :].rearrange("p h n -> p (h n)"),
                                        k.ident[:, :])
                last.then_inc(s["turned"], 1)

            @block.vector
            def _(v):
                st = Steps(v, s["dve"])
                c = cs[:, :, 0:NCMP]
                st.link(v.memset(cs, 0.0))
                v.wait_ge(s["scored"], 1)
                for odd in range(2):
                    st.done(v.tensor_tensor(c[:, odd::2], k.ps[:, 4 + 2 * odd, 0:T].rearrange("p (h n) -> p h n", n=16)[:, odd::2, 0:NCMP],
                                            bc(cmask[:, qt, :].unsqueeze(1), [P, NH // 2, NCMP]), ALU.add))
                st.wait()
                st.link(v.tensor_reduce(cst[:, 0:16], c, AX.X, ALU.max))
                st.link(v.tensor_scalar(cst[:, 0:16], cst[:, 0:16], -1.0e29, None, ALU.max))
                v.tensor_tensor(c, c, bc(cst[:, 0:16].unsqueeze(2), [P, NH, NCMP]), ALU.subtract).then_inc(s["maxed"], 1)
                v.wait_ge(s["exped"], 1)
                st.link(v.tensor_reduce(cst[:, 16:32], c, AX.X, ALU.add))
                st.link(v.tensor_scalar(cst[:, 16:32], cst[:, 16:32], 1.0e-30, None, ALU.max))
                st.link(v.reciprocal(cst[:, 32:48], cst[:, 16:32]))
                st.link(v.tensor_tensor(cst[:, 48:64], cst[:, 32:48], gate[:, 0], ALU.mult))
                v.tensor_tensor(c, c, bc(cst[:, 48:64].unsqueeze(2), [P, NH, NCMP]), ALU.mult).then_inc(s["picked"], 1)
                v.wait_ge(s["turned"], 1)
                v.tensor_copy(csT, k.ps[:, 5, :].rearrange("p (g q) -> p g q", g=NG))

            @block.scalar
            def _(act):
                act.wait_ge(s["maxed"], 1)
                act.activation(cs[:, :, 0:NCMP], cs[:, :, 0:NCMP], ACT.Exp).then_inc(s["exped"], 1)

        with stage(k, "scored dve minned exped weighed turned back summed stored") as (s, block):
            @block.sync
            def _(sp):
                k.w.stream(sp)

            two = lambda ap: ap[:, 0:2 * nk].rearrange("p (b n) -> p b n", b=2)

            @block.tensor
            def _(pe):
                def score(h):
                    r, g = slice(64 * (h % 2), 64 * (h % 2) + 64), h // NR
                    if h >= 2:
                        pe.wait_ge(s["minned"], h - 1)
                    for b in range(2):
                        last = pe.matmul(k.ps[:, 4 + h % 2, b * nk:(b + 1) * nk], qT[r, h // 2, qs], k.kT[r, 4 * b + g, 0:nk],
                                         start=True, stop=True)
                    last.then_inc(s["scored"], 1)

                def turn(h):
                    pe.wait_ge(s["weighed"], h + 1)
                    if h >= 2:
                        pe.wait_ge(s["back"], h - 1)
                    for n in range(2 * nk // P):
                        last = pe.transpose(k.ps[:, 6 + h % 2, n * P:(n + 1) * P], pr[:, h % 2, n * P:(n + 1) * P], k.ident[:, :])
                    last.then_inc(s["turned"], 1)

                def values(h):
                    r, g, j = slice(64 * (h % 2), 64 * (h % 2) + 64), h // NR, h % NR
                    pe.wait_ge(s["back"], h + 1)
                    if h >= 4 and h % 2 == 0:
                        pe.wait_ge(s["stored"], h // 2 - 1)
                    out = k.ps[r, (h // 2) % 2, 0:P]
                    pe.matmul(out, k.vc[32 * j:32 * j + 32, HD * g:HD * g + HD], csT[32 * j:32 * j + 32, g, :],
                              start=True, stop=False)
                    for b in range(2):
                        for kt in range(qt + 1):
                            last = pe.matmul(out, k.val[:, kt, 256 * b + HD * g:256 * b + HD * g + HD],
                                             prT[:, h % 2, b * nk + kt * P:b * nk + kt * P + P], start=False,
                                             stop=b == 1 and kt == qt)
                    last.then_inc(s["summed"], 1)

                for h in range(NH + 2):
                    if h < NH:
                        score(h)
                    if 1 <= h <= NH:
                        turn(h - 1)
                    if h >= 2:
                        values(h - 2)

            @block.vector
            def _(v):
                st = Steps(v, s["dve"])

                def head_max(h):
                    v.wait_ge(s["scored"], h + 1)
                    if h >= 2:
                        v.wait_ge(s["exped"], 2 * (h - 1))
                    st.link(v.tensor_tensor(two(sm[:, h % 2]), two(k.ps[:, 4 + h % 2]), bc(msk.unsqueeze(1), [P, 2, nk]), ALU.add))
                    st.link(v.tensor_reduce(small[:, h % 2, 0:2], two(sm[:, h % 2]), AX.X, ALU.max))
                    v.tensor_scalar(small[:, h % 2, 2:4], small[:, h % 2, 0:2], -1.0, None, ALU.mult).then_inc(s["minned"], 1)

                def head_weigh(h):
                    v.wait_ge(s["exped"], 2 * (h + 1))
                    st.link(v.reciprocal(small[:, h % 2, 6:8], small[:, h % 2, 4:6]))
                    st.link(v.tensor_tensor(small[:, h % 2, 8:10], small[:, h % 2, 6:8], gate[:, 1:3, h], ALU.mult))
                    if h >= 2:
                        v.wait_ge(s["turned"], h - 1)
                    v.tensor_tensor(two(pr[:, h % 2]), two(pr[:, h % 2]),
                                    bc(small[:, h % 2, 8:10].unsqueeze(2), [P, 2, nk]), ALU.mult).then_inc(s["weighed"], 1)

                def head_back(h):
                    v.wait_ge(s["turned"], h + 1)
                    if h >= 2:
                        v.wait_ge(s["summed"], h - 1)
                    v.tensor_copy(prT[:, h % 2, 0:2 * nk], k.ps[:, 6 + h % 2, 0:2 * nk]).then_inc(s["back"], 1)

                for h in range(NH + 2):
                    if h < NH:
                        head_max(h)
                    if 1 <= h <= NH:
                        head_weigh(h - 1)
                    if h >= 2:
                        head_back(h - 2)

            @block.scalar
            def _(act):
                for h in range(NH + 3):
                    if h < NH:
                        act.wait_ge(s["minned"], h + 1)
                        if h >= 2:
                            act.wait_ge(s["turned"], h - 1)
                        for b in range(2):
                            act.activation(pr[:, h % 2, b * nk:(b + 1) * nk], sm[:, h % 2, b * nk:(b + 1) * nk], ACT.Exp,
                                           bias=small[:, h % 2, 2 + b:3 + b],
                                           accum_out=small[:, h % 2, 4 + b:5 + b]).then_inc(s["exped"], 1)
                    if h >= 3 and h % 2 == 0:
                        act.wait_ge(s["summed"], h - 2)
                        act.activation(oT[:, h // 2 - 2, qs], k.ps[:, (h // 2) % 2, 0:P], ACT.Copy).then_inc(s["stored"], 1)
    project_rows(k, KC, lambda kc, tt: oT[:, kc, tt * P:(tt + 1) * P])
    residual_ln(k, mod_row(k, 2), "ln_g10", "ln_b10")



def build(nc, dram, out, total):
    with ExitStack() as ctx:
        def sb(name, shape, dt=F32):
            return ctx.enter_context(nc.sbuf_tensor(name, shape, dt))

        k = Kernel()
        k.nc, k.stages, k.dram = nc, 0, dram
        k.ring = sb("ring", [P, RING, TILE])
        k.x = sb("x", [P, TT, D])
        k.hT = sb("hT", [P, KC, T])
        k.tmp = sb("tmp", [P, TT, D])
        k.row = sb("row", [P, 2, D])
        k.big_t = sb("big", [P, PK * T])
        k.big = k.big_t[:, :]
        k.g2 = sb("g2", [P, D])
        k.cols = sb("cols", [P, NCOLS])
        k.ident = sb("ident", [P, P])
        k.iota = sb("iota", [P, P])
        k.acted = sb("acted", [P, 3, T])
        k.gatedT = sb("gatedT", [P, 3, T])
        k.stat = sb("stat", [P, 64])
        k.pickT = k.acted
        k.ps = ctx.enter_context(nc.psum_tensor("ps", [P, 8, 512], F32))
        landed = [nc.alloc_semaphore(f"landed{j}") for j in range(RING)]
        k.w = Ring(k, landed, nc.alloc_semaphore("tiles_done"), total)
        k.kT = k.big[:, 16384:18432].rearrange("p (c t) -> p c t", c=8)
        k.val = k.big[:, 15360:16384].rearrange("p (c n) -> p c n", c=TT)
        k.kcT = k.big[:, 15104:15164]
        k.vc = k.big[:, 14848:15104]

        with stage(k, "in_") as (s, block):
            @block.sync
            def _(sp):
                sp.dma_start(k.x[:, :, :], k.dram["x_in"].rearrange("(a p) n -> p a n", p=P)).then_inc(s["in_"], 16)
                sp.dma_start(k.cols[:, :], k.dram["cols_in"]).then_inc(s["in_"], 16)
                sp.dma_start(k.ident[:, :], k.dram["ident_in"]).then_inc(s["in_"], 16)
                sp.dma_start(k.iota[:, :], k.dram["iota_in"]).then_inc(s["in_"], 16)
                k.w.stream(sp)
                sp.wait_ge(s["in_"], 64)

        def mod_dst(j):
            return k.g2[:, :] if j == 5 else mod_row(k, j)

        steps = [
            lambda: ffn(k, 0, 0), lambda: s5(k), lambda: ffn(k, 0, 1),
            lambda: ffn(k, 1, 0), lambda: conv(k), lambda: ffn(k, 1, 1),
            lambda: (modulation(k, mod_dst, [f"ada0{j}" for j in range(6)]), retention(k)),
            lambda: (peer(k, 0, mod_row(k, 4), mod_row(k, 3)), residual_ln(k, k.g2, "ln_g01", "ln_b01")),
            lambda: (shared_kv(k), modulation(k, mod_dst, [f"ada1{j}" for j in range(6)]), nsa(k)),
            lambda: (peer(k, 1, mod_row(k, 4), mod_row(k, 3)), residual_ln(k, k.g2, "ln_g11", "ln_b11")),
        ]
        for step in steps:
            step()
        with stage(k, "out_done") as (s, block):
            @block.sync
            def _(sp):
                sp.dma_start(out.rearrange("(a p) n -> p a n", p=P), k.x[:, :, :]).then_inc(s["out_done"], 16)
                sp.wait_ge(s["out_done"], 16)



def column_tiles(w):
    n = w.shape[1] // P
    return w.reshape(KC, P, n, P).transpose(2, 1, 0, 3).reshape(n, P, TILE)


def row_tiles(w):
    nk, g = w.shape[0] // P, w.shape[1] // TILE
    return w.reshape(nk, P, g, TILE).transpose(2, 0, 1, 3).reshape(g * nk, P, TILE)


def weave(ups, downs):
    items = len(downs)
    out = [u[0] for u in ups]
    for f in range(1, items):
        out += [u[f] for u in ups] + [downs[f - 1]]
    return out + [downs[-1]]


def lay_out(a):
    tiles = []

    def ffn_tiles(i, j):
        tiles.extend(weave([column_tiles(a["ffn_w1"][i, j]), column_tiles(a["ffn_w3"][i, j])], row_tiles(a["ffn_w2"][i, j])))

    def peer_tiles(layer):
        tiles.extend(column_tiles(a["peer_w_q_2"][layer]))
        u = a["peer_u_2"][layer].reshape(PK, PK, KC, P).transpose(0, 3, 2, 1).reshape(PK, P, TILE)
        tiles.extend(weave([u], a["peer_v_2"][layer].reshape(PK, PK, TILE)))

    ffn_tiles(0, 0)
    tiles.extend(column_tiles(a["s5_w_in"][0]))
    tiles.extend(column_tiles(a["s5_w_glu"][0]))
    tiles.extend(row_tiles(a["s5_w_out"][0]))
    ffn_tiles(0, 1)
    ffn_tiles(1, 0)
    tiles.extend(column_tiles(a["cv_w_in"][0]))
    tiles.extend(row_tiles(a["cv_w_out"][0]))
    ffn_tiles(1, 1)
    tiles.extend(row_tiles(a["ada_w_2"][0]))
    tiles.extend(column_tiles(a["ret_w_in_2"][0][:, :2048]))
    tiles.extend(row_tiles(a["ret_w_in_2"][0][:, 2048:]))
    tiles.extend(row_tiles(a["ret_w_o_2"][0]))
    peer_tiles(0)
    tiles.extend(row_tiles(a["kv_ada_w_2"]))
    kv = a["nsa_w_kv_2"].reshape(D, 3, 2, NG, HD)
    twice = lambda w: np.concatenate([w, w], axis=2).reshape(D, -1)
    tiles.extend(column_tiles(twice(kv[:, 0].reshape(D, 2 * NG, HD))))
    tiles.extend(column_tiles(twice(kv[:, 1:, 0].reshape(D, 2 * NG, HD))))
    v = kv[:, 1:, 1].reshape(4, 2, P, 512)
    tiles.extend(v.transpose(0, 2, 1, 3).reshape(4, P, TILE))
    w1 = a["cmp_w1_2"].reshape(2, 4, 4, P, CHID)
    tiles.extend(w1.transpose(0, 1, 3, 2, 4).reshape(8, P, TILE))
    tiles.extend(row_tiles(a["ada_w_2"][1]))
    w = a["nsa_w_in_2"][0]
    tiles.extend(column_tiles(w[:, :NH * HD]))
    g = np.zeros((D, P), np.float32)
    g[:, :48] = w[:, NH * HD:]
    tiles.extend(column_tiles(g))
    tiles.extend(row_tiles(a["nsa_w_o_2"][0]))
    peer_tiles(1)

    def cols(vec):
        return vec.reshape(-1, P).T
    parts = [cols(a["norm_pre"]), cols(a["s5_d"]), cols(a["s5_b_glu"]), cols(a["cv_b_in"]), cols(a["cv_dw"]),
             cols(a["cv_dw_b"]), cols(a["cv_ln_g"]), cols(a["cv_ln_b"]), cols(a["c_2"]), cols(a["cmp_b1_2"]),
             cols(a["cmp_pe_2"])]
    rows = [a["norm_post"].reshape(6, D), a["cv_b_out"].reshape(1, D), a["ada_b_2"].reshape(12, D),
            a["kv_ada_b_2"].reshape(2, D)]
    rows += [a[n][l, j].reshape(1, D) for l in range(2) for j in range(2) for n in ("ln_g_2", "ln_b_2")]
    rows = np.concatenate(rows)

    def states(v):
        return v.reshape(ST, P).T
    s5_par = np.stack([states(a["s5_a_re"]), states(a["s5_a_im"]), states(np.repeat(a["s5_log_dt"].reshape(-1), STATE))])
    bcs = [a["s5_b_re"][0], a["s5_b_im"][0], a["s5_c_re"][0].transpose(0, 2, 1), a["s5_c_im"][0].transpose(0, 2, 1)]
    s5_bc = np.stack([v.reshape(ST, P, GH).transpose(1, 0, 2) for v in bcs])
    keys = a["peer_keys_2"].reshape(2, 16, PK, P).transpose(0, 3, 1, 2)
    w2 = a["cmp_w2_2"].reshape(2, 2, P, HD)
    w2k = np.concatenate([w2[0], w2[0]], axis=2).transpose(1, 0, 2)
    w2v = w2[1].transpose(1, 0, 2)

    f32 = np.float32
    theta = (1.0 / (f32(10000.0) ** np.linspace(0.0, 1.0, RDK // 2, dtype=f32))).astype(f32)
    ang = (np.arange(T, dtype=f32)[:, None] * theta[None]).T
    rope = np.stack([np.cos(ang), np.sin(ang)], axis=1).astype(f32)
    log_g = np.log1p(-np.exp2(-5.0 - np.arange(RH)))
    kk, qq = np.arange(P)[:, None], np.arange(T)[None]
    d0 = qq - kk
    dec = np.zeros((P, RH, 384))
    for h in range(RH):
        full = np.where(d0 >= 0, np.exp(np.maximum(d0, 0) * log_g[h]), 0.0) * RDK ** -0.5
        dec[:, h, :T] = full
        dec[:, h, T:] = full[:, :P]
    mask = np.zeros((P, T), f32)
    mask[:, P:] = np.where(np.arange(P)[None] <= np.arange(P)[:, None], 0.0, NEG)
    t = np.arange(T)[:, None]
    cm = np.where(np.arange(NCMP)[None] * CS + CL - 1 <= t, 0.0, NEG).astype(f32)
    arrays = {
        "x_in": a["x"].reshape(T, D), "wts": np.stack(tiles), "cols_in": np.concatenate(parts, axis=1),
        "rows": np.broadcast_to(rows[:, None, :], (len(rows), P, D)), "s5_par": s5_par, "s5_bc": s5_bc,
        "peer_keys": keys, "cmp_w2k": w2k, "cmp_w2v": w2v, "rope": rope, "decay": dec.astype(f32), "mask": mask,
        "cmask": cm.reshape(TT, P, NCMP).transpose(1, 0, 2), "ident_in": np.eye(P, dtype=f32),
        "iota_in": np.broadcast_to(np.arange(P, dtype=f32), (P, P)),
    }
    return {n: np.ascontiguousarray(v) for n, v in arrays.items()}


def program(nc, mybir, arrays):
    dram = {n: nc.dram_tensor(n, v.shape, mybir.dt.from_np(v.dtype), kind="ExternalInput").ap() for n, v in arrays.items()}
    out = nc.dram_tensor("out", (T, D), mybir.dt.float32, kind="ExternalOutput").ap()
    build(nc, dram, out, arrays["wts"].shape[0])


def kernel(**inputs):
    import concourse.bacc as bacc
    from concourse import mybir as _mybir
    from concourse.bass_utils import run_bass_kernel_spmd
    arrays = lay_out({n: np.asarray(v) for n, v in inputs.items()})
    nc = bacc.Bacc("TRN2", target_bir_lowering=False, num_devices=1)
    program(nc, _mybir, arrays)
    r = run_bass_kernel_spmd(nc, [arrays], core_ids=[0])
    return np.asarray(r.results[0]["out"]).reshape(1, T, D)
```

```python
from contextlib import ExitStack, contextmanager

import numpy as np
import concourse.bass as bass
from concourse import mybir

ALU = mybir.AluOpType
ACT = mybir.ActivationFunctionType
AX = mybir.AxisListType
F32 = mybir.dt.float32
F32R = mybir.dt.float32r
U32 = mybir.dt.uint32
I32 = mybir.dt.int32

P = 128
D = 1024
KC = D // P
T = 256
TT = T // P
FF = 2816
TILE = 1024
RING = 4
HALVES = 4
HALF = TILE // 2
EPS = 1e-6
LN_EPS = 1e-5
ALPHA = (2.0 * 2) ** 0.25
NEG = -1e30

GROUPS, STATE, GH = 64, 64, 16
ST = GROUPS * STATE // P
TAPS = 31
RH, RDK, RDV = 4, 256, 512
NG, NR, HD = 4, 4, 64
NH = NG * NR
CS, CL, CHID = 16, 32, 256
NCMP = T // CS - 1
PH, PK, PTOP = 8, 128, 16
ON_VECTOR, ON_GPSIMD, ON_SCALAR = (0, 1), (2,), (3,)
HELD = (0, 40)

FFN_TILES = 3 * (FF // P)
PEER_TILES = 2 * PK
COLS = {}
_at = 0
for _name, _n in (("norm_pre", 6 * KC), ("s5_d", KC), ("s5_b_glu", KC), ("cv_b_in", 2 * KC), ("cv_dw", TAPS * KC),
                  ("cv_dw_b", KC), ("cv_ln_g", KC), ("cv_ln_b", KC), ("c", KC), ("cmp_b1", 4), ("cmp_pe", 32)):
    COLS[_name] = _at
    _at += _n
NCOLS = _at
ROWS = {}
for _i, _name in enumerate(["post00", "post01", "post02", "post10", "post11", "post12", "cv_b_out"]
                           + [f"ln_{a}{l}{j}" for l in range(2) for j in range(2) for a in "gb"]):
    ROWS[_name] = _i


class Kernel:
    pass


class Ring:

    def __init__(self, k, total):
        self.k, self.total = k, total
        self.landed = [k.nc.alloc_semaphore(f"landed{j}") for j in range(RING)]
        self.hi_done = k.nc.alloc_semaphore("hi_done")
        self.lo_done = k.nc.alloc_semaphore("lo_done")
        self.used = k.nc.alloc_semaphore("used")
        self.early = k.nc.alloc_semaphore("early")
        self.issued = self.next = self.n_early = 0

    def take(self, n):
        first = self.next
        self.next += n
        return first

    def part(self, n, half, lo):
        return self.k.parts[:, (2 * n + half) % HALVES, lo, :]

    def raw(self, n, half):
        return self.k.ring[:, n % RING, half * HALF:(half + 1) * HALF]

    def wait_split(self, pe, n, half, i=0):
        pe.wait_ge(self.lo_done, 2 * n + half + 1 + 2 * RING * i)

    def wait_used(self, eng, n, more=0):
        eng.wait_ge(self.used, 2 * n + 2 + 2 * more)

    def split_hi(self, act, n, i=0):
        act.wait_ge(self.landed[n % RING], 16 * (n // RING + 1) + 16 * i)
        for half in range(2):
            if not known(i) or n >= 2:
                act.wait_ge(self.used, 2 * n + half - HALVES + 1 + 2 * RING * i)
            act.activation(self.part(n, half, 0), self.raw(n, half), ACT.Copy).then_inc(self.hi_done, 1)

    def split_lo(self, v, n, i=0):
        for half in range(2):
            v.wait_ge(self.hi_done, 2 * n + half + 1 + 2 * RING * i)
            v.tensor_tensor(self.part(n, half, 1), self.raw(n, half), self.part(n, half, 0).bitcast(F32),
                            ALU.subtract).then_inc(self.lo_done, 1)

    def stream(self, sp, early=()):
        for dst, src in early:
            sp.dma_start(dst, src).then_inc(self.early, 16)
            self.n_early += 16
        end = min(self.total, self.next + RING)
        n = self.issued

        def load(n, i=0):
            if not known(i) or n >= RING:
                sp.wait_ge(self.lo_done, 2 * (n - RING) + 2 + 2 * RING * i)
            sp.dma_start(self.k.ring[:, n % RING, :], self.k.dram["wts"][n + i * RING]).then_inc(self.landed[n % RING], 16)

        while n < end and n < RING:
            load(n)
            n += 1
        turns = (end - n) // RING
        if turns > 1:
            with sp.Fori(0, turns) as i:
                for j in range(RING):
                    load(n + j, i)
            n += turns * RING
        while n < end:
            load(n)
            n += 1
        self.issued = end
        if early:
            sp.wait_ge(self.early, self.n_early)


@contextmanager
def stage(k, names):
    nc = k.nc
    k.stages += 1
    sems = {n: nc.alloc_semaphore(f"{n}_{k.stages}") for n in names.split()}
    with nc.Block(no_gpsimd_drain=True) as block:
        yield sems, block
    nc.clear_and_free_semaphores(list(sems.values()))
    nc.all_engine_barrier()


class Steps:

    def __init__(self, eng, sem):
        self.eng, self.sem, self.n = eng, sem, 0

    def done(self, ins):
        ins.then_inc(self.sem, 1)
        self.n += 1

    def wait(self):
        self.eng.wait_ge(self.sem, self.n)

    def link(self, ins):
        self.done(ins)
        self.wait()


def known(v):
    return isinstance(v, int)


def rounds(eng, n, unroll, body):
    full = n // unroll
    for j in range(min(unroll, n)):
        body(j, j, 0)
    if full > 2:
        with eng.Fori(1, full) as i:
            for j in range(unroll):
                body(i * unroll + j, j, i)
        first = full * unroll
    else:
        first = unroll
    for f in range(first, n):
        body(f, f % unroll, f // unroll)


def col(k, name, i):
    at = COLS[name]
    return k.cols[:, at + i:at + i + 1] if known(i) else k.cols[:, bass.ds(i + at, 1)]


def bc(ap, shape):
    return ap.broadcast_to(shape)



def to_columns(k, rms=None, mod=None):
    with stage(k, "squared rooted normed turned dve hi") as (s, block):
        @block.sync
        def _(sp):
            k.w.stream(sp)

        @block.scalar
        def _(act):
            if rms is not None:
                for tt in range(TT):
                    act.activation(k.tmp[:, tt, :], k.x[:, tt, :], ACT.Square, scale=1.0 / 32,
                                   accum_out=k.stat[:, tt:tt + 1]).then_inc(s["squared"], 1)
                act.wait_ge(s["dve"], 1)
                act.activation(k.stat[:, 4:6], k.stat[:, 2:4], ACT.Sqrt).then_inc(s["rooted"], 1)
            for kp in range(4):
                act.wait_ge(s["turned"], kp + 1)
                for kc in (2 * kp, 2 * kp + 1):
                    at = (kc % 2) * T
                    scale = col(k, "norm_pre", rms * KC + kc) if rms is not None else 1.0
                    act.activation(k.hT[:, 0, kc, :], k.ps[:, 4 + kp, at:at + T], ACT.Copy, scale=scale).then_inc(s["hi"], 1)

        @block.vector
        def _(v):
            st = Steps(v, s["dve"])
            if rms is not None:
                v.wait_ge(s["squared"], TT)
                st.done(v.tensor_scalar(k.stat[:, 2:4], k.stat[:, 0:2], EPS, None, ALU.add))
                v.wait_ge(s["rooted"], 1)
                st.link(v.reciprocal(k.stat[:, 6:8], k.stat[:, 4:6]))
                for tt in range(TT):
                    v.tensor_scalar(k.tmp[:, tt, :], k.x[:, tt, :], k.stat[:, 6 + tt:7 + tt], None,
                                    ALU.mult).then_inc(s["normed"], 1)
            else:
                sc, sh = mod
                for tt in range(TT):
                    st.link(v.scalar_tensor_tensor(k.tmp[:, tt, :], sc, 1.0, k.x[:, tt, :], ALU.add, ALU.mult))
                    v.tensor_tensor(k.tmp[:, tt, :], k.tmp[:, tt, :], sh, ALU.add).then_inc(s["normed"], 1)
            for kc in range(KC):
                v.wait_ge(s["hi"], kc // 2 * 2 + 2)
                at = (kc % 2) * T
                scale = col(k, "norm_pre", rms * KC + kc) if rms is not None else 1.0
                v.scalar_tensor_tensor(k.hT[:, 1, kc, :], k.ps[:, 4 + kc // 2, at:at + T], scale,
                                       k.hT[:, 0, kc, :].bitcast(F32), ALU.mult, ALU.subtract)

        @block.tensor
        def _(pe):
            pe.wait_ge(s["normed"], TT)
            for kp in range(4):
                for kc in (2 * kp, 2 * kp + 1):
                    for tt in range(TT):
                        at = (kc % 2) * T + tt * P
                        last = pe.transpose(k.ps[:, 4 + kp, at:at + P], k.tmp[:, tt, kc * P:(kc + 1) * P], k.ident[:, :])
                last.then_inc(s["turned"], 1)


def rows_to_columns(k, src):
    with stage(k, "turned hi") as (s, block):
        @block.sync
        def _(sp):
            k.w.stream(sp)

        @block.tensor
        def _(pe):
            for c2 in range(KC // 2):
                for c in (2 * c2, 2 * c2 + 1):
                    for tt in range(TT):
                        at = (c % 2) * T + tt * P
                        last = pe.transpose(k.ps[:, 4 + c2, at:at + P], src[:, tt, c * P:(c + 1) * P], k.ident[:, :])
                last.then_inc(s["turned"], 1)

        two = lambda ap: ap.rearrange("p (c t) -> p c t", c=2)

        @block.scalar
        def _(act):
            for c2 in range(KC // 2):
                act.wait_ge(s["turned"], c2 + 1)
                act.activation(k.hT[:, 0, 2 * c2:2 * c2 + 2, :], two(k.ps[:, 4 + c2, :]), ACT.Copy).then_inc(s["hi"], 1)

        @block.vector
        def _(v):
            for c2 in range(KC // 2):
                v.wait_ge(s["hi"], c2 + 1)
                v.tensor_tensor(k.hT[:, 1, 2 * c2:2 * c2 + 2, :], two(k.ps[:, 4 + c2, :]),
                                k.hT[:, 0, 2 * c2:2 * c2 + 2, :].bitcast(F32), ALU.subtract)


def split_columns(k, src, n=KC):
    with stage(k, "hi") as (s, block):
        dst = [part(k, p, n, src.shape[2]) for p in range(2)]

        @block.sync
        def _(sp):
            k.w.stream(sp)

        @block.scalar
        def _(act):
            for h in range(2):
                c = slice(h * n // 2, (h + 1) * n // 2)
                act.activation(dst[0][:, c], src[:, c], ACT.Copy).then_inc(s["hi"], 1)

        @block.vector
        def _(v):
            for h in range(2):
                c = slice(h * n // 2, (h + 1) * n // 2)
                v.wait_ge(s["hi"], h + 1)
                v.tensor_tensor(dst[1][:, c], src[:, c], dst[0][:, c].bitcast(F32), ALU.subtract)


def part(k, lo, n, m):
    return k.hT[:, lo, :, :].rearrange("p c t -> p (c t)")[:, 0:n * m].rearrange("p (c t) -> p c t", c=n)


def products(pe, out, a, b, start, stop):
    for x, y in ((0, 0), (0, 1), (1, 0)):
        last = pe.matmul(out, a(x), b(y), start=start and x + y == 0, stop=stop and x == 1)
    return last


def residual_rms(k, row, coef, bias_row=None):
    with stage(k, "g_in b_in squared rooted dve biased") as (s, block):
        @block.sync
        def _(sp):
            sp.dma_start(k.row[:, 0, :], k.dram["rows"][ROWS[row]]).then_inc(s["g_in"], 16)
            if bias_row:
                sp.dma_start(k.row[:, 1, :], k.dram["rows"][ROWS[bias_row]]).then_inc(s["b_in"], 16)
            k.w.stream(sp)

        def y(b):
            if bias_row:
                return k.tmp[:, b // 2, (b % 2) * 512:(b % 2 + 1) * 512]
            return k.ps[:, b, :]

        @block.scalar
        def _(act):
            for b in range(4):
                if bias_row:
                    act.wait_ge(s["biased"], b + 1)
                act.activation(k.ps[:, 4 + b, :], y(b), ACT.Square, scale=1.0 / 32,
                               accum_out=k.stat[:, b:b + 1]).then_inc(s["squared"], 1)
            act.wait_ge(s["dve"], 2)
            act.activation(k.stat[:, 8:10], k.stat[:, 6:8], ACT.Sqrt).then_inc(s["rooted"], 1)

        @block.vector
        def _(v):
            if bias_row:
                v.wait_ge(s["b_in"], 16)
                for b in range(4):
                    v.tensor_tensor(y(b), k.ps[:, b, :], k.row[:, 1, (b % 2) * 512:(b % 2 + 1) * 512],
                                    ALU.add).then_inc(s["biased"], 1)
            st = Steps(v, s["dve"])
            v.wait_ge(s["squared"], 4)
            ss = k.stat[:, 0:4].rearrange("p (t h) -> p t h", h=2)
            st.link(v.tensor_tensor(k.stat[:, 4:6], ss[:, :, 0], ss[:, :, 1], ALU.add))
            st.done(v.tensor_scalar(k.stat[:, 6:8], k.stat[:, 4:6], EPS, None, ALU.add))
            v.wait_ge(s["rooted"], 1)
            st.link(v.reciprocal(k.stat[:, 10:12], k.stat[:, 8:10]))
            st.link(v.tensor_scalar(k.stat[:, 12:14], k.stat[:, 10:12], float(coef), None, ALU.mult))
            v.wait_ge(s["g_in"], 16)
            if bias_row:
                v.wait_ge(s["biased"], 4)
            for b in range(4):
                tt, half = b // 2, slice((b % 2) * 512, (b % 2 + 1) * 512)
                st.link(v.scalar_tensor_tensor(k.tmp[:, tt, half], y(b), k.stat[:, 12 + tt:13 + tt],
                                               k.row[:, 0, half], ALU.mult, ALU.mult))
                st.done(v.tensor_tensor(k.x[:, tt, half], k.x[:, tt, half], k.tmp[:, tt, half], ALU.add))


def residual_ln(k, gate, ln_g, ln_b, early=()):
    with stage(k, "g_in b_in rooted eps_in dve") as (s, block):
        @block.sync
        def _(sp):
            sp.dma_start(k.row[:, 0, :], k.dram["rows"][ROWS[ln_g]]).then_inc(s["g_in"], 16)
            sp.dma_start(k.row[:, 1, :], k.dram["rows"][ROWS[ln_b]]).then_inc(s["b_in"], 16)
            k.w.stream(sp, early)

        @block.scalar
        def _(act):
            act.wait_ge(s["eps_in"], 1)
            act.activation(k.stat[:, 34:36], k.stat[:, 32:34], ACT.Sqrt).then_inc(s["rooted"], 1)

        @block.vector
        def _(v):
            st = Steps(v, s["dve"])
            for b in range(4):
                tt, half = b // 2, slice((b % 2) * 512, (b % 2 + 1) * 512)
                st.done(v.tensor_tensor(k.tmp[:, tt, half], k.ps[:, b, :], gate[:, half], ALU.mult))
            st.wait()
            for tt in range(TT):
                st.done(v.scalar_tensor_tensor(k.x[:, tt, :], k.x[:, tt, :], ALPHA, k.tmp[:, tt, :], ALU.mult, ALU.add))
            st.wait()
            for b in range(4):
                st.done(v.bn_stats(k.stat[:, 6 * b:6 * b + 6], k.x[:, b // 2, (b % 2) * 512:(b % 2 + 1) * 512]))
            st.wait()
            for tt in range(TT):
                st.done(v.bn_aggr(k.stat[:, 24 + 2 * tt:26 + 2 * tt], k.stat[:, 12 * tt:12 * tt + 12]))
            st.wait()
            mv = k.stat[:, 24:28].rearrange("p (t c) -> p t c", c=2)
            v.tensor_scalar(k.stat[:, 32:34], mv[:, :, 1], LN_EPS, None, ALU.add).then_inc(s["eps_in"], 1)
            v.wait_ge(s["rooted"], 1)
            st.link(v.reciprocal(k.stat[:, 36:38], k.stat[:, 34:36]))
            for tt in range(TT):
                st.done(v.tensor_scalar(k.x[:, tt, :], k.x[:, tt, :], k.stat[:, 24 + 2 * tt:25 + 2 * tt],
                                        k.stat[:, 36 + tt:37 + tt], ALU.subtract, ALU.mult))
            st.wait()
            v.wait_ge(s["g_in"], 16)
            v.wait_ge(s["b_in"], 16)
            for tt in range(TT):
                st.done(v.tensor_tensor(k.x[:, tt, :], k.x[:, tt, :], k.row[:, 0, :], ALU.mult))
            st.wait()
            for tt in range(TT):
                st.done(v.tensor_tensor(k.x[:, tt, :], k.x[:, tt, :], k.row[:, 1, :], ALU.add))



def splitting(k, block, first, n, after=None, act_first=None):
    @block.scalar
    def _(act):
        if act_first:
            act_first(act)
        for f in range(n):
            if after and f >= 2:
                after(act, f - 2)
            k.w.split_hi(act, first + f)
        if after:
            for f in range(max(n - 2, 0), n):
                after(act, f)

    @block.vector
    def _(v):
        def tile(f, j, i):
            k.w.split_lo(v, first + j, i)
        rounds(v, n, RING, tile)


def column_product(k, pe, n, out, i=0):
    for half in range(2):
        k.w.wait_split(pe, n, half, i)
        for q in range(KC // 2):
            kc = half * (KC // 2) + q
            last = products(pe, out, lambda lo: k.w.part(n, half, lo)[:, q * P:(q + 1) * P],
                            lambda lo: k.hT[:, lo, kc, :], start=kc == 0, stop=kc == KC - 1)
        last.then_inc(k.w.used, 1)


def row_product(k, pe, n, out, lhsT, start, stop, i=0):
    for half in range(2):
        k.w.wait_split(pe, n, half, i)
        for tt in range(TT):
            last = products(pe, out(tt, half), lambda lo: lhsT(lo, tt), lambda lo: k.w.part(n, half, lo), start, stop)
        last.then_inc(k.w.used, 1)


def project_columns(k, n, evacuate, early=()):
    first = k.w.take(n)
    with stage(k, "stored") as (s, block):
        @block.sync
        def _(sp):
            k.w.stream(sp, early)

        @block.tensor
        def _(pe):
            def tile(f, j, i):
                if not known(f) or f >= 4:
                    pe.wait_ge(s["stored"], f - 3)
                column_product(k, pe, first + j, k.ps[:, 4 + j % 4, 0:T], i)
            rounds(pe, n, RING, tile)

        def after(act, f):
            k.w.wait_used(act, first + f)
            evacuate(act, f, k.ps[:, 4 + f % 4, 0:T]).then_inc(s["stored"], 1)
        splitting(k, block, first, n, after)


def project_rows(k, groups=1, evacuate=None, start=True, stop=True):
    n = KC * groups
    first = k.w.take(n)
    with stage(k, "stored") as (s, block):
        @block.sync
        def _(sp):
            k.w.stream(sp)

        @block.tensor
        def _(pe):
            for f in range(n):
                g, kc = f // KC, f % KC
                if g >= 2 and kc == 0:
                    pe.wait_ge(s["stored"], 4 * (g - 1))
                row_product(k, pe, first + f, lambda tt, half: k.ps[:, 4 * (g % 2) + 2 * tt + half, :],
                            lambda lo, tt: k.hT[:, lo, kc, tt * P:(tt + 1) * P],
                            start and kc == 0, stop and kc == KC - 1)

        def after(act, f):
            if f % KC == KC - 1:
                g = f // KC
                k.w.wait_used(act, first + f)
                for tt in range(TT):
                    for half in range(2):
                        evacuate(act, g, tt, half, k.ps[:, 4 * (g % 2) + 2 * tt + half, :]).then_inc(s["stored"], 1)
        splitting(k, block, first, n, after if evacuate else None)


MOD_SEMS = "m_bias m_out m_stored"


class Modulation:

    def __init__(self, k, first_row, ng, scratch, bank, s):
        self.k, self.row, self.ng, self.s = k, first_row, ng, s
        self.first = k.w.take(KC * ng)
        self.n = KC * ng
        self.bias = scratch[0:ng, 0:D]
        self.kept = scratch[P - 32:P - 31, 0:D]
        self.bank = bank

    def load(self, sp):
        sp.dma_start(self.bias, self.k.dram["mod_bias"][self.row:self.row + self.ng, :]).then_inc(self.s["m_bias"], 16)

    def tensor(self, pe):
        k = self.k
        for f in range(self.n):
            g, kc = f // KC, f % KC
            if kc == 0:
                if g == 0:
                    pe.wait_ge(self.s["m_bias"], 16)
                else:
                    pe.wait_ge(self.s["m_out"], 2 * g)
                for half in range(2):
                    pe.matmul(k.ps[:, self.bank + half, :], bc(k.ident[0:self.ng, g:g + 1], [self.ng, P]),
                              self.bias[:, half * HALF:(half + 1) * HALF], start=True, stop=False)
            for half in range(2):
                k.w.wait_split(pe, self.first + f, half)
                last = products(pe, k.ps[:, self.bank + half, :], lambda lo: bc(k.c2[:, lo, kc:kc + 1], [P, P]),
                                lambda lo: k.w.part(self.first + f, half, lo), False, kc == KC - 1)
                last.then_inc(k.w.used, 1)

    def keep(self, act, g):
        k = self.k
        k.w.wait_used(act, self.first + (g + 1) * KC - 1)
        if g >= 1:
            act.wait_ge(self.s["m_stored"], 16 * g)
        p = slice(P - 32, P - 31)
        for half in range(2):
            act.activation(self.kept[:, half * HALF:(half + 1) * HALF], k.ps[p, self.bank + half, :],
                           ACT.Copy).then_inc(self.s["m_out"], 1)
        act.wait_ge(self.s["m_out"], 2 * (g + 1))
        act.dma_start(k.mod_rows[self.row + g:self.row + g + 1, :], self.kept).then_inc(self.s["m_stored"], 16)

    def scalar(self, act, begin=0, end=None):
        end = self.n if end is None else end
        for f in range(begin, end):
            if f >= 2 and (f - 2) % KC == KC - 1:
                self.keep(act, (f - 2) // KC)
            self.k.w.split_hi(act, self.first + f)
        if end == self.n:
            self.keep(act, self.ng - 1)
            act.wait_ge(self.s["m_stored"], 16 * self.ng)

    def gpsimd(self, pool):
        def tile(f, j, i):
            self.k.w.split_lo(pool, self.first + j, i)
        rounds(pool, self.n, RING, tile)


HELD_SEMS = "h_stored"


class HeldUps:

    def __init__(self, k, n, func, dst, bank, s):
        self.k, self.n, self.func, self.dst, self.bank, self.s = k, n, func, dst, bank, s
        self.first = k.w.take(n)

    def tensor(self, pe):
        def item(f, j, i):
            if not known(f) or f >= 2:
                pe.wait_ge(self.s["h_stored"], f - 1)
            column_product(self.k, pe, self.first + j, self.k.ps[:, self.bank + j % 2, 0:T], i)
        rounds(pe, self.n, RING, item)

    def store(self, act, f):
        self.k.w.wait_used(act, self.first + f)
        act.activation(self.dst[:, f, :], self.k.ps[:, self.bank + f % 2, 0:T], self.func).then_inc(self.s["h_stored"], 1)

    def scalar(self, act, begin, end):
        for f in range(begin, end):
            self.k.w.split_hi(act, self.first + f)
            if f >= 1:
                self.store(act, f - 1)
        if end == self.n:
            self.store(act, self.n - 1)

    def gpsimd(self, pool):
        def item(f, j, i):
            self.k.w.split_lo(pool, self.first + j, i)
        rounds(pool, self.n, RING, item)


def held_downs(k, items, src):
    first = k.w.take(items)
    with stage(k, "gated_hi gated") as (s, block):
        @block.sync
        def _(sp):
            k.w.stream(sp)

        @block.tensor
        def _(pe):
            def item(f, j, i):
                pe.wait_ge(s["gated"], f + 1)
                row_product(k, pe, first + j, lambda tt, half: k.ps[:, 2 * tt + half, :],
                            lambda lo, tt: k.gatedT[:, j % 2, lo, tt * P:(tt + 1) * P], known(f) and f == 0, False, i)
            rounds(pe, items, RING, item)

        @block.scalar
        def _(act):
            def item(f, j, i):
                k.w.split_hi(act, first + j, i)
            rounds(act, items, RING, item)

        @block.vector
        def _(v):
            def item(f, j, i):
                k.w.split_lo(v, first + j, i)
            rounds(v, items, RING, item)

        @block.gpsimd
        def _(pool):
            def item(f, j):
                if f >= 2:
                    k.w.wait_used(pool, first + f - 2)
                a = src(f)
                pool.tensor_tensor(k.gatedT[:, j % 2, 0, :], a, bc(k.iota[:, 0:1], [P, T]), ALU.subtract).then_inc(s["gated_hi"], 1)
                pool.wait_ge(s["gated_hi"], f + 1)
                pool.tensor_tensor(k.gatedT[:, j % 2, 1, :], a, k.gatedT[:, j % 2, 0, :].bitcast(F32),
                                   ALU.subtract).then_inc(s["gated"], 1)
            for f in range(items):
                item(f, f % 2)


def mod_loads(k, dst, first, n):
    return [(dst(j), bc(k.mod_rows[first + j:first + j + 1, :], [P, D])) for j in range(n)]



def gated_mlp(k, items, ups, func, factor, early=(), start=True):
    per = ups + 1
    n_tiles = per * items
    first = k.w.take(n_tiles)
    steady = first + 2 * ups
    BODY = 4
    with stage(k, "activated multiplied gated_hi gated") as (s, block):
        @block.sync
        def _(sp):
            k.w.stream(sp, early)

        def turns(i):
            return i * (BODY * per // RING)

        @block.tensor
        def _(pe):
            def up(f, bank, n, i):
                if not known(f) or f >= 4:
                    pe.wait_ge(s["multiplied"], f - 3)
                for u in range(ups):
                    column_product(k, pe, n + u, k.ps[:, 4 + bank, u * T:(u + 1) * T], turns(i))

            def down(f, buf, n, i, start=False, stop=False):
                pe.wait_ge(s["gated"], f + 1)
                row_product(k, pe, n, lambda tt, half: k.ps[:, 2 * tt + half, :],
                            lambda lo, tt: k.gatedT[:, buf, lo, tt * P:(tt + 1) * P], start, stop, turns(i))

            def both(g, j, i):
                n = steady + j * per
                up(g + 2, (j + 2) % 4, n, i)
                down(g, j % 2, n + ups, i, start=start and known(g) and g == 0)

            up(0, 0, first, 0)
            up(1, 1, first + ups, 0)
            rounds(pe, items - 2, BODY, both)
            for f in (items - 2, items - 1):
                down(f, f % 2, first + n_tiles - items + f, 0, stop=f == items - 1)

        def splits(eng, split, post):
            for n in range(2 * ups):
                split(eng, first + n, 0)
            post(0, 0)

            def one(g, j, i):
                post(g + 1, j + 1)
                for u in range(per):
                    split(eng, steady + j * per + u, turns(i))
            rounds(eng, items - 2, BODY, one)
            post(items - 1, items - 1)
            for n in range(2):
                split(eng, first + n_tiles - 2 + n, 0)

        @block.scalar
        def _(act):
            def item(f, j):
                if known(f) and f == 0:
                    k.w.wait_used(act, first + ups - 1)
                elif known(f) and f == 1:
                    k.w.wait_used(act, first + 2 * ups - 1)
                else:
                    k.w.wait_used(act, steady + ups - 1 - 2 * per, f * per)
                if not known(f) or f >= 2:
                    act.wait_ge(s["gated"], f - 1)
                act.activation(k.acted[:, j % 2, :], k.ps[:, 4 + j % 4, 0:T], func).then_inc(s["activated"], 1)
            splits(act, k.w.split_hi, item)

        @block.vector
        def _(v):
            def item(f, j):
                v.wait_ge(s["activated"], f + 1)
                v.tensor_tensor(k.acted[:, j % 2, :], k.acted[:, j % 2, :], factor(f, j % 4), ALU.mult).then_inc(s["multiplied"], 1)
            splits(v, k.w.split_lo, item)

        @block.gpsimd
        def _(pool):
            def item(f, j, i):
                pool.wait_ge(s["multiplied"], f + 1)
                if not known(f) or f >= 2:
                    k.w.wait_used(pool, steady + per - 1 - 2 * per, f * per)
                pool.tensor_tensor(k.gatedT[:, j % 2, 0, :], k.acted[:, j % 2, :], bc(k.iota[:, 0:1], [P, T]),
                                   ALU.subtract).then_inc(s["gated_hi"], 1)
                pool.wait_ge(s["gated_hi"], f + 1)
                pool.tensor_tensor(k.gatedT[:, j % 2, 1, :], k.acted[:, j % 2, :], k.gatedT[:, j % 2, 0, :].bitcast(F32),
                                   ALU.subtract).then_inc(s["gated"], 1)
            rounds(pool, items, BODY, item)


def ffn(k, i, j, early=()):
    to_columns(k, rms=3 * i + 2 * j)
    gated_mlp(k, FF // P, 2, ACT.Silu, lambda f, b: k.ps[:, 4 + b, T:2 * T], early)
    residual_rms(k, f"post{i}{2 * j}", 0.5)



def s5(k):
    big = k.big
    uT = big[:, 0:2048].rearrange("p (c t) -> p c t", c=KC)
    yT = big[:, 2048:4096].rearrange("p (c t) -> p c t", c=KC)
    cosT = big[:, 4096:12288].rearrange("p (s t) -> p s t", s=ST)
    sinT = big[:, 12288:20480].rearrange("p (s t) -> p s t", s=ST)
    prod = big[:, 20480:24576].rearrange("p (s t) -> p s t", s=ST)
    b_re = big[:, 24576:25088].rearrange("p (s h) -> p s h", s=ST)
    b_im = big[:, 25088:25600].rearrange("p (s h) -> p s h", s=ST)
    c_re = big[:, 25600:26112].rearrange("p (s h) -> p s h", s=ST)
    c_im = big[:, 26112:26624].rearrange("p (s h) -> p s h", s=ST)
    cy = big[:, 24576:26624].rearrange("p (c t) -> p c t", c=KC)
    par = big[:, 26624:26624 + 40 * ST].rearrange("p (n s) -> p n s", s=ST)
    bx = [big[:, 28672 + 1024 * n:29696 + 1024 * n].rearrange("p (s h) -> p s h", s=ST) for n in range(2)]
    cx = [big[:, 30720 + 1024 * n:31744 + 1024 * n].rearrange("p (s h) -> p s h", s=ST) for n in range(2)]
    bT = [big[:, 20480 + 1024 * n:21504 + 1024 * n].rearrange("p (c m) -> p c m", c=KC) for n in range(2)]
    at, bt, zin = (big[:, 22528 + 512 * n:23040 + 512 * n] for n in range(3))
    z2 = [k.tmp[:, 0, 512 * n:512 * n + 512] for n in range(2)]
    st2 = [k.tmp[:, 1, 512 * n:512 * n + 512] for n in range(2)]
    ga = [k.g2[:, 0:512], k.g2[:, 512:1024]]
    gb = [big[:, 24064:24576], k.acted[:, :, :].rearrange("p b t -> p (b t)")]

    to_columns(k, rms=1)
    project_columns(k, KC, lambda act, f, ps: act.activation(uT[:, f, :], ps, ACT.Copy))

    (A_RE, A_IM, DT, MAG, TH, RED, KQ, SINH, COS, SIN, AB_RE, AB_IM, NR_, DEN, T0, T1, T2, T3, F_RE, F_IM) = range(20)
    POW = 20

    with stage(k, "loaded dt_exp mag_exp red sines zeroed dve " + MOD_SEMS) as (s, block):
        mod = Modulation(k, 0, 4, k.g2[:, :], 6, s)

        @block.sync
        def _(sp):
            for n, (dst, src) in enumerate(((par[:, A_RE, :], k.dram["s5_par"][0]), (par[:, A_IM, :], k.dram["s5_par"][1]),
                                            (par[:, DT, :], k.dram["s5_par"][2]), (b_re, k.dram["s5_bc"][0]), (b_im, k.dram["s5_bc"][1]),
                                            (c_re, k.dram["s5_bc"][2]), (c_im, k.dram["s5_bc"][3]))):
                sp.dma_start(dst, src).then_inc(s["loaded"], 16)
            mod.load(sp)
            k.w.stream(sp)

        @block.tensor
        def _(pe):
            mod.tensor(pe)

        @block.scalar
        def _(act):
            act.wait_ge(s["loaded"], 7 * 16)
            act.activation(par[:, DT, :], par[:, DT, :], ACT.Exp).then_inc(s["dt_exp"], 1)
            act.wait_ge(s["red"], 1)
            act.activation(par[:, MAG, :], par[:, MAG, :], ACT.Exp).then_inc(s["mag_exp"], 1)
            act.wait_ge(s["red"], 2)
            act.activation(par[:, SIN, :], par[:, RED, :], ACT.Sin).then_inc(s["sines"], 1)
            act.activation(par[:, SINH, :], par[:, RED, :], ACT.Sin, scale=0.5).then_inc(s["sines"], 1)
            mod.scalar(act)

        @block.gpsimd
        def _(pool):
            for m in (*bx, *cx):
                pool.memset(m, 0.0).then_inc(s["zeroed"], 1)
            mod.gpsimd(pool)

        @block.vector
        def _(v):
            st = Steps(v, s["dve"])
            q = lambda n: par[:, n, :]
            tt = lambda o, a, b, op: st.link(v.tensor_tensor(q(o), q(a), q(b), op))
            v.wait_ge(s["dt_exp"], 1)
            v.tensor_tensor(q(MAG), q(DT), q(A_RE), ALU.mult).then_inc(s["red"], 1)
            tt(TH, DT, A_IM, ALU.mult)
            st.link(v.tensor_scalar(q(KQ), q(TH), float(np.float32(1 / (2 * np.pi))), 12582912.0, ALU.mult, ALU.add))
            st.link(v.tensor_scalar(q(KQ), q(KQ), -12582912.0, None, ALU.add))
            c1 = 6.28125
            c2 = float(np.float32(np.floor((2 * np.pi - c1) * 2 ** 21) / 2 ** 21))
            c3 = float(np.float32(2 * np.pi - c1 - c2))
            st.link(v.scalar_tensor_tensor(q(RED), q(KQ), -c1, q(TH), ALU.mult, ALU.add))
            st.link(v.scalar_tensor_tensor(q(RED), q(KQ), -c2, q(RED), ALU.mult, ALU.add))
            st.link(v.scalar_tensor_tensor(q(RED), q(KQ), -c3, q(RED), ALU.mult, ALU.add))
            v.tensor_scalar(q(RED), q(RED), 3.1415925, -3.1415925, ALU.min, ALU.max).then_inc(s["red"], 1)
            v.wait_ge(s["sines"], 2)
            v.wait_ge(s["mag_exp"], 1)
            tt(COS, SINH, SINH, ALU.mult)
            st.link(v.tensor_scalar(q(COS), q(COS), -2.0, 1.0, ALU.mult, ALU.add))
            tt(AB_RE, MAG, COS, ALU.mult)
            tt(AB_IM, MAG, SIN, ALU.mult)
            st.link(v.tensor_scalar(q(NR_), q(AB_RE), -1.0, None, ALU.add))
            tt(T0, A_RE, A_RE, ALU.mult)
            tt(T1, A_IM, A_IM, ALU.mult)
            tt(DEN, T0, T1, ALU.add)
            st.link(v.reciprocal(q(DEN), q(DEN)))
            tt(T0, NR_, A_RE, ALU.mult)
            tt(T1, AB_IM, A_IM, ALU.mult)
            tt(T0, T0, T1, ALU.add)
            tt(F_RE, T0, DEN, ALU.mult)
            tt(T2, AB_IM, A_RE, ALU.mult)
            tt(T3, NR_, A_IM, ALU.mult)
            tt(T2, T2, T3, ALU.subtract)
            tt(F_IM, T2, DEN, ALU.mult)
            v.wait_ge(s["zeroed"], 4)
            fr, fi = (bc(q(f).unsqueeze(2), [P, ST, GH]) for f in (F_RE, F_IM))
            pr = k.tmp[:, :, :].rearrange("p a (b n) -> p (a b) n", b=2)
            w = lambda n: pr[:, n, :].rearrange("p (s h) -> p s h", s=ST)
            st.done(v.tensor_tensor(w(0), b_re, fr, ALU.mult))
            st.done(v.tensor_tensor(w(1), b_im, fi, ALU.mult))
            st.done(v.tensor_tensor(w(2), b_im, fr, ALU.mult))
            st.done(v.tensor_tensor(w(3), b_re, fi, ALU.mult))
            st.wait()
            for h in range(2):
                ps, cs = slice(64 * h, 64 * h + 64), slice(GH * h, GH * h + GH)
                st.done(v.tensor_tensor(bx[0][ps, :, cs], w(0)[ps], w(1)[ps], ALU.subtract))
                st.done(v.tensor_tensor(bx[1][ps, :, cs], w(2)[ps], w(3)[ps], ALU.add))
                st.done(v.tensor_copy(cx[0][ps, :, cs], c_re[ps]))
                st.done(v.tensor_scalar(cx[1][ps, :, cs], c_im[ps], -1.0, None, ALU.mult))
            st.done(v.memset(cosT[:, :, 0:1], 1.0))
            st.done(v.memset(sinT[:, :, 0:1], 0.0))
            pc, psn = COS, SIN
            st.wait()
            for n in range(8):
                m = 1 << n
                cb, sb = (bc(q(a).unsqueeze(2), [P, ST, m]) for a in (pc, psn))
                lo, hi = slice(0, m), slice(m, 2 * m)
                pp = prod[:, :, 0:m]
                st.done(v.tensor_tensor(cosT[:, :, hi], cosT[:, :, lo], cb, ALU.mult))
                st.link(v.tensor_tensor(pp, sinT[:, :, lo], sb, ALU.mult))
                st.done(v.tensor_tensor(cosT[:, :, hi], cosT[:, :, hi], pp, ALU.subtract))
                st.done(v.tensor_tensor(sinT[:, :, hi], sinT[:, :, lo], cb, ALU.mult))
                st.wait()
                st.link(v.tensor_tensor(pp, cosT[:, :, lo], sb, ALU.mult))
                st.link(v.tensor_tensor(sinT[:, :, hi], sinT[:, :, hi], pp, ALU.add))
                if n < 7:
                    nc_, ns_ = POW + 2 * n, POW + 2 * n + 1
                    tt(T0, pc, pc, ALU.mult)
                    tt(T1, psn, psn, ALU.mult)
                    tt(nc_, T0, T1, ALU.subtract)
                    tt(T0, pc, psn, ALU.mult)
                    st.link(v.tensor_scalar(q(ns_), q(T0), 2.0, None, ALU.mult))
                    pc, psn = nc_, ns_

    with stage(k, "turned bT_in") as (s, block):
        @block.sync
        def _(sp):
            k.w.stream(sp)

        @block.tensor
        def _(pe):
            for n in range(2):
                for c in range(KC):
                    last = pe.transpose(k.ps[:, 2 * n + c // 4, (c % 4) * P:(c % 4 + 1) * P],
                                        bx[n][:, 4 * c:4 * c + 4, :].rearrange("p s h -> p (s h)"), k.ident[:, :])
                last.then_inc(s["turned"], 1)

        @block.vector
        def _(v):
            for n in range(2):
                v.wait_ge(s["turned"], n + 1)
                v.tensor_copy(bT[n], k.ps[:, 2 * n:2 * n + 2, :].rearrange("p b (c m) -> p (b c) m", m=P))

    with stage(k, "bu_ready bu_read dve zed by_cos by_sin back_re back_im y_ready y_read gel") as (s, block):
        @block.sync
        def _(sp):
            k.w.stream(sp)

        @block.tensor
        def _(pe):
            def bu(t):
                c, j = t // 4, t % 4
                rows = slice(32 * j, 32 * j + 32)
                if t >= 2:
                    pe.wait_ge(s["bu_read"], t - 1)
                for n in range(2):
                    last = pe.matmul(k.ps[:, 4 + t % 2, n * T:(n + 1) * T], bT[n][rows, c, :], uT[rows, c, :],
                                     start=True, stop=True)
                last.then_inc(s["bu_ready"], 1)

            def y(t):
                c, j = t // 4, t % 4
                pe.wait_ge(s["back_re"], t + 1)
                pe.wait_ge(s["back_im"], t + 1)
                if j == 0 and c >= 2:
                    pe.wait_ge(s["y_read"], c - 1)
                for n in range(2):
                    last = pe.matmul(k.ps[32 * j:32 * j + 32, c % 2, 0:T], cx[n][:, t, :],
                                     st2[t % 2][:, n * T:(n + 1) * T], start=n == 0, stop=n == 1)
                last.then_inc(s["y_ready"], 1)

            bu(0)
            for t in range(ST):
                if t + 1 < ST:
                    bu(t + 1)
                if t >= 1:
                    y(t - 1)
            y(ST - 1)

        two = lambda ap: ap.rearrange("p (n t) -> p n t", n=2)

        @block.vector
        def _(v):
            st = Steps(v, s["dve"])

            def sine_product(t):
                v.wait_ge(s["zed"], t + 1)
                if t >= 2:
                    v.wait_ge(s["back_re"], t - 1)
                    v.wait_ge(s["back_im"], t - 1)
                v.tensor_tensor(two(gb[t % 2]), two(z2[t % 2]), bc(sinT[:, t, :].unsqueeze(1), [P, 2, T]),
                                ALU.mult).then_inc(s["by_sin"], 1)

            for t in range(ST):
                v.wait_ge(s["bu_ready"], t + 1)
                cb, sb = (bc(x[:, t, :].unsqueeze(1), [P, 2, T]) for x in (cosT, sinT))
                bu = k.ps[:, 4 + t % 2, :]
                st.done(v.tensor_tensor(two(at), two(bu), cb, ALU.mult))
                v.tensor_tensor(two(bt), two(bu), sb, ALU.mult).then_inc(s["bu_read"], 1)
                if t >= 1:
                    sine_product(t - 1)
                v.wait_ge(s["bu_read"], t + 1)
                st.wait()
                st.done(v.tensor_tensor(zin[:, 0:T], at[:, 0:T], bt[:, T:2 * T], ALU.add))
                st.done(v.tensor_tensor(zin[:, T:2 * T], at[:, T:2 * T], bt[:, 0:T], ALU.subtract))
                st.wait()
                if t >= 2:
                    v.wait_ge(s["by_cos"], t - 1)
                    v.wait_ge(s["by_sin"], t - 1)
                mag = bc(par[:, MAG, t:t + 1], [P, T])
                for n in range(2):
                    last = v.tensor_tensor_scan(z2[t % 2][:, n * T:(n + 1) * T], mag, zin[:, n * T:(n + 1) * T], 0.0,
                                                ALU.mult, ALU.add)
                    if n == 0:
                        st.done(last)
                last.then_inc(s["zed"], 1)
            sine_product(ST - 1)

        @block.gpsimd
        def _(pool):
            for t in range(ST):
                u = t % 2
                pool.wait_ge(s["zed"], t + 1)
                if t >= 2:
                    pool.wait_ge(s["back_re"], t - 1)
                    pool.wait_ge(s["back_im"], t - 1)
                pool.tensor_tensor(two(ga[u]), two(z2[u]), bc(cosT[:, t, :].unsqueeze(1), [P, 2, T]),
                                   ALU.mult).then_inc(s["by_cos"], 1)
                pool.wait_ge(s["by_cos"], t + 1)
                pool.wait_ge(s["by_sin"], t + 1)
                if t >= 2:
                    pool.wait_ge(s["y_ready"], t - 1)
                pool.tensor_tensor(st2[u][:, 0:T], ga[u][:, 0:T], gb[u][:, T:2 * T], ALU.subtract).then_inc(s["back_re"], 1)
                pool.tensor_tensor(st2[u][:, T:2 * T], ga[u][:, T:2 * T], gb[u][:, 0:T], ALU.add).then_inc(s["back_im"], 1)

        @block.scalar
        def _(act):
            for c in range(KC):
                act.wait_ge(s["y_ready"], 4 * c + 4)
                act.activation(yT[:, c, :], uT[:, c, :], ACT.Copy, scale=col(k, "s5_d", c)).then_inc(s["gel"], 1)
                act.wait_ge(s["gel"], c + 1)
                act.activation(cy[:, c, :], k.ps[:, c % 2, 0:T], ACT.Copy).then_inc(s["y_read"], 1)

    with stage(k, "sum") as (s, block):
        @block.vector
        def _(v):
            v.tensor_tensor(yT, yT, cy, ALU.add).then_inc(s["sum"], 1)

        @block.scalar
        def _(act):
            act.wait_ge(s["sum"], 1)
            act.activation(yT, yT, ACT.Gelu_apprx_tanh)
    split_columns(k, yT)

    project_columns(k, KC, lambda act, f, ps: act.activation(uT[:, f, :], ps, ACT.Sigmoid, bias=col(k, "s5_b_glu", f)))
    with stage(k, "gated") as (s, block):
        @block.vector
        def _(v):
            v.tensor_tensor(yT, yT, uT, ALU.mult).then_inc(s["gated"], 1)
    split_columns(k, yT)
    project_rows(k)
    residual_rms(k, "post01", 1.0)



def conv(k):
    big = k.big
    PAD = TAPS - 1
    L = PAD + T
    a = big[:, 0:2048].rearrange("p (c t) -> p c t", c=KC)
    g = big[:, 2048:4096].rearrange("p (c t) -> p c t", c=KC)
    zp = big[:, 4096:4096 + KC * L].rearrange("p (c t) -> p c t", c=KC)
    z = big[:, 8192:10240].rearrange("p (c t) -> p c t", c=KC)
    sq = big[:, 10240:12288].rearrange("p (c t) -> p c t", c=KC)
    mean_w = big[:, 12288:12416]
    sd = big[:, 12416:12672]
    rstd = big[:, 12672:12928]
    to_columns(k, rms=4)
    both = big[:, 0:4096].rearrange("p (c t) -> p c t", c=2 * KC)
    project_columns(k, 2 * KC, lambda act, f, ps: act.activation(
        both[:, f, :], ps, ACT.Identity if f < KC else ACT.Sigmoid, bias=col(k, "cv_b_in", f)))
    with stage(k, "dve tap mean_in centred squared_ var_in rooted normed " + MOD_SEMS) as (s, block):
        mod = Modulation(k, 4, 5, k.g2[:, :], 6, s)

        @block.sync
        def _(sp):
            mod.load(sp)
            k.w.stream(sp)

        @block.gpsimd
        def _(pool):
            mod.gpsimd(pool)

        @block.vector
        def _(v):
            st = Steps(v, s["dve"])
            st.done(v.memset(mean_w, 1.0 / D))
            st.done(v.memset(zp[:, :, 0:PAD], 0.0))
            st.done(v.tensor_tensor(zp[:, :, PAD:L], a, g, ALU.mult))
            st.wait()
            for f in range(KC):
                v.tensor_scalar(z[:, f, :], zp[:, f, 0:T], col(k, "cv_dw", f), col(k, "cv_dw_b", f), ALU.mult,
                                ALU.add).then_inc(s["tap"], 1)
            with v.Fori(1, TAPS) as i:
                for f in range(KC):
                    v.wait_ge(s["tap"], i * KC + f - KC + 1)
                    v.scalar_tensor_tensor(z[:, f, :], zp[:, f, bass.ds(i, T)], col(k, "cv_dw", i * KC + f),
                                           z[:, f, :], ALU.mult, ALU.add).then_inc(s["tap"], 1)
            v.wait_ge(s["mean_in"], 1)
            mean = bc(k.ps[:, 4, 0:T].unsqueeze(1), [P, KC, T])
            v.tensor_tensor(z, z, mean, ALU.subtract).then_inc(s["centred"], 1)
            v.wait_ge(s["centred"], 1)
            v.tensor_tensor(sq, z, z, ALU.mult).then_inc(s["squared_"], 1)
            v.wait_ge(s["var_in"], 1)
            st.done(v.tensor_scalar(sd, k.ps[:, 5, 0:T], EPS, None, ALU.add))
            v.wait_ge(s["rooted"], 1)
            st.link(v.reciprocal(rstd, sd))
            v.tensor_tensor(z, z, bc(rstd.unsqueeze(1), [P, KC, T]), ALU.mult).then_inc(s["normed"], 1)

        @block.tensor
        def _(pe):
            mod.tensor(pe)
            pe.wait_ge(s["tap"], TAPS * KC)
            for f in range(KC):
                last = pe.matmul(k.ps[:, 4, 0:T], mean_w, z[:, f, :], start=f == 0, stop=f == KC - 1)
            last.then_inc(s["mean_in"], 1)
            pe.wait_ge(s["squared_"], 1)
            for f in range(KC):
                last = pe.matmul(k.ps[:, 5, 0:T], mean_w, sq[:, f, :], start=f == 0, stop=f == KC - 1)
            last.then_inc(s["var_in"], 1)

        @block.scalar
        def _(act):
            mod.scalar(act)
            act.wait_ge(s["dve"], 4)
            act.activation(sd, sd, ACT.Sqrt).then_inc(s["rooted"], 1)
            act.wait_ge(s["normed"], 1)
            for f in range(KC):
                act.activation(sq[:, f, :], z[:, f, :], ACT.Silu, scale=col(k, "cv_ln_g", f), bias=col(k, "cv_ln_b", f))
    split_columns(k, sq)
    project_rows(k)
    residual_rms(k, "post11", 1.0, bias_row="cv_b_out")



def mod_row(k, j):
    return k.big[:, 26624 + 1024 * j:27648 + 1024 * j]


def retention(k):
    big = k.big
    view = lambda at, c, n: big[:, at:at + c * n].rearrange("p (c t) -> p c t", c=c)
    raw = view(0, 16, T)
    qk = view(4096, 16, T)
    val = view(8192, TT, 2048)
    gate = view(12288, TT, 2048)
    out = view(16384, TT, 2048)
    dec = view(20480, RH, 384)
    rope = view(22016, 2, T)
    half = view(22528, 8, T)
    prob = view(24576, 2, 384)
    to_columns(k, mod=(mod_row(k, 1), mod_row(k, 0)))
    project_columns(k, 16, lambda act, f, ps: act.activation(raw[:, f, :], ps, ACT.Copy))

    def store(act, g, tt, h, ps):
        cols = slice((g % 2) * 1024 + h * 512, (g % 2) * 1024 + h * 512 + 512)
        if g < 2:
            return act.activation(val[:, tt, cols], ps, ACT.Copy)
        return act.activation(gate[:, tt, cols], ps, ACT.Silu)
    project_rows(k, 4, store)

    with stage(k, "loaded dve scored decayed summed st mv eps_in rooted done_ scaled") as (s, block):
        @block.sync
        def _(sp):
            sp.dma_start(dec, k.dram["decay"]).then_inc(s["loaded"], 16)
            sp.dma_start(rope, k.dram["rope"]).then_inc(s["loaded"], 16)
            k.w.stream(sp)

        @block.vector
        def _(v):
            st = Steps(v, s["dve"])
            v.wait_ge(s["loaded"], 32)
            x1 = raw.rearrange("p (h c) t -> p c h t", c=2)[:, 0]
            x2 = raw.rearrange("p (h c) t -> p c h t", c=2)[:, 1]
            y1 = qk.rearrange("p (h c) t -> p c h t", c=2)[:, 0]
            y2 = qk.rearrange("p (h c) t -> p c h t", c=2)[:, 1]
            cb, sb = (bc(rope[:, n, :].unsqueeze(1), [P, 8, T]) for n in range(2))
            st.done(v.tensor_tensor(y1, x1, cb, ALU.mult))
            st.link(v.tensor_tensor(half, x2, sb, ALU.mult))
            st.done(v.tensor_tensor(y1, y1, half, ALU.subtract))
            st.done(v.tensor_tensor(y2, x2, cb, ALU.mult))
            st.wait()
            st.link(v.tensor_tensor(half, x1, sb, ALU.mult))
            v.tensor_tensor(y2, y2, half, ALU.add).then_inc(s["scaled"], 1)
            for h in range(RH):
                v.wait_ge(s["scored"], h + 1)
                if h >= 2:
                    v.wait_ge(s["summed"], h - 1)
                v.tensor_tensor(prob[:, h % 2, :], k.ps[:, 4 + h % 2, 0:384], dec[:, h, :], ALU.mult).then_inc(s["decayed"], 1)
                v.wait_ge(s["summed"], h + 1)
                for tt in range(TT):
                    st.done(v.bn_stats(k.stat[:, 6 * tt:6 * tt + 6], k.ps[:, 2 * (h % 2) + tt, :]))
                st.wait()
                for tt in range(TT):
                    st.done(v.bn_aggr(k.stat[:, 24 + 2 * tt:26 + 2 * tt], k.stat[:, 6 * tt:6 * tt + 6]))
                st.wait()
                mv = k.stat[:, 24:28].rearrange("p (t c) -> p t c", c=2)
                v.tensor_scalar(k.stat[:, 32:34], mv[:, :, 1], LN_EPS, None, ALU.add).then_inc(s["eps_in"], 1)
                v.wait_ge(s["rooted"], h + 1)
                st.link(v.reciprocal(k.stat[:, 36:38], k.stat[:, 34:36]))
                for tt in range(TT):
                    last = v.tensor_scalar(out[:, tt, 512 * h:512 * h + 512], k.ps[:, 2 * (h % 2) + tt, :],
                                           k.stat[:, 24 + 2 * tt:25 + 2 * tt], k.stat[:, 36 + tt:37 + tt],
                                           ALU.subtract, ALU.mult)
                    if tt == 0:
                        st.done(last)
                last.then_inc(s["done_"], 1)
                v.wait_ge(s["done_"], h + 1)
            st.wait()
            for tt in range(TT):
                st.done(v.tensor_tensor(out[:, tt, :], out[:, tt, :], gate[:, tt, :], ALU.mult))

        @block.scalar
        def _(act):
            for h in range(RH):
                act.wait_ge(s["eps_in"], h + 1)
                act.activation(k.stat[:, 34:36], k.stat[:, 32:34], ACT.Sqrt).then_inc(s["rooted"], 1)

        @block.tensor
        def _(pe):
            pe.wait_ge(s["scaled"], 1)

            def score(h):
                if h >= 2:
                    pe.wait_ge(s["decayed"], h - 1)
                for c in range(2):
                    pe.matmul(k.ps[:, 4 + h % 2, 0:T], qk[:, 8 + 2 * h + c, 0:P], qk[:, 2 * h + c, :],
                              start=c == 0, stop=c == 1)
                for c in range(2):
                    last = pe.matmul(k.ps[:, 4 + h % 2, T:T + P], qk[:, 8 + 2 * h + c, P:T], qk[:, 2 * h + c, P:T],
                                     start=c == 0, stop=c == 1)
                last.then_inc(s["scored"], 1)
            score(0)
            for h in range(RH):
                if h + 1 < RH:
                    score(h + 1)
                pe.wait_ge(s["decayed"], h + 1)
                if h >= 2:
                    pe.wait_ge(s["done_"], h - 1)
                cols = slice(512 * h, 512 * h + 512)
                b = 2 * (h % 2)
                pe.matmul(k.ps[:, b, :], prob[:, h % 2, 0:P], val[:, 0, cols], start=True, stop=True)
                pe.matmul(k.ps[:, b + 1, :], prob[:, h % 2, P:T], val[:, 0, cols], start=True, stop=False)
                pe.matmul(k.ps[:, b + 1, :], prob[:, h % 2, T:T + P], val[:, 1, cols], start=False,
                          stop=True).then_inc(s["summed"], 1)
    for h in range(2):
        rows_to_columns(k, out[:, :, h * D:(h + 1) * D])
        project_rows(k, start=h == 0, stop=h == 1)
    residual_ln(k, mod_row(k, 2), "ln_g00", "ln_b00")



def peer(k, layer, sc, sh):
    big = k.big
    qT = big[:, 0:4096].rearrange("p (c t) -> p c t", c=16)
    keys = big[:, 4096:6144].rearrange("p (c n) -> p c n", c=16)
    sc_ = big[:, 6144:10240].rearrange("p (t c n) -> p t c n", t=TT, c=16)
    comb = big[:, 10240:14336].rearrange("p (t h n) -> p t h n", t=TT, h=PH)
    eq = big[:, 14336:18432].rearrange("p (t h a b) -> p t h a b", t=TT, h=PH, a=PTOP)
    sv = big[:, 18432:18944].rearrange("p (t c n) -> p t c n", t=TT, c=16)
    si = big[:, 18944:19456].bitcast(U32).rearrange("p (t c n) -> p t c n", t=TT, c=16)
    sif = big[:, 19456:19968].rearrange("p (t c n) -> p t c n", t=TT, c=16)
    cv = big[:, 19968:20224].rearrange("p (t h n) -> p t h n", t=TT, h=PH)
    ci = big[:, 20224:20480].bitcast(U32).rearrange("p (t h n) -> p t h n", t=TT, h=PH)
    ca = big[:, 20480:20736].bitcast(U32).rearrange("p (t h n) -> p t h n", t=TT, h=PH)
    caf = big[:, 20736:20992].rearrange("p (t h n) -> p t h n", t=TT, h=PH)
    pick = big[:, 20992:21760].rearrange("p (w t m) -> p w t m", w=3, t=TT)
    sm = big[:, 21760:21792]
    W = big.rearrange("p (i t) -> p i t", i=PK)
    one1 = k.tmp[:, 0, :].rearrange("p (g q i) -> p g q i", g=2, q=4)
    one2 = k.tmp[:, 1, :].rearrange("p (g q i) -> p g q i", g=2, q=4)

    held, func = HELD[layer], ACT.Gelu_apprx_tanh
    to_columns(k, mod=(sc, sh))
    project_columns(k, 16, lambda act, f, ps: act.activation(qT[:, f, :], ps, ACT.Copy))

    with stage(k, "keys_in scored stored dve maxed exped picked turned "
               + (HELD_SEMS if held else MOD_SEMS)) as (s, block):
        beside = HeldUps(k, held, func, W[:, PK - held:, :], 6, s) if held else Modulation(k, 9, 5, k.tmp[:, 0, :], 6, s)

        @block.sync
        def _(sp):
            sp.dma_start(keys, k.dram["peer_keys"][layer]).then_inc(s["keys_in"], 16)
            if not held:
                beside.load(sp)
            k.w.stream(sp)

        @block.gpsimd
        def _(pool):
            beside.gpsimd(pool)

        @block.tensor
        def _(pe):
            pe.wait_ge(s["keys_in"], 16)
            for tt in range(TT):
                for g in range(4):
                    if tt:
                        pe.wait_ge(s["stored"], g + 1)
                    for c in range(4 * g, 4 * g + 4):
                        last = pe.matmul(k.ps[:, g, (c % 4) * P:(c % 4 + 1) * P], qT[:, c, tt * P:(tt + 1) * P],
                                         keys[:, c, :], start=True, stop=True)
                    last.then_inc(s["scored"], 1)
            beside.tensor(pe)
            pe.wait_ge(s["picked"], 1)
            for w in range(3):
                for tt in range(TT):
                    last = pe.transpose(k.ps[:, w, tt * P:(tt + 1) * P], pick[:, w, tt, :], k.ident[:, :])
            last.then_inc(s["turned"], 1)

        @block.scalar
        def _(act):
            for n in range(8):
                act.wait_ge(s["scored"], n + 1)
                act.activation(sc_[:, n // 4, 4 * (n % 4):4 * (n % 4) + 4, :].rearrange("p c n -> p (c n)"),
                               k.ps[:, n % 4, :], ACT.Copy).then_inc(s["stored"], 1)
            beside.scalar(act, 0, 4 * KC)
            act.wait_ge(s["maxed"], 1)
            act.activation(cv, cv, ACT.Exp).then_inc(s["exped"], 1)
            beside.scalar(act, 4 * KC, beside.n)

        @block.vector
        def _(v):
            st = Steps(v, s["dve"])

            def best16(rows):
                for r, vo, io in rows:
                    st.done(v.max(vo[:, 0:8], r))
                st.wait()
                for r, vo, io in rows:
                    st.done(v.max_index(io[:, 0:8], vo[:, 0:8], r))
                st.wait()
                for r, vo, io in rows:
                    st.done(v.match_replace(r, vo[:, 0:8], r, -3.0e38))
                st.wait()
                for r, vo, io in rows:
                    st.done(v.max(vo[:, 8:16], r))
                st.wait()
                for r, vo, io in rows:
                    st.done(v.max_index(io[:, 8:16], vo[:, 8:16], r))
                st.wait()

            for tt in range(TT):
                v.wait_ge(s["stored"], 4 * tt + 4)
                best16([(sc_[:, tt, c, :], sv[:, tt, c, :], si[:, tt, c, :]) for c in range(16)])
            st.done(v.tensor_copy(sif, si))
            for tt in range(TT):
                s0 = sv[:, tt].rearrange("p (h c) n -> p c h n", c=2)
                st.done(v.tensor_tensor(comb[:, tt].rearrange("p h (a b) -> p h a b", a=PTOP),
                                        bc(s0[:, 0].unsqueeze(3), [P, PH, PTOP, PTOP]),
                                        bc(s0[:, 1].unsqueeze(2), [P, PH, PTOP, PTOP]), ALU.add))
            st.wait()
            for tt in range(TT):
                best16([(comb[:, tt, h, :], cv[:, tt, h, :], ci[:, tt, h, :]) for h in range(PH)])
            st.link(v.tensor_copy(sm[:, 0:16].rearrange("p (t h) -> p t h", t=TT), cv[:, :, :, 0]))
            cvf = cv.rearrange("p t h n -> p (t h) n")
            v.tensor_tensor(cvf, cvf, bc(sm[:, 0:16].unsqueeze(2), [P, TT * PH, PTOP]), ALU.subtract).then_inc(s["maxed"], 1)
            for side, (op, n) in enumerate(((ALU.logical_shift_right, 4), (ALU.bitwise_and, 15))):
                st.link(v.tensor_scalar(ca, ci, n, None, op))
                st.link(v.tensor_copy(caf, ca))
                for tt in range(TT):
                    st.done(v.tensor_tensor(eq[:, tt], bc(caf[:, tt].unsqueeze(3), [P, PH, PTOP, PTOP]),
                                            bc(k.iota[:, 0:PTOP].unsqueeze(1).unsqueeze(1), [P, PH, PTOP, PTOP]), ALU.is_equal))
                st.wait()
                for tt in range(TT):
                    rows = sif[:, tt].rearrange("p (h c) n -> p c h n", c=2)[:, side]
                    st.done(v.tensor_tensor(eq[:, tt], eq[:, tt], bc(rows.unsqueeze(2), [P, PH, PTOP, PTOP]), ALU.mult))
                st.wait()
                for tt in range(TT):
                    st.done(v.tensor_reduce(pick[:, side, tt, :].rearrange("p (h a) -> p h a", h=PH), eq[:, tt], AX.X, ALU.add))
                st.wait()
            v.wait_ge(s["exped"], 1)
            st.link(v.tensor_reduce(sm[:, 16:32], cvf, AX.X, ALU.add))
            st.link(v.reciprocal(sm[:, 16:32], sm[:, 16:32]))
            v.tensor_tensor(pick[:, 2].rearrange("p t (h n) -> p (t h) n", h=PH), cvf,
                            bc(sm[:, 16:32].unsqueeze(2), [P, TT * PH, PTOP]), ALU.mult).then_inc(s["picked"], 1)
            v.wait_ge(s["turned"], 1)
            v.tensor_copy(k.pickT[:, :, :], k.ps[:, 0:3, 0:T])
            v.tensor_scalar(k.acted[:, :, :], k.ps[:, 1:3, 0:T], -1.0, None, ALU.mult)

    groups = T // 4
    def pick_at(row, t):
        return k.pickT[:, row, t:t + 1] if known(t) else k.pickT[:, row, bass.ds(t, 1)]

    def negated_at(row, t):
        return k.acted[:, row, t:t + 1] if known(t) else k.acted[:, row, bass.ds(t, 1)]

    def tokens(g, rows):
        return W[:, rows, 4 * g:4 * g + 4] if known(g) else W[:, rows, bass.ds(g * 4, 4)]

    with stage(k, "first second_v second_p second_a far scattered act_stored weighted") as (s, block):
        @block.sync
        def _(sp):
            k.w.stream(sp)

        def second(eng, g, b, qs):
            for q in qs:
                t = g * 4 + q
                last = eng.tensor_scalar(one2[:, b, q, :], k.iota[:, :], pick_at(1, t), pick_at(2, t), ALU.is_equal, ALU.mult)
            return last

        @block.vector
        def _(v):
            def group(g, j, i):
                b = j % 2
                if not known(g) or g >= 2:
                    v.wait_ge(s["scattered"], g - 1)
                t4 = k.pickT[:, 0, 4 * g:4 * g + 4] if known(g) else k.pickT[:, 0, bass.ds(g * 4, 4)]
                v.tensor_tensor(one1[:, b], bc(k.iota[:, :].unsqueeze(1), [P, 4, P]), bc(t4.unsqueeze(2), [P, 4, P]),
                                ALU.is_equal).then_inc(s["first"], 1)
                second(v, g, b, ON_VECTOR).then_inc(s["second_v"], 1)
                if held and (not known(g) or g >= 2):
                    weigh(g - 2, (j - 2) % 4)

            def weigh(g, j):
                v.wait_ge(s["act_stored"], g + 1)
                dst = tokens(g, slice(PK - held, PK))
                v.tensor_tensor(dst, dst, k.ps[:, j, :].rearrange("p (q i) -> p i q", q=4)[:, PK - held:, :],
                                ALU.mult).then_inc(s["weighted"], 1)
            rounds(v, groups, 4, group)
            if held:
                for g in (groups - 2, groups - 1):
                    weigh(g, g % 4)

        @block.gpsimd
        def _(pool):
            def group(g, j, i):
                b = j % 2
                if not known(g) or g >= 2:
                    pool.wait_ge(s["scattered"], g - 1)
                second(pool, g, b, ON_GPSIMD).then_inc(s["second_p"], 1)
            for g in range(groups):
                group(g, g % 4, 0)

        @block.tensor
        def _(pe):
            def group(g, j, i):
                b = j % 2
                pe.wait_ge(s["second_v"], g + 1)
                pe.wait_ge(s["second_p"], g + 1)
                pe.wait_ge(s["second_a"], g + 1)
                if not known(g) or g >= 4:
                    pe.wait_ge(s["weighted" if held else "act_stored"], g - 3)
                for q in range(4):
                    last = pe.matmul(k.ps[:, j, q * P:(q + 1) * P], one2[:, b, q, :], one1[:, b, q, :],
                                     start=True, stop=True)
                last.then_inc(s["scattered"], 1)
            rounds(pe, groups, 4, group)

        @block.scalar
        def _(act):
            def group(g, j, i):
                b = j % 2
                if not known(g) or g >= 2:
                    act.wait_ge(s["scattered"], g - 1)
                for q in ON_SCALAR:
                    act.activation(one2[:, b, q, :], k.iota[:, :], ACT.Abs, bias=negated_at(0, g * 4 + q)).then_inc(s["far"], 1)
                if not known(g) or g >= 2:
                    store(g - 2, (j - 2) % 4)
                act.wait_ge(s["far"], (g + 1) * len(ON_SCALAR))
                for q in ON_SCALAR:
                    t = g * 4 + q
                    last = act.activation(one2[:, b, q, :], one2[:, b, q, :], ACT.Relu, bias=pick_at(2, t), scale=negated_at(1, t))
                last.then_inc(s["second_a"], 1)

            def store(g, j):
                act.wait_ge(s["scattered"], g + 1)
                act.activation(tokens(g, slice(0, PK - held)), k.ps[:, j, :].rearrange("p (q i) -> p i q", q=4)[:, 0:PK - held, :],
                               ACT.Copy).then_inc(s["act_stored"], 1)
            rounds(act, groups, 4, group)
            for g in (groups - 2, groups - 1):
                store(g, g % 4)

    def weight(f, b):
        return W[:, f, :] if known(f) else big[:, bass.ds(f * T, T)]
    if held:
        held_downs(k, held, lambda f: weight(f + PK - held, 0))
    gated_mlp(k, PK - held, 1, func, weight, start=not held)



def shared_kv(k, early):
    big = k.big
    kvs = big[:, 0:2048].rearrange("p (c t) -> p c t", c=8)
    blk = big[:, 2048:3968].rearrange("p (c m n) -> p c m n", c=2, m=16)
    hid = big[:, 4096:4336].rearrange("p (c h n) -> p c h n", c=2, h=2)
    hidv = big[:, 4608:5632].rearrange("p (h g r n) -> p h g r n", h=2, g=NG, r=NR)
    w2k = big[:, 5632:5888].rearrange("p (h n) -> p h n", h=2)
    w2v = big[:, 5888:6016].rearrange("p (h n) -> p h n", h=2)
    mod = lambda j: big[:, 26624 + 1024 * j:27648 + 1024 * j]
    to_columns(k, mod=(mod(1), mod(0)))

    def keep(act, f, ps):
        if f < 8:
            act.activation(kvs[0:64, f, :], ps[0:64, 0:T], ACT.Copy)
            return act.activation(kvs[64:128, f, 0:T - 1], ps[64:128, 1:T], ACT.Copy)
        return act.activation(k.kT[:, f - 8, :], ps, ACT.Copy)
    project_columns(k, 16, keep, early)

    first = k.w.take(4)
    with stage(k, "blocked") as (s, block):
        @block.sync
        def _(sp):
            k.w.stream(sp)

        @block.tensor
        def _(pe):
            for kc in range(KC):
                n, half = first + kc // 2, kc % 2
                k.w.wait_split(pe, n, half)
                for tt in range(TT):
                    last = products(pe, k.ps[:, tt, :], lambda lo: k.hT[:, lo, kc, tt * P:(tt + 1) * P],
                                    lambda lo: k.w.part(n, half, lo), kc == 0, kc == KC - 1)
                last.then_inc(k.w.used, 1)

        def after(act, f):
            if f == 3:
                k.w.wait_used(act, first + 3)
                for tt in range(TT):
                    act.activation(k.val[:, tt, :], k.ps[:, tt, :], ACT.Copy)
        splitting(k, block, first, 4, after)

    with stage(k, "blocked") as (s, block):
        @block.vector
        def _(v):
            for c in range(2):
                for m in range(16):
                    v.tensor_scalar(blk[:, c, m, :].rearrange("p (g n) -> p g n", g=NG),
                                    kvs[:, 4 * c:4 * c + 4, 2 * m:2 * m + CS * (NCMP - 1) + 1:CS],
                                    col(k, "cmp_pe", 16 * c + m), None, ALU.add).then_inc(s["blocked"], 1)
    split_columns(k, blk.rearrange("p c m n -> p (c m) n"), 32)

    first = k.w.take(8)
    NB = NG * NCMP
    with stage(k, "w2_in gelued spread zeroed multiplied kept") as (s, block):
        @block.sync
        def _(sp):
            sp.dma_start(w2k, k.dram["cmp_w2k"]).then_inc(s["w2_in"], 16)
            sp.dma_start(w2v, k.dram["cmp_w2v"]).then_inc(s["w2_in"], 16)
            k.w.stream(sp)

        @block.tensor
        def _(pe):
            for c in range(2):
                for q in range(4):
                    for half in range(2):
                        n = first + 4 * c + q
                        k.w.wait_split(pe, n, half)
                        for m in range(2):
                            mm = 4 * q + 2 * half + m
                            for h in range(2):
                                at = m * CHID + h * P
                                last = products(pe, k.ps[:, 2 * c + h, 0:NB], lambda lo: k.w.part(n, half, lo)[:, at:at + P],
                                                lambda lo: part(k, lo, 32, NB)[:, 16 * c + mm, :], mm == 0, mm == 15)
                        last.then_inc(k.w.used, 1)
            pe.wait_ge(s["gelued"], 4)
            pe.wait_ge(s["w2_in"], 32)
            for h in range(2):
                last = pe.matmul(k.ps[:, 4, 0:NB], w2k[:, h, :], hid[:, 0, h, :], start=h == 0, stop=h == 1)
            last.then_inc(s["multiplied"], 1)
            pe.wait_ge(s["spread"], 1)
            for g in range(NG):
                for h in range(2):
                    last = pe.matmul(k.ps[:, 5, 64 * g:64 * g + 64], hidv[:, h, g].rearrange("p r n -> p (r n)"),
                                     w2v[:, h, :], start=h == 0, stop=h == 1)
            last.then_inc(s["multiplied"], 1)

        @block.scalar
        def _(act):
            for f in range(8):
                k.w.split_hi(act, first + f)
            for c in range(2):
                k.w.wait_used(act, first + 4 * c + 3)
                for h in range(2):
                    act.activation(hid[:, c, h, :], k.ps[:, 2 * c + h, 0:NB], ACT.Gelu_apprx_tanh,
                                   bias=col(k, "cmp_b1", 2 * c + h)).then_inc(s["gelued"], 1)
            act.wait_ge(s["multiplied"], 1)
            act.activation(k.kcT[:, :], k.ps[:, 4, 0:NB], ACT.Copy)
            act.wait_ge(s["multiplied"], 2)
            act.activation(k.vc[:, :], k.ps[:, 5, 0:NG * HD], ACT.Copy)

        @block.vector
        def _(v):
            v.memset(big[:, 4608:5632], 0.0).then_inc(s["zeroed"], 1)
            for f in range(8):
                k.w.split_lo(v, first + f)
            v.wait_ge(s["zeroed"], 1)
            v.wait_ge(s["gelued"], 4)
            for h in range(2):
                last = v.tensor_copy(hidv[:, h, :, :, 0:NCMP],
                                     bc(hid[:, 1, h, :].rearrange("p (g n) -> p g n", g=NG).unsqueeze(2),
                                        [P, NG, NR, NCMP]))
                if h == 0:
                    last.then_inc(s["zeroed"], 1)
            v.wait_ge(s["zeroed"], 2)
            last.then_inc(s["spread"], 1)



def nsa(k):
    big = k.big
    view = lambda at, c, n: big[:, at:at + c * n].rearrange("p (c t) -> p c t", c=c)
    qT = view(0, KC, T)
    oT = view(2048, KC, T)
    gates = view(4096, TT, 48)
    mask = big[:, 4352:4608]
    cmask = view(4608, TT, NCMP)
    cs = big[:, 4864:5376].rearrange("p (h n) -> p h n", h=NH)
    csT = view(5376, NG, P)
    cst = big[:, 5888:5888 + 64]
    sm = view(6144, 2, 512)
    pr = view(7168, 2, 512)
    prT = view(8192, 2, 512)
    small = view(9216, 2, 16)
    to_columns(k, mod=(mod_row(k, 1), mod_row(k, 0)))
    project_columns(k, KC, lambda act, f, ps: act.activation(qT[:, f, :], ps, ACT.Copy, scale=float(HD) ** -0.5))
    first = k.w.take(1)
    with stage(k, "loaded") as (s, block):
        @block.sync
        def _(sp):
            sp.dma_start(mask, k.dram["mask"]).then_inc(s["loaded"], 16)
            sp.dma_start(cmask, k.dram["cmask"]).then_inc(s["loaded"], 16)
            sp.wait_ge(s["loaded"], 32)
            k.w.stream(sp)

        @block.tensor
        def _(pe):
            for half in range(2):
                k.w.wait_split(pe, first, half)
                for tt in range(TT):
                    for q in range(KC // 2):
                        kc = half * (KC // 2) + q
                        last = products(pe, k.ps[:, tt, 0:48], lambda lo: k.hT[:, lo, kc, tt * P:(tt + 1) * P],
                                        lambda lo: k.w.part(first, half, lo)[:, q * P:q * P + 48], kc == 0, kc == KC - 1)
                last.then_inc(k.w.used, 1)

        def after(act, f):
            k.w.wait_used(act, first)
            for tt in range(TT):
                act.activation(gates[:, tt, :], k.ps[:, tt, 0:48], ACT.Sigmoid)
        splitting(k, block, first, 1, after)

    for qt in range(TT):
        nk = P * (qt + 1)
        qs = slice(P * qt, P * qt + P)
        gate = gates[:, qt, :].rearrange("p (h b) -> p b h", b=3)
        msk = mask[:, T - nk:T]
        with stage(k, "scored dve maxed exped picked turned kept") as (s, block):
            @block.sync
            def _(sp):
                k.w.stream(sp)

            @block.tensor
            def _(pe):
                for h in range(NH):
                    r = slice(64 * (h % 2), 64 * (h % 2) + 64)
                    g = h // NR
                    last = pe.matmul(k.ps[:, 4 + 2 * (h % 2), 16 * h:16 * h + NCMP], qT[r, h // 2, qs], k.kcT[r, NCMP * g:NCMP * g + NCMP],
                                     start=True, stop=True)
                last.then_inc(s["scored"], 1)
                pe.wait_ge(s["picked"], 1)
                for g in range(NG):
                    last = pe.transpose(k.ps[:, 5, g * P:(g + 1) * P], cs[:, 4 * g:4 * g + 4, :].rearrange("p h n -> p (h n)"),
                                        k.ident[:, :])
                last.then_inc(s["turned"], 1)

            @block.vector
            def _(v):
                st = Steps(v, s["dve"])
                c = cs[:, :, 0:NCMP]
                st.link(v.memset(cs, 0.0))
                v.wait_ge(s["scored"], 1)
                for odd in range(2):
                    st.done(v.tensor_tensor(c[:, odd::2], k.ps[:, 4 + 2 * odd, 0:T].rearrange("p (h n) -> p h n", n=16)[:, odd::2, 0:NCMP],
                                            bc(cmask[:, qt, :].unsqueeze(1), [P, NH // 2, NCMP]), ALU.add))
                st.wait()
                st.link(v.tensor_reduce(cst[:, 0:16], c, AX.X, ALU.max))
                st.link(v.tensor_scalar(cst[:, 0:16], cst[:, 0:16], -1.0e29, None, ALU.max))
                v.tensor_tensor(c, c, bc(cst[:, 0:16].unsqueeze(2), [P, NH, NCMP]), ALU.subtract).then_inc(s["maxed"], 1)
                v.wait_ge(s["exped"], 1)
                st.link(v.tensor_reduce(cst[:, 16:32], c, AX.X, ALU.add))
                st.link(v.tensor_scalar(cst[:, 16:32], cst[:, 16:32], 1.0e-30, None, ALU.max))
                st.link(v.reciprocal(cst[:, 32:48], cst[:, 16:32]))
                st.link(v.tensor_tensor(cst[:, 48:64], cst[:, 32:48], gate[:, 0], ALU.mult))
                v.tensor_tensor(c, c, bc(cst[:, 48:64].unsqueeze(2), [P, NH, NCMP]), ALU.mult).then_inc(s["picked"], 1)
                v.wait_ge(s["turned"], 1)
                v.tensor_copy(csT, k.ps[:, 5, :].rearrange("p (g q) -> p g q", g=NG))

            @block.scalar
            def _(act):
                act.wait_ge(s["maxed"], 1)
                act.activation(cs[:, :, 0:NCMP], cs[:, :, 0:NCMP], ACT.Exp).then_inc(s["exped"], 1)

        with stage(k, "scored dve minned exped weighed turned back summed stored") as (s, block):
            @block.sync
            def _(sp):
                k.w.stream(sp)

            two = lambda ap: ap[:, 0:2 * nk].rearrange("p (b n) -> p b n", b=2)

            @block.tensor
            def _(pe):
                def score(h):
                    r, g = slice(64 * (h % 2), 64 * (h % 2) + 64), h // NR
                    if h >= 2:
                        pe.wait_ge(s["minned"], h - 1)
                    for b in range(2):
                        last = pe.matmul(k.ps[:, 4 + h % 2, b * nk:(b + 1) * nk], qT[r, h // 2, qs], k.kT[r, 4 * b + g, 0:nk],
                                         start=True, stop=True)
                    last.then_inc(s["scored"], 1)

                def turn(h):
                    pe.wait_ge(s["weighed"], h + 1)
                    if h >= 2:
                        pe.wait_ge(s["back"], h - 1)
                    for n in range(2 * nk // P):
                        last = pe.transpose(k.ps[:, 6 + h % 2, n * P:(n + 1) * P], pr[:, h % 2, n * P:(n + 1) * P], k.ident[:, :])
                    last.then_inc(s["turned"], 1)

                def values(h):
                    r, g, j = slice(64 * (h % 2), 64 * (h % 2) + 64), h // NR, h % NR
                    pe.wait_ge(s["back"], h + 1)
                    if h >= 4 and h % 2 == 0:
                        pe.wait_ge(s["stored"], h // 2 - 1)
                    out = k.ps[r, (h // 2) % 2, 0:P]
                    pe.matmul(out, k.vc[32 * j:32 * j + 32, HD * g:HD * g + HD], csT[32 * j:32 * j + 32, g, :],
                              start=True, stop=False)
                    for b in range(2):
                        for kt in range(qt + 1):
                            last = pe.matmul(out, k.val[:, kt, 256 * b + HD * g:256 * b + HD * g + HD],
                                             prT[:, h % 2, b * nk + kt * P:b * nk + kt * P + P], start=False,
                                             stop=b == 1 and kt == qt)
                    last.then_inc(s["summed"], 1)

                score(0)
                for h in range(NH + 3):
                    if h + 1 < NH:
                        score(h + 1)
                    if h >= 3:
                        values(h - 3)
                    if 1 <= h <= NH:
                        turn(h - 1)

            @block.vector
            def _(v):
                st = Steps(v, s["dve"])

                for h in range(NH + 1):
                    new, old, m, o = h < NH, h >= 1, h % 2, (h - 1) % 2
                    if new:
                        v.wait_ge(s["scored"], h + 1)
                        if h >= 2:
                            v.wait_ge(s["exped"], 2 * (h - 1))
                        st.done(v.tensor_tensor(two(sm[:, m]), two(k.ps[:, 4 + m]), bc(msk.unsqueeze(1), [P, 2, nk]), ALU.add))
                    if old:
                        v.wait_ge(s["exped"], 2 * h)
                        st.done(v.reciprocal(small[:, o, 6:8], small[:, o, 4:6]))
                    st.wait()
                    if new:
                        st.done(v.tensor_reduce(small[:, m, 0:2], two(sm[:, m]), AX.X, ALU.max))
                    if old:
                        st.done(v.tensor_tensor(small[:, o, 8:10], small[:, o, 6:8], gate[:, 1:3, h - 1], ALU.mult))
                    st.wait()
                    if new:
                        v.tensor_scalar(small[:, m, 2:4], small[:, m, 0:2], -1.0, None, ALU.mult).then_inc(s["minned"], 1)
                    if old:
                        v.tensor_tensor(two(pr[:, o]), two(pr[:, o]), bc(small[:, o, 8:10].unsqueeze(2), [P, 2, nk]),
                                        ALU.mult).then_inc(s["weighed"], 1)

            @block.scalar
            def _(act):
                for h in range(NH + 5):
                    if h < NH:
                        act.wait_ge(s["minned"], h + 1)
                        if h >= 2:
                            act.wait_ge(s["turned"], h - 1)
                        for b in range(2):
                            act.activation(pr[:, h % 2, b * nk:(b + 1) * nk], sm[:, h % 2, b * nk:(b + 1) * nk], ACT.Exp,
                                           bias=small[:, h % 2, 2 + b:3 + b],
                                           accum_out=small[:, h % 2, 4 + b:5 + b]).then_inc(s["exped"], 1)
                    if 2 <= h < NH + 2:
                        act.wait_ge(s["turned"], h - 1)
                        if h >= 4:
                            act.wait_ge(s["summed"], h - 3)
                        act.activation(prT[:, h % 2, 0:2 * nk], k.ps[:, 6 + h % 2, 0:2 * nk], ACT.Copy).then_inc(s["back"], 1)
                    if h >= 5 and h % 2 == 1:
                        act.wait_ge(s["summed"], h - 3)
                        act.activation(oT[:, (h - 5) // 2, qs], k.ps[:, ((h - 5) // 2) % 2, 0:P], ACT.Copy).then_inc(s["stored"], 1)
    split_columns(k, oT)
    project_rows(k)
    residual_ln(k, mod_row(k, 2), "ln_g10", "ln_b10")



def build(nc, dram, out, total):
    with ExitStack() as ctx:
        def sb(name, shape, dt=F32):
            return ctx.enter_context(nc.sbuf_tensor(name, shape, dt))

        k = Kernel()
        k.nc, k.stages, k.dram = nc, 0, dram
        k.ring = sb("ring", [P, RING, TILE])
        k.x = sb("x", [P, TT, D])
        k.hT = sb("hT", [P, 2, KC, T], F32R)
        k.parts = sb("parts", [P, HALVES, 2, HALF], F32R)
        k.tmp = sb("tmp", [P, TT, D])
        k.big_t = sb("big", [P, PK * T])
        k.big = k.big_t[:, :]
        k.g2 = sb("g2", [P, D])
        k.cols = sb("cols", [P, NCOLS])
        k.ident = sb("ident", [P, P])
        k.iota = sb("iota", [P, P])
        k.acted = sb("acted", [P, 2, T])
        k.gatedT = sb("gatedT", [P, 2, 2, T], F32R)
        k.pickT = sb("pickT", [P, 3, T])
        k.stat = sb("stat", [P, 40])
        k.c2 = sb("c2", [P, 2, KC], F32R)
        k.ps = ctx.enter_context(nc.psum_tensor("ps", [P, 8, 512], F32))
        k.row = k.big[:, 24576:26624].rearrange("p (a n) -> p a n", a=2)
        k.w = Ring(k, total)
        k.mod_rows = nc.dram_tensor("mod_rows", (14, D), F32).ap()
        k.kT = k.big[:, 16384:18432].rearrange("p (c t) -> p c t", c=8)
        k.val = k.big[:, 15360:16384].rearrange("p (c n) -> p c n", c=TT)
        k.kcT = k.big[:, 15104:15164]
        k.vc = k.big[:, 14848:15104]

        with stage(k, "in_ silu hi") as (s, block):
            @block.scalar
            def _(act):
                act.wait_ge(s["in_"], 64)
                act.activation(k.stat[:, 0:KC], k.cols[:, COLS["c"]:COLS["c"] + KC], ACT.Silu).then_inc(s["silu"], 1)
                act.wait_ge(s["silu"], 1)
                act.activation(k.c2[:, 0, :], k.stat[:, 0:KC], ACT.Copy).then_inc(s["hi"], 1)

            @block.vector
            def _(v):
                v.wait_ge(s["hi"], 1)
                v.tensor_tensor(k.c2[:, 1, :], k.stat[:, 0:KC], k.c2[:, 0, :].bitcast(F32), ALU.subtract)

            @block.sync
            def _(sp):
                sp.dma_start(k.x[:, :, :], k.dram["x_in"].rearrange("(a p) n -> p a n", p=P)).then_inc(s["in_"], 16)
                sp.dma_start(k.cols[:, :], k.dram["cols_in"]).then_inc(s["in_"], 16)
                sp.dma_start(k.ident[:, :], k.dram["ident_in"]).then_inc(s["in_"], 16)
                sp.dma_start(k.iota[:, :], k.dram["iota_in"]).then_inc(s["in_"], 16)
                k.w.stream(sp)
                sp.wait_ge(s["in_"], 64)

        def mod_dst(j):
            return k.g2[:, :] if j == 5 else mod_row(k, j)

        steps = [
            lambda: ffn(k, 0, 0), lambda: s5(k), lambda: ffn(k, 0, 1),
            lambda: ffn(k, 1, 0), lambda: conv(k), lambda: ffn(k, 1, 1, mod_loads(k, mod_dst, 0, 6)),
            lambda: retention(k),
            lambda: (peer(k, 0, mod_row(k, 4), mod_row(k, 3)),
                     residual_ln(k, k.g2, "ln_g01", "ln_b01", mod_loads(k, lambda j: mod_row(k, j), 6, 2))),
            lambda: (shared_kv(k, mod_loads(k, mod_dst, 8, 6)), nsa(k)),
            lambda: (peer(k, 1, mod_row(k, 4), mod_row(k, 3)), residual_ln(k, k.g2, "ln_g11", "ln_b11")),
        ]
        for step in steps:
            step()
        with stage(k, "out_done") as (s, block):
            @block.sync
            def _(sp):
                sp.dma_start(out.rearrange("(a p) n -> p a n", p=P), k.x[:, :, :]).then_inc(s["out_done"], 16)
                sp.wait_ge(s["out_done"], 16)



def column_tiles(w):
    n = w.shape[1] // P
    return w.reshape(KC, P, n, P).transpose(2, 1, 0, 3).reshape(n, P, TILE)


def row_tiles(w):
    nk, g = w.shape[0] // P, w.shape[1] // TILE
    return w.reshape(nk, P, g, TILE).transpose(2, 0, 1, 3).reshape(g * nk, P, TILE)


def weave(ups, downs):
    out = [u[f] for f in range(2) for u in ups]
    for g in range(len(downs) - 2):
        out += [u[g + 2] for u in ups] + [downs[g]]
    return out + [downs[-2], downs[-1]]


def lay_out(a):
    tiles = []

    mod_tiles = np.concatenate([row_tiles(w) for w in (a["ada_w_2"][0], a["kv_ada_w_2"], a["ada_w_2"][1])])

    def ffn_tiles(i, j):
        tiles.extend(weave([column_tiles(a["ffn_w1"][i, j]), column_tiles(a["ffn_w3"][i, j])], row_tiles(a["ffn_w2"][i, j])))

    def peer_tiles(layer):
        tiles.extend(column_tiles(a["peer_w_q_2"][layer]))
        if layer == 0:
            tiles.extend(mod_tiles[9 * KC:])
        u = a["peer_u_2"][layer].reshape(PK, PK, KC, P).transpose(0, 3, 2, 1).reshape(PK, P, TILE)
        v = a["peer_v_2"][layer].reshape(PK, PK, TILE)
        n = PK - HELD[layer]
        tiles.extend(u[n:])
        tiles.extend(v[n:])
        tiles.extend(weave([u[:n]], v[:n]))

    ffn_tiles(0, 0)
    tiles.extend(column_tiles(a["s5_w_in"][0]))
    tiles.extend(mod_tiles[:4 * KC])
    tiles.extend(column_tiles(a["s5_w_glu"][0]))
    tiles.extend(row_tiles(a["s5_w_out"][0]))
    ffn_tiles(0, 1)
    ffn_tiles(1, 0)
    tiles.extend(column_tiles(a["cv_w_in"][0]))
    tiles.extend(mod_tiles[4 * KC:9 * KC])
    tiles.extend(row_tiles(a["cv_w_out"][0]))
    ffn_tiles(1, 1)
    tiles.extend(column_tiles(a["ret_w_in_2"][0][:, :2048]))
    tiles.extend(row_tiles(a["ret_w_in_2"][0][:, 2048:]))
    tiles.extend(row_tiles(a["ret_w_o_2"][0]))
    peer_tiles(0)
    kv = a["nsa_w_kv_2"].reshape(D, 3, 2, NG, HD)
    twice = lambda w: np.concatenate([w, w], axis=2).reshape(D, -1)
    tiles.extend(column_tiles(twice(kv[:, 0].reshape(D, 2 * NG, HD))))
    tiles.extend(column_tiles(twice(kv[:, 1:, 0].reshape(D, 2 * NG, HD))))
    v = kv[:, 1:, 1].reshape(4, 2, P, 512)
    tiles.extend(v.transpose(0, 2, 1, 3).reshape(4, P, TILE))
    w1 = a["cmp_w1_2"].reshape(2, 4, 4, P, CHID)
    tiles.extend(w1.transpose(0, 1, 3, 2, 4).reshape(8, P, TILE))
    w = a["nsa_w_in_2"][0]
    tiles.extend(column_tiles(w[:, :NH * HD]))
    g = np.zeros((D, P), np.float32)
    g[:, :48] = w[:, NH * HD:]
    tiles.extend(column_tiles(g))
    tiles.extend(row_tiles(a["nsa_w_o_2"][0]))
    peer_tiles(1)

    def cols(vec):
        return vec.reshape(-1, P).T
    parts = [cols(a["norm_pre"]), cols(a["s5_d"]), cols(a["s5_b_glu"]), cols(a["cv_b_in"]), cols(a["cv_dw"]),
             cols(a["cv_dw_b"]), cols(a["cv_ln_g"]), cols(a["cv_ln_b"]), cols(a["c_2"]), cols(a["cmp_b1_2"]),
             cols(a["cmp_pe_2"])]
    rows = [a["norm_post"].reshape(6, D), a["cv_b_out"].reshape(1, D)]
    mod_bias = np.concatenate([a["ada_b_2"][0].reshape(6, D), a["kv_ada_b_2"].reshape(2, D), a["ada_b_2"][1].reshape(6, D)])
    rows += [a[n][l, j].reshape(1, D) for l in range(2) for j in range(2) for n in ("ln_g_2", "ln_b_2")]
    rows = np.concatenate(rows)

    def states(v):
        return v.reshape(ST, P).T
    s5_par = np.stack([states(a["s5_a_re"]), states(a["s5_a_im"]), states(np.repeat(a["s5_log_dt"].reshape(-1), STATE))])
    bcs = [a["s5_b_re"][0], a["s5_b_im"][0], a["s5_c_re"][0].transpose(0, 2, 1), a["s5_c_im"][0].transpose(0, 2, 1)]
    s5_bc = np.stack([v.reshape(ST, P, GH).transpose(1, 0, 2) for v in bcs])
    keys = a["peer_keys_2"].reshape(2, 16, PK, P).transpose(0, 3, 1, 2)
    w2 = a["cmp_w2_2"].reshape(2, 2, P, HD)
    w2k = np.concatenate([w2[0], w2[0]], axis=2).transpose(1, 0, 2)
    w2v = w2[1].transpose(1, 0, 2)

    f32 = np.float32
    theta = (1.0 / (f32(10000.0) ** np.linspace(0.0, 1.0, RDK // 2, dtype=f32))).astype(f32)
    ang = (np.arange(T, dtype=f32)[:, None] * theta[None]).T
    rope = np.stack([np.cos(ang), np.sin(ang)], axis=1).astype(f32)
    log_g = np.log1p(-np.exp2(-5.0 - np.arange(RH)))
    kk, qq = np.arange(P)[:, None], np.arange(T)[None]
    d0 = qq - kk
    dec = np.zeros((P, RH, 384))
    for h in range(RH):
        full = np.where(d0 >= 0, np.exp(np.maximum(d0, 0) * log_g[h]), 0.0) * RDK ** -0.5
        dec[:, h, :T] = full
        dec[:, h, T:] = full[:, :P]
    mask = np.zeros((P, T), f32)
    mask[:, P:] = np.where(np.arange(P)[None] <= np.arange(P)[:, None], 0.0, NEG)
    t = np.arange(T)[:, None]
    cm = np.where(np.arange(NCMP)[None] * CS + CL - 1 <= t, 0.0, NEG).astype(f32)
    arrays = {
        "x_in": a["x"].reshape(T, D), "wts": np.stack(tiles), "cols_in": np.concatenate(parts, axis=1),
        "mod_bias": mod_bias, "rows": np.broadcast_to(rows[:, None, :], (len(rows), P, D)), "s5_par": s5_par, "s5_bc": s5_bc,
        "peer_keys": keys, "cmp_w2k": w2k, "cmp_w2v": w2v, "rope": rope, "decay": dec.astype(f32), "mask": mask,
        "cmask": cm.reshape(TT, P, NCMP).transpose(1, 0, 2), "ident_in": np.eye(P, dtype=f32),
        "iota_in": np.broadcast_to(np.arange(P, dtype=f32), (P, P)),
    }
    return {n: np.ascontiguousarray(v) for n, v in arrays.items()}


def program(nc, mybir, arrays):
    dram = {n: nc.dram_tensor(n, v.shape, mybir.dt.from_np(v.dtype), kind="ExternalInput").ap() for n, v in arrays.items()}
    out = nc.dram_tensor("out", (T, D), mybir.dt.float32, kind="ExternalOutput").ap()
    build(nc, dram, out, arrays["wts"].shape[0])


def kernel(**inputs):
    import concourse.bacc as bacc
    from concourse import mybir as _mybir
    from concourse.bass_utils import run_bass_kernel_spmd
    arrays = lay_out({n: np.asarray(v) for n, v in inputs.items()})
    nc = bacc.Bacc("TRN2", target_bir_lowering=False, num_devices=1)
    program(nc, _mybir, arrays)
    r = run_bass_kernel_spmd(nc, [arrays], core_ids=[0])
    return np.asarray(r.results[0]["out"]).reshape(1, T, D)
```
